# Optimizing a Trainium2 kernel written in Bass

```python
import jax
import jax.numpy as jnp
from jax import lax
import numpy as np

D_MODEL = 1024
BATCH = 1
SEQ = 256
DEPTH = 2

MLA_HEADS = 8
MLA_Q_RANK = 256
MLA_KV_RANK = 128
MLA_NOPE = 64
MLA_ROPE = 32
MLA_V = 64
ROPE_THETA = 10000.0
GDN_HEADS = 4
GDN_DK = 128
GDN_DV = 128
GDN_CONV = 4
GDN_CHUNK = 64
FOX_HEADS = 8
FOX_DH = 64
FOX_FORGET_BIAS_MEAN = 2.0
N_BRANCH = 3
BRANCH_W = 512
Q_BLOCK = 128
N_EXPERTS = 16
N_GROUPS = 4
TOP_K = 2
GROUP_SCORE_TOPK = 2
D_EXPERT = 512
DN_ALPHA = (2 * DEPTH) ** 0.25
DN_BETA = (8 * DEPTH) ** -0.25
EPS = 1e-6

GDN_QKV = GDN_HEADS * (2 * GDN_DK + GDN_DV)
FOX_QKV = 3 * FOX_HEADS * FOX_DH
IN_SPLITS = (MLA_Q_RANK, MLA_KV_RANK, MLA_ROPE,
             GDN_QKV, GDN_HEADS * GDN_DV, GDN_HEADS, GDN_HEADS,
             FOX_QKV, FOX_HEADS,
             N_BRANCH * D_MODEL)
D_IN = sum(IN_SPLITS)

kernel_name = "hybrid_mla_gdn_fox_grouped_moe_deepnorm"

def _split_cols(h, sizes):
    parts, start = [], 0
    for size in sizes:
        parts.append(h[..., start:start + size])
        start += size
    return parts

def layer_norm(x, g, b):
    xf = x.astype(jnp.float32)
    mu = jnp.mean(xf, axis=-1, keepdims=True)
    var = jnp.mean(jnp.square(xf - mu), axis=-1, keepdims=True)
    return ((xf - mu) * lax.rsqrt(var + EPS) * g + b).astype(x.dtype)

def rms_norm(x, g):
    xf = x.astype(jnp.float32)
    y = xf * lax.rsqrt(jnp.mean(jnp.square(xf), axis=-1, keepdims=True) + EPS) * g
    return y.astype(x.dtype)

def l2_normalize(x):
    return x * lax.rsqrt(jnp.sum(jnp.square(x), axis=-1, keepdims=True) + EPS)

def rope(x, positions):
    half = x.shape[-1] // 2
    inv_freq = ROPE_THETA ** (-jnp.arange(half, dtype=jnp.float32) / half)
    ang = positions.astype(jnp.float32)[..., None] * inv_freq
    cos = jnp.cos(ang)[:, :, None, :]
    sin = jnp.sin(ang)[:, :, None, :]
    x1 = x[..., :half].astype(jnp.float32)
    x2 = x[..., half:].astype(jnp.float32)
    return jnp.concatenate([x1 * cos - x2 * sin, x2 * cos + x1 * sin], axis=-1).astype(x.dtype)

def causal_block_attention(q, k, v, scale, log_cum=None):
    B, S, H, _ = q.shape
    nb = S // Q_BLOCK
    qb = jnp.moveaxis(q.reshape(B, nb, Q_BLOCK, H, q.shape[-1]), 1, 0)
    kpos = jnp.arange(S)
    cum_h = None if log_cum is None else jnp.moveaxis(log_cum.astype(jnp.float32), 1, 2)

    def one_block(inp):
        i, qi = inp
        s = jnp.einsum('bqhd,bkhd->bhqk', qi, k).astype(jnp.float32) * scale
        if cum_h is not None:
            cq = lax.dynamic_slice_in_dim(cum_h, i * Q_BLOCK, Q_BLOCK, axis=2)
            s = s + cq[..., :, None] - cum_h[..., None, :]
        qpos = i * Q_BLOCK + jnp.arange(Q_BLOCK)
        s = jnp.where(kpos[None, :] <= qpos[:, None], s, -jnp.inf)
        p = jax.nn.softmax(s, axis=-1)
        return jnp.einsum('bhqk,bkhd->bqhd', p.astype(v.dtype), v)

    o = lax.map(one_block, (jnp.arange(nb), qb))
    return jnp.moveaxis(o, 0, 1).reshape(B, S, H, v.shape[-1])

def causal_dwconv(x, w):
    return lax.conv_general_dilated(
        x, w[:, None, :].astype(x.dtype), window_strides=(1,),
        padding=[(GDN_CONV - 1, 0)], dimension_numbers=('NWC', 'WIO', 'NWC'),
        feature_group_count=x.shape[-1])

def gated_delta_chunked(q, k, v, g, beta):
    B, S, H, DK = q.shape
    DV = v.shape[-1]
    C = GDN_CHUNK
    N = S // C

    def to_chunks(t):
        return jnp.moveaxis(t.reshape(B, N, C, H, t.shape[-1]), 3, 1)

    q = to_chunks(q) * (DK ** -0.5)
    k = to_chunks(k)
    v = to_chunks(v)
    gc = jnp.cumsum(to_chunks(g[..., None])[..., 0], axis=-1)
    bt = to_chunks(beta[..., None])
    tril = jnp.tril(jnp.ones((C, C), dtype=bool))
    strict = jnp.tril(jnp.ones((C, C), dtype=bool), -1)
    diff = gc[..., :, None] - gc[..., None, :]
    decay = jnp.where(tril, jnp.exp(jnp.where(tril, diff, 0.0)), 0.0)
    kk = jnp.einsum('bhnid,bhnjd->bhnij', k, k)
    lower = jnp.where(strict, bt * kk * decay, 0.0)
    rhs = jnp.concatenate([v * bt, k * bt * jnp.exp(gc)[..., None]], axis=-1)
    sol = lax.linalg.triangular_solve(lower, rhs, left_side=True, lower=True, unit_diagonal=True)
    u, w = sol[..., :DV], sol[..., DV:]
    a_intra = jnp.einsum('bhnid,bhnjd->bhnij', q, k) * decay
    q_dec = q * jnp.exp(gc)[..., None]
    k_dec = k * jnp.exp(gc[..., -1:] - gc)[..., None]
    g_last = jnp.exp(gc[..., -1])
    xs = tuple(jnp.moveaxis(t, 2, 0) for t in (u, w, q_dec, k_dec, a_intra, g_last))

    def step(state, inp):
        u_i, w_i, qd_i, kd_i, a_i, gl_i = inp
        v_new = u_i - jnp.einsum('bhck,bhkv->bhcv', w_i, state)
        o_i = jnp.einsum('bhck,bhkv->bhcv', qd_i, state) + jnp.einsum('bhcs,bhsv->bhcv', a_i, v_new)
        state = state * gl_i[..., None, None] + jnp.einsum('bhck,bhcv->bhkv', kd_i, v_new)
        return state, o_i

    state0 = jnp.zeros((B, H, DK, DV), jnp.float32)
    _, o = lax.scan(step, state0, xs)
    return o.transpose(1, 0, 3, 2, 4).reshape(B, S, H, DV)

def mla_branch(cq, ckv, kr, positions, q_norm, w_uq, kv_norm, w_ukv):
    B, S, _ = cq.shape
    q = (rms_norm(cq, q_norm) @ w_uq).reshape(B, S, MLA_HEADS, MLA_NOPE + MLA_ROPE)
    kv = (rms_norm(ckv, kv_norm) @ w_ukv).reshape(B, S, MLA_HEADS, MLA_NOPE + MLA_V)
    q = jnp.concatenate([q[..., :MLA_NOPE], rope(q[..., MLA_NOPE:], positions)], axis=-1)
    k_rope = jnp.broadcast_to(rope(kr[:, :, None, :], positions), (B, S, MLA_HEADS, MLA_ROPE))
    k = jnp.concatenate([kv[..., :MLA_NOPE], k_rope], axis=-1)
    v = kv[..., MLA_NOPE:]
    o = causal_block_attention(q, k, v, (MLA_NOPE + MLA_ROPE) ** -0.5)
    return o.reshape(B, S, MLA_HEADS * MLA_V)

def gdn_branch(qkv, z, a, b, conv_w, a_log, dt_bias, out_norm):
    B, S, _ = qkv.shape
    out_dtype = qkv.dtype
    qkv = jax.nn.silu(causal_dwconv(qkv, conv_w))
    q, k, v = _split_cols(qkv, (GDN_HEADS * GDN_DK, GDN_HEADS * GDN_DK, GDN_HEADS * GDN_DV))
    q = l2_normalize(q.reshape(B, S, GDN_HEADS, GDN_DK).astype(jnp.float32))
    k = l2_normalize(k.reshape(B, S, GDN_HEADS, GDN_DK).astype(jnp.float32))
    v = v.reshape(B, S, GDN_HEADS, GDN_DV).astype(jnp.float32)
    g = -jnp.exp(a_log.astype(jnp.float32)) * jax.nn.softplus(a.astype(jnp.float32) + dt_bias.astype(jnp.float32))
    beta = jax.nn.sigmoid(b.astype(jnp.float32))
    o = gated_delta_chunked(q, k, v, g, beta)
    o = rms_norm(o, out_norm) * jax.nn.silu(z.reshape(B, S, GDN_HEADS, GDN_DV).astype(jnp.float32))
    return o.reshape(B, S, GDN_HEADS * GDN_DV).astype(out_dtype)

def fox_branch(qkv, f_logit, f_bias):
    B, S, _ = qkv.shape
    q, k, v = [t.reshape(B, S, FOX_HEADS, FOX_DH) for t in _split_cols(qkv, (FOX_HEADS * FOX_DH,) * 3)]
    log_f = jax.nn.log_sigmoid(f_logit.astype(jnp.float32) + f_bias.astype(jnp.float32))
    log_cum = jnp.cumsum(log_f, axis=1)
    o = causal_block_attention(q, k, v, FOX_DH ** -0.5, log_cum)
    return o.reshape(B, S, FOX_HEADS * FOX_DH)

def grouped_moe(x, router_w, router_bias, w_gate, w_up, w_down):
    B, S, D = x.shape
    xt = x.reshape(B * S, D)
    scores = jax.nn.sigmoid((xt @ router_w).astype(jnp.float32))
    sel = scores + router_bias.astype(jnp.float32)
    per_group = N_EXPERTS // N_GROUPS
    group_score = lax.top_k(sel.reshape(-1, N_GROUPS, per_group), GROUP_SCORE_TOPK)[0].sum(-1)
    best = jnp.argmax(group_score, axis=-1)
    in_group = jnp.repeat(jnp.arange(N_GROUPS)[None, :] == best[:, None], per_group, axis=1)
    _, idx = lax.top_k(jnp.where(in_group, sel, -jnp.inf), TOP_K)
    wts = jnp.take_along_axis(scores, idx, axis=-1)
    wts = wts / jnp.sum(wts, axis=-1, keepdims=True)
    comb = jnp.sum(jax.nn.one_hot(idx, N_EXPERTS, dtype=jnp.float32) * wts[..., None], axis=1)
    comb = comb.astype(xt.dtype)
    y = jnp.zeros_like(xt)
    for e in range(N_EXPERTS):
        h = jax.nn.silu(xt @ w_gate[e]) * (xt @ w_up[e])
        y = y + comb[:, e:e + 1] * (h @ w_down[e])
    return y.reshape(B, S, D)

def setup_inputs(seed: int = 0) -> dict:
    key = jax.random.key(seed)
    ks = jax.random.split(key, 24)
    f32 = jnp.float32
    L, D, E, F = DEPTH, D_MODEL, N_EXPERTS, D_EXPERT

    def nrm(k, shape, scale):
        return jax.random.normal(k, shape, f32) * scale

    x = jax.random.normal(ks[0], (BATCH, SEQ, D), f32)
    positions = jnp.broadcast_to(jnp.arange(SEQ, dtype=jnp.int32)[None, :], (BATCH, SEQ))
    w_in = nrm(ks[1], (L, D, D_IN), D ** -0.5)
    mla_q_norm = 1.0 + nrm(ks[2], (L, MLA_Q_RANK), 0.02)
    mla_w_uq = nrm(ks[3], (L, MLA_Q_RANK, MLA_HEADS * (MLA_NOPE + MLA_ROPE)), MLA_Q_RANK ** -0.5)
    mla_kv_norm = 1.0 + nrm(ks[4], (L, MLA_KV_RANK), 0.02)
    mla_w_ukv = nrm(ks[5], (L, MLA_KV_RANK, MLA_HEADS * (MLA_NOPE + MLA_V)), MLA_KV_RANK ** -0.5)
    gdn_conv = nrm(ks[6], (L, GDN_CONV, GDN_QKV), GDN_CONV ** -0.5)
    gdn_a_log = jnp.log(jax.random.uniform(ks[7], (L, GDN_HEADS), f32, 1.0, 16.0))
    dt = jnp.exp(jax.random.uniform(ks[8], (L, GDN_HEADS), f32, np.log(1e-3), np.log(1e-1)))
    gdn_dt_bias = jnp.log(jnp.expm1(dt))
    gdn_out_norm = 1.0 + nrm(ks[9], (L, GDN_DV), 0.02)
    fox_f_bias = FOX_FORGET_BIAS_MEAN + nrm(ks[10], (L, FOX_HEADS), 0.1)
    w_branch = nrm(ks[11], (L, N_BRANCH, BRANCH_W, D), BRANCH_W ** -0.5 * DN_BETA)
    w_out = nrm(ks[12], (L, D, D), D ** -0.5 * DN_BETA)
    ln1_g = 1.0 + nrm(ks[13], (L, D), 0.02)
    ln1_b = nrm(ks[14], (L, D), 0.02)
    router_w = nrm(ks[15], (D, E), D ** -0.5)
    router_bias = nrm(ks[16], (E,), 0.01)
    exp_w_gate = nrm(ks[17], (L, E, D, F), D ** -0.5)
    exp_w_up = nrm(ks[18], (L, E, D, F), D ** -0.5)
    exp_w_down = nrm(ks[19], (L, E, F, D), F ** -0.5 * DN_BETA)
    ln2_g = 1.0 + nrm(ks[20], (L, D), 0.02)
    ln2_b = nrm(ks[21], (L, D), 0.02)
    return {"x": x, "positions": positions, "w_in": w_in,
            "mla_q_norm": mla_q_norm, "mla_w_uq": mla_w_uq,
            "mla_kv_norm": mla_kv_norm, "mla_w_ukv": mla_w_ukv,
            "gdn_conv": gdn_conv, "gdn_a_log": gdn_a_log, "gdn_dt_bias": gdn_dt_bias,
            "gdn_out_norm": gdn_out_norm, "fox_f_bias": fox_f_bias,
            "w_branch": w_branch, "w_out": w_out, "ln1_g": ln1_g, "ln1_b": ln1_b,
            "router_w": router_w, "router_bias": router_bias,
            "exp_w_gate": exp_w_gate, "exp_w_up": exp_w_up, "exp_w_down": exp_w_down,
            "ln2_g": ln2_g, "ln2_b": ln2_b}

def reference(x, positions, w_in, mla_q_norm, mla_w_uq, mla_kv_norm, mla_w_ukv,
              gdn_conv, gdn_a_log, gdn_dt_bias, gdn_out_norm, fox_f_bias,
              w_branch, w_out, ln1_g, ln1_b, router_w, router_bias,
              exp_w_gate, exp_w_up, exp_w_down, ln2_g, ln2_b):
    B, S, D = x.shape
    for l in range(DEPTH):
        h = x @ w_in[l]
        (cq, ckv, kr, g_qkv, g_z, g_a, g_b, f_qkv, f_logit, gate_logits) = _split_cols(h, IN_SPLITS)
        o_mla = mla_branch(cq, ckv, kr, positions, mla_q_norm[l], mla_w_uq[l], mla_kv_norm[l], mla_w_ukv[l])
        o_gdn = gdn_branch(g_qkv, g_z, g_a, g_b, gdn_conv[l], gdn_a_log[l], gdn_dt_bias[l], gdn_out_norm[l])
        o_fox = fox_branch(f_qkv, f_logit, fox_f_bias[l])
        branches = jnp.stack([o_mla, o_gdn, o_fox], axis=2)
        gates = jax.nn.sigmoid(gate_logits.reshape(B, S, N_BRANCH, D).astype(jnp.float32)).astype(x.dtype)
        merged = jnp.sum(gates * jnp.einsum('bsnc,ncd->bsnd', branches, w_branch[l]), axis=2)
        x = layer_norm(DN_ALPHA * x + merged @ w_out[l], ln1_g[l], ln1_b[l])
        y = grouped_moe(x, router_w, router_bias, exp_w_gate[l], exp_w_up[l], exp_w_down[l])
        x = layer_norm(DN_ALPHA * x + y, ln2_g[l], ln2_b[l])
    return x


_drawn_inputs = setup_inputs


def setup_inputs(seed=0):
    import zlib

    import numpy as np

    out = dict(_drawn_inputs(seed))
    spreads = {}
    factors = {'mla_q_norm': 8.0,
     'mla_kv_norm': 5.99,
     'gdn_a_log': 2.674,
     'gdn_out_norm': 5.922,
     'fox_f_bias': 45.848}
    for name, (base, spread) in spreads.items():
        noise = np.random.default_rng([zlib.crc32(name.encode()), seed]).standard_normal(out[name].shape)
        drawn = base * np.exp(spread * noise) if base else spread * noise
        out[name] = jnp.asarray(drawn.astype(out[name].dtype))
    for name, factor in factors.items():
        out[name] = (out[name] * factor).astype(out[name].dtype)
    return out
```

```python
from contextlib import ExitStack

import concourse.bass as bass
import numpy as np
from concourse import mybir

F32 = mybir.dt.float32
I32 = mybir.dt.int32
ALU = mybir.AluOpType
ACT = mybir.ActivationFunctionType
AX = mybir.AxisListType

P = 128
D, T, L = 1024, 256, 2
TT = T // P
DK = D // P
Q_RANK, KV_RANK, ROPE, NOPE, HV = 256, 128, 32, 64, 64
H = 8
QH = NOPE + ROPE
FXH = 64 + 16
GH, GC = 4, 64
CONV = 4
E, F, GROUPS = 16, 512, 4
BW, NB = 512, 3
ALPHA = float((2 * L) ** 0.25)
EPS = 1e-6
MLA_SCALE, FOX_SCALE, GDN_SCALE = QH ** -0.5, 64 ** -0.5, 128 ** -0.5
D_IN = 7088
NEG = -1e30

W_COLS = 520
LOADS = [("in", 0, 416), ("in", 416, 512), ("in", 928, 512), ("in", 1440, 512), ("in", 1952, 520),
         ("in", 2472, 512), ("in", 2984, 512), ("in", 3496, 520), ("uq", 0, 768), ("ukv", 0, 1024)]
LOADS += [("in", 4016 + 512 * i, 512) for i in range(6)]
LOADS += [("branch", n, 1024) for n in range(NB)]
LOADS += [("out", 512 * i, 512) for i in range(2)]
NSLOT = 3
PRE = len(LOADS)
assert PRE % NSLOT == 0
USES = PRE // NSLOT + E
J_UQ, J_UKV, J_GATE, J_BR, J_OUT = 8, 9, 10, 16, 19

C_ID, C_TRIBD, C_ONES, C_ONESBD, C_TRI, C_LVL = 0, 128, 256, 384, 512, 640
LEVELS = (1, 2, 4, 8, 16, 32)
C_CAUS = C_LVL + 128 * len(LEVELS)
C_ROT = C_CAUS + 384
C_MISC = C_ROT + 128
C_END = C_MISC + 32
PR = 2 + 1 + 1 + CONV * 12
R_QN, R_KVN, R_ON, R_CONV = 0, 2, 3, 4


def constants():
    c = np.zeros((P, C_END), np.float32)
    i, j = np.arange(P)[:, None], np.arange(P)[None, :]
    same = i // GC == j // GC
    c[:, C_ID:C_ID + P] = i == j
    c[:, C_TRIBD:C_TRIBD + P] = same & (i <= j)
    c[:, C_ONES:C_ONES + P] = 1
    c[:, C_ONESBD:C_ONESBD + P] = same
    c[:, C_TRI:C_TRI + P] = i <= j
    for n, s in enumerate(LEVELS):
        c[:, C_LVL + P * n:C_LVL + P * n + P] = (i // (2 * s) == j // (2 * s)) & (i % (2 * s) < s) & (j % (2 * s) >= s)
    causal = np.where(j <= i, 0.0, NEG)
    c[:, C_CAUS:C_CAUS + P] = causal
    c[:, C_CAUS + 2 * P:C_CAUS + 3 * P] = causal
    half = ROPE // 2
    a = np.arange(half)
    c[NOPE + half + a, C_ROT + NOPE + a] = 1
    c[NOPE + a, C_ROT + NOPE + half + a] = 1
    freq = np.float32(10000.0) ** (-a.astype(np.float32) / np.float32(half))
    c[NOPE:NOPE + half, C_MISC] = freq
    c[NOPE + half:NOPE + ROPE, C_MISC] = freq
    c[NOPE:NOPE + half, C_MISC + 1] = -1
    c[NOPE + half:NOPE + ROPE, C_MISC + 1] = 1
    c[64:72, C_MISC + 2] = 1
    c[72:80, C_MISC + 3] = 1
    for r in range(16):
        c[64 + r, C_MISC + 4 + r % 8] = 1
    ii, jj = np.arange(4)[:, None], np.arange(4)[None, :]
    c[:, C_MISC + 12:C_MISC + 28] = (jj < ii).reshape(1, 16)
    c[:, C_MISC + 28] = np.pi / 2
    c[:, C_MISC + 29] = EPS
    c[:, C_MISC + 30] = np.log(GDN_SCALE)
    return c


def interleaved():
    gdn = ["gn0", "gn1", "gn2", "gn3", "gcc", "gcb0", "gcb1", "gbt0", "gbt1", "kk0", "kk1", "kq0", "kq1",
           "tk0", "tk1", "tv0", "tv1", "tx0", "tx1"]
    groups = [["gn0", "gn1", "gn2", "gn3"], ["gcc"], ["gcb0", "gcb1"], ["gbt0", "gbt1"], ["kk0", "kk1"],
              ["kq0", "kq1"], ["tk0", "tk1"], ["tv0", "tv1"], ["tx0", "tx1"]]
    for s in LEVELS[1:]:
        groups.append([f"t1_{s}_0", f"t1_{s}_1"])
        groups.append(([f"xd_{s}_0", f"xd_{s}_1"] if s < LEVELS[-1] else []) + [f"yd_{s}_0", f"yd_{s}_1"])
    groups.append(["wt0", "wt1"])
    for n in range(4):
        groups.append([f"vn{n}"])
        groups.append([f"ot{n}"] + ([f"su{n}"] if n < 3 else []))
    groups.append(["gr0", "gr1"])
    att = []
    for a in range(2 * H + 3):
        step = []
        if a < 2 * H:
            step.append(f"S{a}")
        if 0 <= a - 2 < 2 * H:
            step.append(f"PT{a - 2}")
        if 0 <= a - 3 < 2 * H:
            step.append(f"O{a - 3}")
        att.append(step)
    gates = [[f"gate{c}"] for c in range(24)]
    out = []
    n = max(len(groups), len(att), len(gates))
    late = []
    for i in range(n):
        for seq in (groups, att, gates):
            for step in seq[i * len(seq) // n:(i + 1) * len(seq) // n]:
                if seq is gates and int(step[0][4:]) >= 16 and f"yd_{LEVELS[-1]}_1" not in out:
                    late.append(step)
                else:
                    while late and seq is gates:
                        out += late.pop(0)
                    out += step
    assert not late
    return out


MIX = interleaved()
FRONT = [f"xa{i}" for i in range(4)] + ["cq", "ckv"] + [f"gp{i}" for i in range(6)] + ["gz0", "gz1", "gab"] + \
    ["fq0", "fq1", "fk0", "fk1", "fv0", "fv1", "ff", "crms"] + [f"mq{i}" for i in range(4)] + \
    [f"mr{i}" for i in range(4)] + ["mkr"] + [f"mk{i}" for i in range(4)] + ["mv0", "mv1", "fF"]
BACK = [f"br{n}_{j}" for n in range(NB) for j in range(4)] + [f"wo{h}_{t}" for h in range(2) for t in range(TT)] + \
    [f"xb{i}" for i in range(4)] + ["rt"]
BANK_ORDER = FRONT + MIX + BACK
NBANK = 8
BANK = {name: (i % NBANK, i // NBANK) for i, name in enumerate(BANK_ORDER)}
BEFORE = [sum(1 for b, _ in BANK.values() if b == n) for n in range(NBANK)]
EXPERT = {"G0": (0, 0), "U0": (1, 0), "G1": (2, 0), "U1": (3, 0), "HT0": (4, 0), "HT1": (5, 0),
          "D0_0": (6, 0), "D0_1": (7, 0), "D1_0": (6, 1), "D1_1": (7, 1)}
PER_EXPERT = [1, 1, 1, 1, 1, 1, 2, 2]

EVENTS = """rows_ready pad_zero conv_ready silu_ready crstd_ready cn_ready small_neg small_ln gexp_ready small_ready
beta_ready fe_ready fext_ready mq_ready kr_turned kr_ready gsq_ready grstd_ready qk_ready gb_ready bb_ready
tok_diff tok_exp decay_diff decay_min decay_exp decay_ready  qd_ready y_first ct_ready
osq_ready orstd_ready og_ready p_exp p_ready gates_sig merged_ready ln_in ln_sum ln_negmean ln_sq ln_rstd x_normed
y_zero lnp_loaded""".split()


def build(nc, x, positions, w_in, w_uq, w_ukv, w_branch, w_out, w_gate, w_up, w_down, router_w,
          param_rows, row_params, ln_params, consts, out):
    ctx = ExitStack()
    with ctx:
        def sb(name, shape, dt=F32):
            return ctx.enter_context(nc.sbuf_tensor(name, shape, dt))

        def sem(name):
            return ctx.enter_context(nc.semaphore(name))

        W = sb("W", [P, NSLOT, DK * W_COLS])
        cst = sb("cst", [P, C_END])
        x_tok = sb("x_tok", [P, TT, D])
        xT = sb("xT", [P, DK, T])
        gate_lo = sb("gate_lo", [P, 16, T])
        oT = sb("oT", [P, NB, 4, T])
        mq = sb("mq", [P, H, T])
        mk = sb("mk", [P, H, T])
        mv = sb("mv", [P, TT, 512])
        fq = sb("fq", [P, H, T])
        fk = sb("fk", [P, H, T])
        fv = sb("fv", [P, TT, 512])
        kr = sb("kr", [P, 2, T])
        rtmp = sb("rtmp", [P, 2, T])
        fe = sb("fe", [P, 2, T])
        rope_c = sb("rope_c", [P, T])
        rope_s = sb("rope_s", [P, T])
        pre = sb("pre", [P, 12, T + 4])
        cv = sb("cv", [P, 12, T])
        zs = sb("zs", [P, 4, T])
        gA = sb("gA", [P, 16, P])
        gR = sb("gR", [P, 16, P])
        DEC = sb("DEC", [P, 8, P])
        EGC = sb("EGC", [P, 8, P])
        CT = sb("CT", [P, 8, P])
        vn = sb("vn", [P, 512])
        state = sb("state", [P, 4, P])
        sm = sb("sm", [P, 4, 384])
        pt = sb("pt", [P, 2, 384])
        pcols_all = sb("pcols_all", [P, L * PR])
        prow = sb("prow", [P, P])
        pc = sb("pc", [P, PR])
        rowb = sb("rowb", [P, L * 16 + E])
        rl = sb("rl", [P, 16])
        rw = sb("rw", [P, DK, E])
        small = sb("small", [P, 6, TT, 16])
        gcc = sb("gcc", [P, TT, 8])
        tex = sb("tex", [P, 4, TT, 4])
        att = sb("att", [P, 4, 32])
        lnst = sb("lnst", [P, 8])
        comb = sb("comb", [P, TT, E])

        c_raw = DEC[:, 0:6, :].rearrange("p (a b) c -> p a (b c)", b=2)
        c_sq = EGC[:, 0:6, :].rearrange("p (a b) c -> p a (b c)", b=2)
        c_n = gA[:, 0:6, :].rearrange("p (a b) c -> p a (b c)", b=2)
        c_rstd = CT[:, 0:4, :].rearrange("p (a b) c -> p a (b c)", b=2)
        gsq = gA[:, :, :].rearrange("p (a b) c -> p a (b c)", b=2)
        grstd = gR[:, :, :].rearrange("p (a b) c -> p a (b c)", b=2)
        LT, AT = gA[:, 0:8, :], gA[:, 8:16, :]
        RK, WT = gR[:, 0:8, :], gR[:, 8:16, :]
        gB, bB = CT, WT
        preflat = pre[:, :, :].rearrange("p a b -> p (a b)")
        Y, X, T1 = [preflat[:, 1024 * i:1024 * i + 1024].rearrange("p (a b) -> p a b", b=P) for i in range(3)]
        gate_hi = preflat[:, 1024:3072].rearrange("p (a b) -> p a b", b=T)
        KD = cv[:, 4:8, :].rearrange("p a (b c) -> p (a b) c", c=P)
        RV = cv[:, 8:12, :].rearrange("p a (b c) -> p (a b) c", c=P)
        merged = mq
        brtmp = mk[:, 0:4, :].rearrange("p (a b) c -> p a (b c)", b=2)
        res = fq[:, :, :].rearrange("p (t a) c -> p t (a c)", t=TT)
        lnp = fk[:, :, :].rearrange("p (t a) c -> p t (a c)", t=TT)
        y = gate_lo[:, 0:8, :].rearrange("p (t a) c -> p t (a c)", t=TT)
        hs = gate_lo[:, 8:12, :].rearrange("p (t a) c -> p t (a c)", t=TT)
        hh = gate_lo[:, 12:16, :].rearrange("p (t a) c -> p t (a c)", t=TT)
        hT = mv[:, :, :].rearrange("p t (a c) -> p t a c", c=P)

        rtt = sm[:, :, :].rearrange("p a b -> p (a b)")[:, 0:1024].rearrange("p (a b) -> p a b", b=P)

        ident = cst[:, C_ID:C_ID + P]
        tri_bd = cst[:, C_TRIBD:C_TRIBD + P]
        ones = cst[:, C_ONES:C_ONES + P]
        ones_bd = cst[:, C_ONESBD:C_ONESBD + P]
        tri = cst[:, C_TRI:C_TRI + P]
        causal = cst[:, C_CAUS:C_CAUS + 384]

        def level(n):
            return cst[:, C_LVL + P * n:C_LVL + P * n + P]

        def misc(i, lo=0, hi=P, n=1):
            return cst[lo:hi, C_MISC + i:C_MISC + i + n]

        bank = [ctx.enter_context(nc.psum_tensor(f"bank{i}", [P, 512], F32)) for i in range(NBANK)]

        filled = [sem(f"filled{i}") for i in range(NBANK)]
        drained = [sem(f"drained{i}") for i in range(NBANK)]
        ev = {name: sem(name) for name in EVENTS}
        act_chain, dve_chain = sem("act_chain"), sem("dve_chain")
        w_loaded = [sem(f"w_loaded{i}") for i in range(NSLOT)]
        w_free = [sem(f"w_free{i}") for i in range(NSLOT)]
        consts_loaded, x_loaded = sem("consts_loaded"), sem("x_loaded")
        rows_turned, pcols_ready = sem("rows_turned"), sem("pcols_ready")
        rope_chain, rope_in, rope_sin, rope_ready = sem("rope_chain"), sem("rope_in"), sem("rope_sin"), sem("rope_ready")
        dve_start = sem("dve_start")
        layer_done, layer_seen, layer_go, stored = sem("layer_done"), sem("layer_seen"), sem("layer_go"), sem("stored")

        def view(name):
            return bank[BANK[name][0]]

        def claim(pe, name):
            b, k = BANK[name]
            if k:
                pe.wait_ge(drained[b], k)
            return bank[b]

        def full(name):
            return filled[BANK[name][0]]

        def free(name):
            return drained[BANK[name][0]]

        def arrived(eng, name):
            b, k = BANK[name]
            eng.wait_ge(filled[b], k + 1)
            return bank[b]

        def landed(eng, name):
            b, k = BANK[name]
            eng.wait_ge(drained[b], k + 1)

        def gate_tile(c):
            return gate_lo[:, c, :] if c < 16 else gate_hi[:, c - 16, :]

        def arrived_e(eng, e, name):
            b, k = EXPERT[name]
            eng.wait_ge(filled[b], e * PER_EXPERT[b] + (BEFORE[b] + k + 1))
            return bank[b]

        def landed_e(eng, e, name):
            b, k = EXPERT[name]
            eng.wait_ge(drained[b], e * PER_EXPERT[b] + (BEFORE[b] + k + 1))

        def free_e(name):
            return drained[EXPERT[name][0]]

        block = ctx.enter_context(nc.Block())

        N_CONST = 5

        @block.sync
        def _(sp):
            sp.dma_start(cst[:, :], consts).then_inc(consts_loaded, 16)
            sp.dma_start(x_tok[:, :, :], x.rearrange("(t p) d -> p t d", p=P)).then_inc(x_loaded, 16)
            sp.dma_start(prow[0:L * PR, :], param_rows).then_inc(consts_loaded, 16)
            sp.dma_start(rowb[:, :], row_params.partition_broadcast(P)).then_inc(consts_loaded, 16)
            sp.dma_start(rw[:, :, :], router_w.rearrange("(k p) e -> p k e", p=P)).then_inc(consts_loaded, 16)
            sp.dma_start(kr[64:96, 0, :].bitcast(I32), positions.partition_broadcast(32)).then_inc(consts_loaded, 16)
            for s in range(NSLOT - 1):
                sp.sem_inc(w_free[s], 1)
            with sp.Fori(0, L) as l:
                for j, (kind, c0, n) in enumerate(LOADS):
                    s, k = j % NSLOT, j // NSLOT
                    if kind == "in":
                        src = w_in[bass.ds(l, 1), :, c0:c0 + n].rearrange("l (k p) n -> p (l k) n", p=P)
                    elif kind == "uq":
                        src = w_uq[bass.ds(l, 1), :, :].rearrange("l (k p) n -> p (l k) n", p=P)
                    elif kind == "ukv":
                        src = w_ukv[bass.ds(l, 1), :, :].rearrange("l (k p) n -> p (l k) n", p=P)
                    elif kind == "branch":
                        src = w_branch[bass.ds(l, 1), c0, :, :].rearrange("l (k p) n -> p (l k) n", p=P)
                    else:
                        src = w_out[bass.ds(l, 1), :, c0:c0 + n].rearrange("l (k p) n -> p (l k) n", p=P)
                    rows = src.shape[1]
                    dst = W[:, s, 0:rows * n].rearrange("p (k n) -> p k n", n=n)
                    sp.wait_ge(w_free[s], l * USES + (k + 1))
                    sp.dma_start(dst, src).then_inc(w_loaded[s], 16)
                with sp.Fori(0, E) as e:
                    for s, (wt, n) in enumerate(((w_gate, F), (w_up, F), (w_down, D))):
                        src = wt[bass.ds(l * E + e, 1), :, :].rearrange("e (k p) n -> p (e k) n", p=P)
                        dst = W[:, s, 0:src.shape[1] * n].rearrange("p (k n) -> p k n", n=n)
                        sp.wait_ge(w_free[s], l * USES + e + (PRE // NSLOT + 1))
                        sp.dma_start(dst, src).then_inc(w_loaded[s], 16)
            sp.wait_ge(layer_go, L)
            sp.dma_start(out.rearrange("(t p) d -> p t d", p=P), x_tok[:, :, :]).then_inc(stored, 16)
            sp.wait_ge(stored, 16)

        @block.tensor
        def _(pe):
            def group(o, pairs, release=None):
                for i, (a, b) in enumerate(pairs):
                    mm = pe.matmul(o, a, b, start=i == 0, stop=i == len(pairs) - 1)
                    if i == 0 and release is not None:
                        mm.then_inc(w_free[release], 1)
                return mm

            def turn(o, src, release=None):
                mm = pe.transpose(o, src, ident)
                if release is not None:
                    mm.then_inc(w_free[release], 1)
                return mm

            pe.wait_ge(consts_loaded, 16 * N_CONST)
            pe.transpose(bank[7][:, 0:L * PR], prow[0:L * PR, :], cst[0:L * PR, 0:L * PR]).then_inc(rows_turned, 1)
            pe.wait_ge(x_loaded, 16)
            pe.wait_ge(pcols_ready, 1)

            with pe.Fori(0, L) as l:
                def weights(j, n):
                    s = j % NSLOT
                    pe.wait_ge(w_loaded[s], l * (16 * USES) + 16 * (j // NSLOT + 1))
                    rows = {J_UQ: 2, J_UKV: 1}.get(j, 4 if J_BR <= j < J_OUT else DK)
                    return W[:, s, 0:rows * n].rearrange("p (k n) -> p k n", n=n)

                def turn_x(kind, first):
                    for i in range(4):
                        t, k0 = i // 2, 4 * (i % 2)
                        o = claim(pe, f"{kind}{i}")
                        for k in range(k0, k0 + 4):
                            mm = turn(o[:, (k - k0) * P:(k - k0 + 1) * P], x_tok[:, t, k * P:(k + 1) * P],
                                      first if i == 0 and k == 0 else None)
                        mm.then_inc(full(f"{kind}{i}"), 1)

                turn_x("xa", 2)
                for i in range(4):
                    landed(pe, f"xa{i}")

                def project(o, w, c, m, release=None):
                    return group(o, [(w[:, k, c:c + m], xT[:, k, :]) for k in range(DK)], release)

                def project_tok(o, w, c, n, t, release=None):
                    return group(o, [(xT[:, k, t * P:(t + 1) * P], w[:, k, c:c + n]) for k in range(DK)], release)

                w = weights(0, 416)
                o = claim(pe, "cq")
                project(o[:, 0:T], w, 0, P)
                project(o[:, T:2 * T], w, P, P).then_inc(full("cq"), 1)
                o = claim(pe, "ckv")
                project(o[:, 0:T], w, 2 * P, P)
                project(o[64:96, T:2 * T], w, 3 * P, ROPE).then_inc(full("ckv"), 1)
                for i in range(6):
                    j = 1 + i // 2
                    w = weights(j, 512)
                    o = claim(pe, f"gp{i}")
                    for c in range(2):
                        mm = project(o[:, c * T:(c + 1) * T], w, ((2 * i + c) % 4) * P, P,
                                     (j - 1) % NSLOT if i % 2 == 0 and c == 0 else None)
                    mm.then_inc(full(f"gp{i}"), 1)
                w = weights(4, 520)
                for i in range(2):
                    o = claim(pe, f"gz{i}")
                    for c in range(2):
                        mm = project(o[:, c * T:(c + 1) * T], w, (2 * i + c) * P, P, 3 % NSLOT if i == c == 0 else None)
                    mm.then_inc(full(f"gz{i}"), 1)
                o = claim(pe, "gab")
                for t in range(TT):
                    mm = project_tok(o[:, 8 * t:8 * t + 8], w, 512, 8, t)
                mm.then_inc(full("gab"), 1)
                for j, kind in ((5, "fq"), (6, "fk")):
                    w = weights(j, 512)
                    for i in range(2):
                        o = claim(pe, f"{kind}{i}")
                        for c in range(2):
                            mm = project(o[:, c * T:(c + 1) * T], w, (2 * i + c) * P, P,
                                         (j - 1) % NSLOT if i == c == 0 else None)
                        mm.then_inc(full(f"{kind}{i}"), 1)
                w = weights(7, 520)
                for t in range(TT):
                    o = claim(pe, f"fv{t}")
                    project_tok(o[:, :], w, 0, 512, t, 6 % NSLOT if t == 0 else None).then_inc(full(f"fv{t}"), 1)
                o = claim(pe, "ff")
                for t in range(TT):
                    mm = project_tok(o[:, 8 * t:8 * t + 8], w, 512, 8, t)
                mm.then_inc(full("ff"), 1)
                landed(pe, "cq")
                landed(pe, "ckv")
                o = claim(pe, "crms")
                group(o[:, 0:T], [(ones, c_sq[:, 0, :]), (ones, c_sq[:, 1, :])], 7 % NSLOT)
                group(o[:, T:2 * T], [(ones, c_sq[:, 2, :])]).then_inc(full("crms"), 1)
                w = weights(J_UQ, 768)
                pe.wait_ge(ev["cn_ready"], 3)
                for i in range(4):
                    o = claim(pe, f"mq{i}")
                    for c in range(2):
                        h = 2 * i + c
                        mm = group(o[0:QH, c * T:(c + 1) * T], [(w[:, k, h * QH:(h + 1) * QH], c_n[:, k, :]) for k in range(2)])
                    mm.then_inc(full(f"mq{i}"), 1)
                for i in range(4):
                    landed(pe, f"mq{i}")
                    o = claim(pe, f"mr{i}")
                    pe.matmul(o[0:QH, :], cst[0:QH, C_ROT:C_ROT + QH],
                              mq[0:QH, 2 * i:2 * i + 2, :].rearrange("p a b -> p (a b)"),
                              start=True, stop=True).then_inc(full(f"mr{i}"), 1)
                o = claim(pe, "mkr")
                pe.matmul(o[64:96, 0:T], cst[64:96, C_ROT + 64:C_ROT + 96], kr[64:96, 0, :],
                          start=True, stop=True).then_inc(full("mkr"), 1)
                w = weights(J_UKV, 1024)
                for i in range(4):
                    o = claim(pe, f"mk{i}")
                    for c in range(2):
                        h = 2 * i + c
                        mm = group(o[0:NOPE, c * T:(c + 1) * T], [(w[:, 0, h * P:h * P + NOPE], c_n[:, 2, :])],
                                   J_UQ % NSLOT if h == 0 else None)
                    mm.then_inc(full(f"mk{i}"), 1)
                wv = w[:, 0, :].rearrange("p (h c) -> p h c", c=P)[:, :, NOPE:P]
                for t in range(TT):
                    o = claim(pe, f"mv{t}")
                    pe.matmul(o[:, :].rearrange("p (h c) -> p h c", c=HV), c_n[:, 2, t * P:(t + 1) * P], wv,
                              start=True, stop=True).then_inc(full(f"mv{t}"), 1)
                pe.wait_ge(ev["small_ready"], 1)
                o = claim(pe, "fF")
                lf = small[:, 5, :, :]
                pe.matmul(o[64:80, 0:P], lf[:, 0, :], tri, start=True, stop=True).then_inc(w_free[J_UKV % NSLOT], 1)
                group(o[64:80, P:T], [(lf[:, 0, :], ones), (lf[:, 1, :], tri)]).then_inc(full("fF"), 1)

                def step_pe(name):
                    o = claim(pe, name)
                    if name.startswith("gate"):
                        c = int(name[4:])
                        j = J_GATE + c // 4
                        w = weights(j, 512)
                        mm = project(o[:, 0:T], w, (c % 4) * P, P,
                                     (j - 1) % NSLOT if c % 4 == 0 and c > 0 else None)
                    elif name[0] == "S" and name[1:].isdigit():
                        a = int(name[1:])
                        h = a % H
                        if a < H:
                            pe.wait_ge(ev["mq_ready"], h // 2 + 1)
                            landed(pe, f"mk{h // 2}")
                            if a == 0:
                                pe.wait_ge(ev["kr_ready"], 1)
                            q, k = mq[0:QH, h, :], mk[0:QH, h, :]
                        else:
                            if a == H:
                                for i in range(2):
                                    landed(pe, f"fq{i}")
                                    landed(pe, f"fk{i}")
                                pe.wait_ge(ev["fext_ready"], 2)
                            q, k = fq[0:FXH, h, :], fk[0:FXH, h, :]
                        pe.matmul(o[:, 0:P], q[:, 0:P], k[:, 0:P], start=True, stop=True)
                        mm = pe.matmul(o[:, P:P + T], q[:, P:T], k[:, 0:T], start=True, stop=True)
                    elif name.startswith("PT"):
                        a = int(name[2:])
                        pe.wait_ge(ev["p_ready"], a + 1)
                        for i in range(3):
                            mm = turn(o[:, i * P:(i + 1) * P], sm[:, a % 4, i * P:(i + 1) * P])
                    elif name[0] == "O":
                        a = int(name[1:])
                        h = a % H
                        landed(pe, f"PT{a}")
                        if a % H == 0:
                            for t in range(TT):
                                landed(pe, f"mv{t}" if a < H else f"fv{t}")
                        v = (mv if a < H else fv)[:, :, h * HV:(h + 1) * HV]
                        r = 64 * (h % 2)
                        p = pt[:, a % 2, :]
                        pe.matmul(o[r:r + 64, 0:T], v[:, 0, :], p[:, 0:T], start=True, stop=False)
                        mm = pe.matmul(o[r:r + 64, P:T], v[:, 1, :], p[:, T:T + P], start=False, stop=True)
                    elif name.startswith("gn"):
                        i = int(name[2:])
                        pe.wait_ge(ev["gsq_ready"], i // 2 + 1)
                        mm = pe.matmul(o[:, :], ones, gsq[:, 2 * i:2 * i + 2, :].rearrange("p a b -> p (a b)"),
                                       start=True, stop=True)
                    elif name == "gcc":
                        g = small[:, 4, :, 0:4]
                        pe.wait_ge(ev["small_ready"], 1)
                        for t in range(TT):
                            pe.matmul(o[:, 8 * t:8 * t + 4], tri_bd, g[:, t, :], start=True, stop=True)
                            mm = pe.matmul(o[:, 8 * t + 4:8 * t + 8], ones_bd, g[:, t, :], start=True, stop=True)
                    elif name.startswith("gcb") or name.startswith("gbt"):
                        t = int(name[3:])
                        src, by = (gB, tri_bd) if name.startswith("gcb") else (bB, ident)
                        pe.wait_ge(ev["gb_ready" if name.startswith("gcb") else "bb_ready"], 1)
                        for h in range(GH):
                            mm = pe.matmul(o[:, h * P:(h + 1) * P], src[:, 4 * t + h, :], by, start=True, stop=True)
                    elif name[:2] in ("kk", "kq"):
                        t = int(name[2:])
                        if name == "kk0":
                            pe.wait_ge(ev["qk_ready"], 4)
                        for h in range(GH):
                            k = cv[:, 4 + h, t * P:(t + 1) * P]
                            mm = pe.matmul(o[:, h * P:(h + 1) * P], k,
                                           k if name[:2] == "kk" else cv[:, h, t * P:(t + 1) * P], start=True, stop=True)
                    elif name[:2] in ("tk", "tv"):
                        t = int(name[2:])
                        base = 4 if name[:2] == "tk" else 8
                        for h in range(GH):
                            mm = turn(o[:, h * P:(h + 1) * P], cv[:, base + h, t * P:(t + 1) * P])
                    elif name.startswith("tx"):
                        t = int(name[2:])
                        pe.wait_ge(ev["y_first"], 1)
                        for h in range(GH):
                            mm = turn(o[:, h * P:(h + 1) * P], Y[:, 4 * t + h, :])
                    elif name.startswith("t1_"):
                        _, s, t = name.split("_")
                        n, t = LEVELS.index(int(s)), int(t)
                        pe.wait_ge(ev["ct_ready"], n)
                        landed(pe, f"tx{t}" if n == 1 else f"xd_{LEVELS[n - 1]}_{t}")
                        for h in range(GH):
                            mm = pe.matmul(o[:, h * P:(h + 1) * P], CT[:, 4 * t + h, :], X[:, 4 * t + h, :], start=True, stop=True)
                    elif name[:3] in ("xd_", "yd_"):
                        _, s, t = name.split("_")
                        n, t = LEVELS.index(int(s)), int(t)
                        landed(pe, f"t1_{s}_{t}")
                        if n > 1:
                            landed(pe, f"yd_{LEVELS[n - 1]}_{t}")
                        for h in range(GH):
                            p = 4 * t + h
                            a, b = (Y, T1) if name[0] == "x" else (T1, Y)
                            mm = pe.matmul(o[:, h * P:(h + 1) * P], a[:, p, :], b[:, p, :], start=True, stop=True)
                    elif name.startswith("wt"):
                        t = int(name[2:])
                        landed(pe, f"yd_{LEVELS[-1]}_{t}")
                        landed(pe, "tk1")
                        landed(pe, "tk0")
                        for h in range(GH):
                            p = 4 * t + h
                            mm = pe.matmul(o[:, h * P:(h + 1) * P], RK[:, p, :], Y[:, p, :], start=True, stop=True)
                    elif name.startswith("vn"):
                        n = int(name[2:])
                        t, r = n // 2, 64 * (n % 2)
                        if n == 0:
                            landed(pe, "tv0")
                            landed(pe, "tv1")
                        else:
                            landed(pe, f"wt{t}")
                            landed(pe, f"su{n - 1}")
                        for h in range(GH):
                            p = 4 * t + h
                            dst = o[r:r + 64, h * P:(h + 1) * P]
                            mm = pe.matmul(dst, Y[:, p, r:r + 64], RV[:, p, :], start=True, stop=n == 0)
                            if n:
                                mm = pe.matmul(dst, WT[:, p, r:r + 64], state[:, h, :], start=False, stop=True)
                    elif name.startswith("ot"):
                        n = int(name[2:])
                        t, r = n // 2, 64 * (n % 2)
                        landed(pe, f"vn{n}")
                        if n == 0:
                            landed(pe, "kq0")
                            landed(pe, "kq1")
                            pe.wait_ge(ev["qd_ready"], 1)
                        for h in range(GH):
                            p = 4 * t + h
                            dst = o[:, h * 64:(h + 1) * 64]
                            if n:
                                pe.matmul(dst, state[:, h, :], cv[:, h, t * P + r:t * P + r + 64], start=True, stop=False)
                            mm = pe.matmul(dst, vn[r:r + 64, h * P:(h + 1) * P], AT[r:r + 64, p, r:r + 64],
                                           start=n == 0, stop=True)
                    elif name.startswith("su"):
                        n = int(name[2:])
                        t, r = n // 2, 64 * (n % 2)
                        for h in range(GH):
                            mm = pe.matmul(o[:, h * P:(h + 1) * P], KD[r:r + 64, 4 * t + h, :],
                                           vn[r:r + 64, h * P:(h + 1) * P], start=True, stop=True)
                    elif name.startswith("gr"):
                        i = int(name[2:])
                        pe.wait_ge(ev["osq_ready"], 1)
                        mm = pe.matmul(o[:, :], ones, EGC[:, 4 * i:4 * i + 4, :].rearrange("p a b -> p (a b)"),
                                       start=True, stop=True)
                    mm.then_inc(full(name), 1)

                for name in MIX:
                    step_pe(name)

                for n in range(NB):
                    j = J_BR + n
                    w = weights(j, 1024)
                    if n == 1:
                        pe.wait_ge(ev["og_ready"], 2)
                    else:
                        for a in range(H):
                            landed(pe, f"O{a + (H if n else 0)}")
                    for i in range(4):
                        o = claim(pe, f"br{n}_{i}")
                        for c in range(2):
                            m = 2 * i + c
                            mm = group(o[:, c * T:(c + 1) * T], [(w[:, k, m * P:(m + 1) * P], oT[:, n, k, :]) for k in range(4)],
                                       (j - 1) % NSLOT if m == 0 else None)
                        mm.then_inc(full(f"br{n}_{i}"), 1)
                pe.wait_ge(ev["merged_ready"], 4)
                for i in range(2):
                    w = weights(J_OUT + i, 512)
                    for t in range(TT):
                        o = claim(pe, f"wo{i}_{t}")
                        group(o[:, :], [(merged[:, k, t * P:(t + 1) * P], w[:, k, :]) for k in range(DK)],
                              (J_OUT + i - 1) % NSLOT if t == 0 else None).then_inc(full(f"wo{i}_{t}"), 1)
                pe.wait_ge(ev["x_normed"], 2)
                turn_x("xb", None)
                for i in range(4):
                    landed(pe, f"xb{i}")
                o = claim(pe, "rt")
                for t in range(TT):
                    mm = group(o[:, t * E:(t + 1) * E], [(xT[:, k, t * P:(t + 1) * P], rw[:, k, :]) for k in range(DK)])
                mm.then_inc(full("rt"), 1)

                with pe.Fori(0, E) as e:
                    def claim_e(name):
                        b, k = EXPERT[name]
                        pe.wait_ge(drained[b], e * PER_EXPERT[b] + (BEFORE[b] + k))
                        return bank[b]

                    def weights_e(s, rows, n):
                        pe.wait_ge(w_loaded[s], l * (16 * USES) + e * 16 + 16 * (PRE // NSLOT + 1))
                        return W[:, s, 0:rows * n].rearrange("p (k n) -> p k n", n=n)

                    for t in range(TT):
                        for s, kind in enumerate("GU"):
                            w = weights_e(s, DK, F)
                            o = claim_e(f"{kind}{t}")
                            release = 2 if (kind, t) == ("G", 0) else 0 if (kind, t) == ("U", 1) else None
                            group(o[:, :], [(xT[:, k, t * P:(t + 1) * P], w[:, k, :]) for k in range(DK)], release)\
                                .then_inc(filled[EXPERT[f"{kind}{t}"][0]], 1)
                    for t in range(TT):
                        o = claim_e(f"HT{t}")
                        landed_e(pe, e, f"U{t}")
                        for k in range(4):
                            mm = turn(o[:, k * P:(k + 1) * P], hh[:, t, k * P:(k + 1) * P], 1 if t == k == 0 else None)
                        mm.then_inc(filled[EXPERT[f"HT{t}"][0]], 1)
                        w = weights_e(2, 4, D)
                        landed_e(pe, e, f"HT{t}")
                        for i in range(2):
                            o = claim_e(f"D{t}_{i}")
                            group(o[:, :], [(hT[:, t, k, :], w[:, k, i * 512:(i + 1) * 512]) for k in range(4)])\
                                .then_inc(filled[EXPERT[f"D{t}_{i}"][0]], 1)

                pe.drain().then_inc(layer_done, 1)
                pe.wait_ge(layer_go, l + 1)

        eps = misc(29)

        def halves(ap, n=2):
            return ap.rearrange("p (a b) -> p a b", a=n)

        @block.scalar
        def _(act):
            act.wait_ge(rope_in, 1)
            act.activation(rope_s[64:96, :], rtmp[64:96, 0, :], ACT.Sin).then_inc(rope_sin, 1)
            act.activation(rtmp[64:96, 1, :], rtmp[64:96, 0, :], ACT.Abs).then_inc(rope_chain, 1)
            act.wait_ge(rope_chain, 1)
            act.activation(rope_c[64:96, :], rtmp[64:96, 1, :], ACT.Sin, scale=-1.0, bias=misc(28, 64, 96)).then_inc(rope_sin, 1)

            with act.Fori(0, L) as l:
                count = [0]

                def link(ins):
                    count[0] += 1
                    ins.then_inc(act_chain, 1)
                    act.wait_ge(act_chain, count[0])

                def turned(kind, i):
                    t, k0 = i // 2, 4 * (i % 2)
                    o = arrived(act, f"{kind}{i}")
                    act.activation(xT[:, k0:k0 + 4, t * P:(t + 1) * P], halves(o[:, :], 4), ACT.Copy).then_inc(free(f"{kind}{i}"), 1)

                turned("xa", 0)
                turned("xa", 2)
                o = arrived(act, "cq")
                act.activation(c_raw[:, 0:2, :], halves(o[:, :]), ACT.Copy)
                act.activation(c_sq[:, 0:2, :], halves(o[:, :]), ACT.Square).then_inc(free("cq"), 1)
                o = arrived(act, "ckv")
                act.activation(c_raw[:, 2, :], o[:, 0:T], ACT.Copy)
                act.activation(kr[64:96, 0, :], o[64:96, T:2 * T], ACT.Copy)
                act.activation(c_sq[:, 2, :], o[:, 0:T], ACT.Square).then_inc(free("ckv"), 1)
                act.wait_ge(ev["pad_zero"], 1)
                for i in range(6):
                    o = arrived(act, f"gp{i}")
                    act.activation(pre[:, 2 * i:2 * i + 2, 3:3 + T], halves(o[:, :]), ACT.Copy).then_inc(free(f"gp{i}"), 1)
                for i in range(2):
                    o = arrived(act, f"gz{i}")
                    act.activation(zs[:, 2 * i:2 * i + 2, :], halves(o[:, :]), ACT.Silu).then_inc(free(f"gz{i}"), 1)
                for kind, dst, scale in (("fq", fq, FOX_SCALE), ("fk", fk, 1.0)):
                    for i in range(2):
                        o = arrived(act, f"{kind}{i}")
                        for r in range(2):
                            ins = act.activation(dst[0:64, 4 * i + r:4 * i + r + 3:2, :], halves(o[64 * r:64 * r + 64, :]),
                                                 ACT.Copy, scale=scale)
                        ins.then_inc(free(f"{kind}{i}"), 1)
                for t in range(TT):
                    o = arrived(act, f"fv{t}")
                    act.activation(fv[:, t, :], o[:, :], ACT.Copy).then_inc(free(f"fv{t}"), 1)
                for i in range(3):
                    act.wait_ge(ev["conv_ready"], i + 1)
                    act.activation(cv[:, 4 * i:4 * i + 4, :], cv[:, 4 * i:4 * i + 4, :], ACT.Silu).then_inc(ev["silu_ready"], 1)
                act.preload_act_table_set("natural_log_exp_and_others")
                o = arrived(act, "crms")
                act.activation(c_rstd[:, 0, :], o[:, 0:T], ACT.Ln, scale=1.0 / Q_RANK, bias=eps)
                act.activation(c_rstd[:, 1, :], o[:, T:2 * T], ACT.Ln, scale=1.0 / KV_RANK, bias=eps).then_inc(free("crms"), 1)
                landed(act, "crms")
                act.activation(c_rstd[:, 0:2, :], c_rstd[:, 0:2, :], ACT.Exp, scale=-0.5).then_inc(ev["crstd_ready"], 1)
                act.wait_ge(ev["rows_ready"], 1)
                act.activation(rl[:, 0:4], rl[:, 0:4], ACT.Exp).then_inc(ev["gexp_ready"], 1)
                act.wait_ge(ev["small_neg"], 1)
                link(act.activation(small[:, 2, :, :], small[:, 1, :, :], ACT.Exp))
                act.activation(small[:, 3, :, :], small[:, 2, :, :], ACT.Ln, bias=ones[:, 0:1]).then_inc(ev["small_ln"], 1)
                act.wait_ge(ev["small_ready"], 1)
                act.activation(small[:, 4, :, 4:8], small[:, 4, :, 4:8], ACT.Exp).then_inc(ev["beta_ready"], 1)
                for i in range(4):
                    o = arrived(act, f"mq{i}")
                    act.activation(mq[0:QH, 2 * i:2 * i + 2, :], halves(o[0:QH, :]), ACT.Copy).then_inc(free(f"mq{i}"), 1)
                for i in range(4):
                    o = arrived(act, f"mk{i}")
                    act.activation(mk[0:NOPE, 2 * i:2 * i + 2, :], halves(o[0:NOPE, :]), ACT.Copy).then_inc(free(f"mk{i}"), 1)
                for t in range(TT):
                    o = arrived(act, f"mv{t}")
                    act.activation(mv[:, t, :], o[:, :], ACT.Copy).then_inc(free(f"mv{t}"), 1)
                for i in range(2):
                    act.activation(gsq[:, 4 * i:4 * i + 4, :], cv[:, 4 * i:4 * i + 4, :], ACT.Square).then_inc(ev["gsq_ready"], 1)

                def exps(a):
                    landed(act, f"S{a}")
                    for i, (lo, hi) in enumerate(((0, P), (P, P + T))):
                        ins = act.activation(sm[:, a % 4, lo:hi], sm[:, a % 4, lo:hi], ACT.Exp, scale=-1.0,
                                             bias=att[:, 0, 2 * a + i:2 * a + i + 1], accum_out=att[:, 1, 2 * a + i:2 * a + i + 1])
                    ins.then_inc(ev["p_exp"], 1)

                def step_act(name):
                    if name.startswith("gate"):
                        c = int(name[4:])
                        if c == 16:
                            arrived(act, f"yd_{LEVELS[-1]}_1")
                            landed(act, f"xd_{LEVELS[-2]}_1")
                        o = arrived(act, name)
                        act.activation(gate_tile(c), o[:, 0:T], ACT.Copy).then_inc(free(name), 1)
                    elif name[0] == "S" and name[1:].isdigit():
                        if int(name[1:]) > 0:
                            exps(int(name[1:]) - 1)
                    elif name.startswith("PT"):
                        a = int(name[2:])
                        if a == 2 * H - 2:
                            exps(2 * H - 1)
                        o = arrived(act, name)
                        act.activation(pt[:, a % 2, :], o[:, 0:384], ACT.Copy).then_inc(free(name), 1)
                    elif name.startswith("gn"):
                        i = int(name[2:])
                        o = arrived(act, name)
                        act.activation(grstd[:, 2 * i:2 * i + 2, :], halves(o[:, :]), ACT.Ln, bias=eps).then_inc(free(name), 1)
                        landed(act, name)
                        if i < 2:
                            ins = act.activation(grstd[:, 2 * i:2 * i + 2, :], grstd[:, 2 * i:2 * i + 2, :], ACT.Exp,
                                                 scale=-0.5, bias=misc(30))
                        else:
                            ins = act.activation(grstd[:, 2 * i:2 * i + 2, :], grstd[:, 2 * i:2 * i + 2, :], ACT.Exp, scale=-0.5)
                        ins.then_inc(ev["grstd_ready"], 1)
                    elif name == "gcb0":
                        act.wait_ge(ev["tok_diff"], 1)
                        act.activation(tex[:, 1, :, :], gcc[:, :, 0:4], ACT.Exp)
                        act.activation(tex[:, 2, :, :], tex[:, 0, :, :], ACT.Exp).then_inc(ev["tok_exp"], 1)
                        row_exp(0)
                    elif name == "gcb1":
                        row_exp(1)
                        act.wait_ge(ev["decay_min"], 1)
                        act.activation(DEC[:, :, :], DEC[:, :, :], ACT.Exp).then_inc(ev["decay_exp"], 1)
                    elif name.startswith("tx") or name.startswith("t1_"):
                        t = int(name[-1])
                        o = arrived(act, name)
                        dst = (X if name.startswith("tx") else T1)[:, 4 * t:4 * t + 4, :]
                        act.activation(dst, halves(o[:, :], 4), ACT.Copy).then_inc(free(name), 1)
                    elif name.startswith("wt"):
                        t = int(name[2:])
                        o = arrived(act, name)
                        act.activation(WT[:, 4 * t:4 * t + 4, :], halves(o[:, :], 4), ACT.Copy, scale=-1.0).then_inc(free(name), 1)
                    elif name.startswith("vn"):
                        r = 64 * (int(name[2:]) % 2)
                        o = arrived(act, name)
                        act.activation(vn[r:r + 64, :], o[r:r + 64, :], ACT.Copy).then_inc(free(name), 1)
                    elif name.startswith("gr"):
                        i = int(name[2:])
                        if i == 0:
                            landed(act, "ot3")
                            landed(act, "su2")
                            act.activation(EGC[:, :, :].rearrange("p (a b) c -> p a (b c)", b=2), oT[:, 1, :, :],
                                           ACT.Square).then_inc(ev["osq_ready"], 1)
                        o = arrived(act, name)
                        act.activation(DEC[:, 4 * i:4 * i + 4, :], halves(o[:, :], 4), ACT.Ln, scale=1.0 / P,
                                       bias=eps).then_inc(free(name), 1)
                        landed(act, name)
                        act.activation(DEC[:, 4 * i:4 * i + 4, :], DEC[:, 4 * i:4 * i + 4, :], ACT.Exp,
                                       scale=-0.5).then_inc(ev["orstd_ready"], 1)

                def row_exp(t):
                    act.wait_ge(ev["decay_diff"], t + 1)
                    o = arrived(act, f"gcb{t}")
                    act.activation(EGC[:, 4 * t:4 * t + 4, :], halves(o[:, :], 4), ACT.Exp).then_inc(free(f"gcb{t}"), 1)

                for name in MIX:
                    step_act(name)

                arrived(act, f"S{2 * H - 1}")
                act.dma_start(lnp[:, :, :], ln_params[bass.ds(l * 2, 1), :, :].rearrange("l a d -> (l a) d")
                              .partition_broadcast(P)).then_inc(ev["lnp_loaded"], 16)
                for n in range(NB):
                    g = gate_lo[:, 8 * n:8 * n + 8, :] if n < 2 else gate_hi
                    landed(act, f"gate{8 * n + 7}")
                    for i in range(2):
                        act.activation(g[:, 4 * i:4 * i + 4, :], g[:, 4 * i:4 * i + 4, :], ACT.Sigmoid).then_inc(ev["gates_sig"], 1)
                act.preload_act_table_set("natural_log_exp_and_others")

                def norm_stats(which):
                    for t in range(TT):
                        if which == 0:
                            landed(act, f"wo1_{t}")
                        else:
                            act.wait_ge(ev["ln_in"], t + 1)
                        act.activation(zs[:, :, :].rearrange("p a b -> p (a b)"), res[:, t, :], ACT.Copy,
                                       accum_out=lnst[:, t:t + 1]).then_inc(ev["ln_sum"], 1)
                        act.wait_ge(ev["ln_negmean"], 2 * which + t + 1)
                        act.activation(zs[:, :, :].rearrange("p a b -> p (a b)"), res[:, t, :], ACT.Square,
                                       bias=lnst[:, 2 + t:3 + t], accum_out=lnst[:, 4 + t:5 + t]).then_inc(ev["ln_sq"], 1)
                        act.wait_ge(ev["ln_sq"], 2 * which + t + 1)
                        link(act.activation(lnst[:, 6 + t:7 + t], lnst[:, 4 + t:5 + t], ACT.Ln, scale=1.0 / D, bias=eps))
                        act.activation(lnst[:, 6 + t:7 + t], lnst[:, 6 + t:7 + t], ACT.Exp, scale=-0.5).then_inc(ev["ln_rstd"], 1)

                norm_stats(0)
                act.wait_ge(ev["x_normed"], 2)
                act.dma_start(lnp[:, :, :], ln_params[bass.ds(l * 2 + 1, 1), :, :].rearrange("l a d -> (l a) d")
                              .partition_broadcast(P)).then_inc(ev["lnp_loaded"], 16)
                turned("xb", 0)
                turned("xb", 2)
                o = arrived(act, "rt")
                act.activation(rtt[:, 0, 0:2 * E], o[:, 0:2 * E], ACT.Sigmoid).then_inc(free("rt"), 1)

                with act.Fori(0, E) as e:
                    for t in range(TT):
                        o = arrived_e(act, e, f"G{t}")
                        b, k = EXPERT[f"U{t}"]
                        act.wait_ge(drained[b], e * PER_EXPERT[b] + (BEFORE[b] + k))
                        act.activation(hs[:, t, 0:512], o[:, :], ACT.Silu).then_inc(free_e(f"G{t}"), 1)
                    for t in range(TT):
                        o = arrived_e(act, e, f"HT{t}")
                        act.activation(hT[:, t, :, :], halves(o[:, :], 4), ACT.Copy).then_inc(free_e(f"HT{t}"), 1)
                act.preload_act_table_set("natural_log_exp_and_others")
                norm_stats(1)
                act.drain().then_inc(layer_done, 1)
                act.wait_ge(layer_go, l + 1)

        @block.vector
        def _(dve):
            dve.wait_ge(rows_turned, 1)
            dve.tensor_copy(pcols_all[:, :], bank[7][:, 0:L * PR]).then_inc(pcols_ready, 1)
            dve.wait_ge(consts_loaded, 16 * N_CONST)
            ang, turns, rest = rtmp[64:96, 0, :], rtmp[64:96, 1, :], rope_s[64:96, :]
            start = [0]

            def rope_link(ins):
                start[0] += 1
                ins.then_inc(dve_start, 1)
                dve.wait_ge(dve_start, start[0])

            rope_link(dve.tensor_copy(rest, kr[64:96, 0, :].bitcast(I32)))
            rope_link(dve.tensor_scalar(ang, rest, misc(0, 64, 96), None, ALU.mult))
            magic = 1.5 * 2.0 ** 23
            rope_link(dve.tensor_scalar(rest, ang, 1.0 / (2 * np.pi), magic, ALU.mult, ALU.add))
            rope_link(dve.tensor_scalar(turns, rest, magic, None, ALU.subtract))
            two_pi, parts = 2 * np.pi, []
            for bits in (7, 12):
                q = 2.0 ** (bits - 3)
                parts.append(np.floor(two_pi * q) / q if not parts else np.round((two_pi - sum(parts)) * 2.0 ** 20) / 2.0 ** 20)
            parts.append(two_pi - sum(parts))
            for part in parts:
                rope_link(dve.scalar_tensor_tensor(ang, turns, -float(part), ang, ALU.mult, ALU.add))
            dve.tensor_scalar(ang, ang, 3.1415925, -3.1415925, ALU.min, ALU.max).then_inc(rope_in, 1)
            dve.wait_ge(rope_sin, 2)
            dve.tensor_scalar(rope_s[64:96, :], rope_s[64:96, :], misc(1, 64, 96), None, ALU.mult).then_inc(rope_ready, 1)
            dve.wait_ge(rope_ready, 1)

            with dve.Fori(0, L) as l:
                count = [0]

                def link(ins):
                    count[0] += 1
                    ins.then_inc(dve_chain, 1)
                    dve.wait_ge(dve_chain, count[0])

                dve.tensor_copy(pc[:, :], pcols_all[:, bass.ds(l * PR, PR)])
                link(dve.tensor_copy(rl[:, :], rowb[:, bass.ds(l * 16, 16)]))
                dve.sem_inc(ev["rows_ready"], 1)

                def turned(kind, i):
                    t, k0 = i // 2, 4 * (i % 2)
                    o = arrived(dve, f"{kind}{i}")
                    dve.tensor_copy(xT[:, k0:k0 + 4, t * P:(t + 1) * P], halves(o[:, :], 4)).then_inc(free(f"{kind}{i}"), 1)

                turned("xa", 1)
                turned("xa", 3)

                def conv(i):
                    landed(dve, f"gp{2 * i}")
                    landed(dve, f"gp{2 * i + 1}")
                    for j in range(CONV):
                        for c in range(4 * i, 4 * i + 4):
                            tap = pc[:, R_CONV + 12 * j + c:R_CONV + 12 * j + c + 1]
                            if j == 0:
                                ins = dve.tensor_scalar(cv[:, c, :], pre[:, c, 0:T], tap, None, ALU.mult)
                            else:
                                ins = dve.scalar_tensor_tensor(cv[:, c, :], pre[:, c, j:j + T], tap, cv[:, c, :], ALU.mult, ALU.add)
                        if j < CONV - 1:
                            link(ins)
                    ins.then_inc(ev["conv_ready"], 1)

                for i in range(3):
                    conv(i)
                o = arrived(dve, "gab")[:, 0:16].rearrange("p (t c) -> p t c", t=TT)
                dve.scalar_tensor_tensor(small[:, 0, :, 0:4], o[:, :, 0:4], -1.0,
                                         rl[:, 4:8].unsqueeze(1).broadcast_to([P, TT, 4]), ALU.mult, ALU.subtract)
                dve.tensor_copy(small[:, 0, :, 4:8], o[:, :, 4:8]).then_inc(free("gab"), 1)
                o = arrived(dve, "ff")[:, 0:16].rearrange("p (t c) -> p t c", t=TT)
                dve.tensor_tensor(small[:, 0, :, 8:16], o, rl[:, 8:16].unsqueeze(1).broadcast_to([P, TT, 8]),
                                  ALU.add).then_inc(free("ff"), 1)
                landed(dve, "gab")
                landed(dve, "ff")
                dve.scalar_tensor_tensor(small[:, 1, :, :], small[:, 0, :, :], -1.0, small[:, 0, :, :],
                                         ALU.mult, ALU.min).then_inc(ev["small_neg"], 1)
                dve.wait_ge(ev["crstd_ready"], 1)
                landed(dve, "cq")
                landed(dve, "ckv")
                for i in range(3):
                    dve.scalar_tensor_tensor(c_n[:, i, :], c_raw[:, i, :], pc[:, i:i + 1], c_rstd[:, i // 2, :],
                                             ALU.mult, ALU.mult).then_inc(ev["cn_ready"], 1)
                dve.wait_ge(ev["small_ln"], 1)
                link(dve.scalar_tensor_tensor(small[:, 4, :, :], small[:, 0, :, :], 0.0, small[:, 3, :, :], ALU.min, ALU.subtract))
                dve.tensor_copy(small[:, 5, :, 0:8], small[:, 4, :, 8:16])
                dve.tensor_scalar(small[:, 5, :, 8:16], small[:, 4, :, 8:16], -1.0, None, ALU.mult)
                dve.wait_ge(ev["gexp_ready"], 1)
                dve.tensor_tensor(small[:, 4, :, 0:4], small[:, 4, :, 0:4], rl[:, 0:4].unsqueeze(1).broadcast_to([P, TT, 4]),
                                  ALU.mult).then_inc(ev["small_ready"], 1)
                dve.wait_ge(ev["small_ready"], 1)

                def spread(dst, cols, done):
                    dve.tensor_copy(dst.rearrange("p (t h) c -> p t h c", t=TT),
                                    small[:, 4, :, cols:cols + 4].unsqueeze(3).broadcast_to([P, TT, 4, P])).then_inc(ev[done], 1)

                spread(gB[:, :, :], 0, "gb_ready")
                def both(ap):
                    return ap[64:96, :].unsqueeze(1).broadcast_to([32, 2, T])

                for i in range(4):
                    o = arrived(dve, f"mr{i}")
                    q = mq[64:96, 2 * i:2 * i + 2, :]
                    dve.tensor_tensor(rtmp[64:96, :, :], halves(o[64:96, :]), both(rope_s), ALU.mult).then_inc(free(f"mr{i}"), 1)
                    link(dve.tensor_tensor(q, q, both(rope_c), ALU.mult))
                    dve.tensor_tensor(q, q, rtmp[64:96, :, :], ALU.add).then_inc(ev["mq_ready"], 1)
                    dve.wait_ge(ev["mq_ready"], i + 1)
                o = arrived(dve, "mkr")
                dve.tensor_tensor(rtmp[64:96, 0, :], o[64:96, 0:T], rope_s[64:96, :], ALU.mult).then_inc(free("mkr"), 1)
                link(dve.tensor_tensor(kr[64:96, 1, :], kr[64:96, 0, :], rope_c[64:96, :], ALU.mult))
                dve.tensor_tensor(kr[64:96, 1, :], kr[64:96, 1, :], rtmp[64:96, 0, :], ALU.add).then_inc(ev["kr_turned"], 1)
                o = arrived(dve, "fF")
                dve.tensor_scalar(fe[64:80, 0, :], o[64:80, 0:T], misc(2, 64, 80), misc(3, 64, 80), ALU.mult, ALU.add)
                dve.tensor_scalar(fe[64:80, 1, :], o[64:80, 0:T], misc(3, 64, 80), misc(2, 64, 80), ALU.mult, ALU.add)\
                   .then_inc(free("fF"), 1)

                def rows4(ap):
                    return ap.unsqueeze(2).broadcast_to([P, 4, P])

                def masks4(ap, n=8):
                    return ap.unsqueeze(1).broadcast_to([P, n, P])

                def step_dve(name):
                    if name[0] == "S" and name[1:].isdigit():
                        a = int(name[1:])
                        if a >= 4:
                            arrived(dve, f"PT{a - 4}")
                        o = arrived(dve, name)
                        scale = MLA_SCALE if a < H else 1.0
                        for i, (lo, hi) in enumerate(((0, P), (P, P + T))):
                            ins = dve.tensor_tensor_reduce(sm[:, a % 4, lo:hi], o[:, lo:hi],
                                                           causal[:, 0:P] if i == 0 else causal[:, P:P + T],
                                                           -scale, 3e38, ALU.add, ALU.min, att[:, 0, 2 * a + i:2 * a + i + 1])
                        ins.then_inc(free(name), 1)
                    elif name.startswith("PT"):
                        a = int(name[2:])
                        dve.wait_ge(ev["p_exp"], a + 1)
                        link(dve.reciprocal(att[:, 2, 2 * a:2 * a + 2], att[:, 1, 2 * a:2 * a + 2]))
                        for i, (lo, hi) in enumerate(((0, P), (P, P + T))):
                            ins = dve.tensor_scalar(sm[:, a % 4, lo:hi], sm[:, a % 4, lo:hi],
                                                    att[:, 2, 2 * a + i:2 * a + i + 1], None, ALU.mult)
                        ins.then_inc(ev["p_ready"], 1)
                    elif name[0] == "O":
                        a = int(name[1:])
                        h, r = a % H, 64 * (a % 2)
                        o = arrived(dve, name)
                        dve.tensor_copy(oT[r:r + 64, 0 if a < H else 2, h // 2, :], o[r:r + 64, 0:T]).then_inc(free(name), 1)
                    elif name.startswith("gn"):
                        i = int(name[2:])
                        dve.wait_ge(ev["grstd_ready"], i + 1)
                        q = cv[:, 2 * i:2 * i + 2, :]
                        dve.tensor_tensor(q, q, grstd[:, 2 * i:2 * i + 2, :], ALU.mult).then_inc(ev["qk_ready"], 1)
                        if i == 3:
                            dve.wait_ge(ev["qk_ready"], 4)
                            dve.wait_ge(ev["beta_ready"], 1)
                            spread(bB, 4, "bb_ready")
                    elif name == "gcc":
                        o = arrived(dve, name)
                        dve.tensor_copy(gcc[:, :, :], o[:, 0:16].rearrange("p (t c) -> p t c", t=TT)).then_inc(free(name), 1)
                        landed(dve, name)
                        dve.tensor_tensor(tex[:, 0, :, :], gcc[:, :, 4:8], gcc[:, :, 0:4], ALU.subtract).then_inc(ev["tok_diff"], 1)
                    elif name.startswith("gcb"):
                        t = int(name[3:])
                        o = arrived(dve, name)
                        dve.tensor_tensor(DEC[:, 4 * t:4 * t + 4, :], halves(o[:, :], 4), rows4(gcc[:, t, 0:4]),
                                          ALU.subtract).then_inc(ev["decay_diff"], 1)
                        if t == 1:
                            dve.wait_ge(ev["decay_diff"], 2)
                            dve.tensor_scalar(DEC[:, :, :], DEC[:, :, :], 0.0, None, ALU.min).then_inc(ev["decay_min"], 1)
                            dve.wait_ge(ev["tok_exp"], 1)
                            link(dve.tensor_tensor(tex[:, 3, :, :], tex[:, 1, :, :], small[:, 4, :, 4:8], ALU.mult))
                    elif name.startswith("gbt"):
                        t = int(name[3:])
                        dve.wait_ge(ev["decay_ready"], 1)
                        o = arrived(dve, name)
                        dve.tensor_tensor(LT[:, 4 * t:4 * t + 4, :], halves(o[:, :], 4), DEC[:, 4 * t:4 * t + 4, :],
                                          ALU.mult).then_inc(free(name), 1)
                    elif name.startswith("kk"):
                        t = int(name[2:])
                        landed(dve, f"gbt{t}")
                        o = arrived(dve, name)
                        dve.tensor_tensor(LT[:, 4 * t:4 * t + 4, :], halves(o[:, :], 4), LT[:, 4 * t:4 * t + 4, :],
                                          ALU.mult).then_inc(free(name), 1)
                        if t == 1:
                            landed(dve, "kk0")
                            landed(dve, "kk1")
                            link(dve.tensor_tensor(T1, LT, masks4(level(0)), ALU.mult))
                            dve.tensor_tensor(Y, masks4(ident), T1, ALU.subtract).then_inc(ev["y_first"], 1)
                    elif name.startswith("kq"):
                        t = int(name[2:])
                        o = arrived(dve, name)
                        dve.tensor_tensor(AT[:, 4 * t:4 * t + 4, :], halves(o[:, :], 4), DEC[:, 4 * t:4 * t + 4, :],
                                          ALU.mult).then_inc(free(name), 1)
                    elif name == "tk1" or name == "tv1":
                        arrived(dve, name)
                        for t in range(TT):
                            o = arrived(dve, f"{name[:2]}{t}")
                            if name == "tk1":
                                dve.tensor_tensor(RK[:, 4 * t:4 * t + 4, :], halves(o[:, :], 4), rows4(tex[:, 3, t, :]), ALU.mult)
                                ins = dve.tensor_tensor(KD[:, 4 * t:4 * t + 4, :], halves(o[:, :], 4), rows4(tex[:, 2, t, :]), ALU.mult)
                            else:
                                ins = dve.tensor_tensor(RV[:, 4 * t:4 * t + 4, :], halves(o[:, :], 4),
                                                        rows4(small[:, 4, t, 4:8]), ALU.mult)
                            ins.then_inc(free(f"{name[:2]}{t}"), 1)
                    elif name[:3] in ("xd_", "yd_"):
                        t = int(name[-1])
                        dst = (X if name[0] == "x" else Y)[:, 4 * t:4 * t + 4, :]
                        o = arrived(dve, name)
                        if name.startswith("xd_2_"):
                            landed(dve, f"tx{t}")
                        dve.tensor_tensor(dst, dst, halves(o[:, :], 4), ALU.subtract).then_inc(free(name), 1)
                    elif name.startswith("ot"):
                        n = int(name[2:])
                        o = arrived(dve, name)
                        dve.tensor_copy(oT[:, 1, :, n * GC:(n + 1) * GC], o[:, 0:GH * GC].rearrange("p (h c) -> p h c", c=GC))\
                           .then_inc(free(name), 1)
                        if 0 < n < 3:
                            t, r = n // 2, 64 * (n % 2)
                            last = EGC[:, 4 * t:4 * t + 4, r + 63]
                            link(dve.tensor_tensor(state[:, :, :], state[:, :, :], rows4(last), ALU.mult))
                    elif name.startswith("su"):
                        o = arrived(dve, name)
                        if name == "su0":
                            dve.tensor_copy(state[:, :, :], halves(o[:, :], 4)).then_inc(free(name), 1)
                        else:
                            dve.tensor_tensor(state[:, :, :], state[:, :, :], halves(o[:, :], 4), ALU.add).then_inc(free(name), 1)
                    elif name == "gr1":
                        og = oT[:, 1, :, :].rearrange("p h c -> p (h c)")
                        for i in range(2):
                            dve.wait_ge(ev["orstd_ready"], i + 1)
                            part = og[:, 512 * i:512 * i + 512]
                            link(dve.scalar_tensor_tensor(part, part, pc[:, R_ON:R_ON + 1],
                                                          DEC[:, 4 * i:4 * i + 4, :].rearrange("p a b -> p (a b)"), ALU.mult, ALU.mult))
                            dve.tensor_tensor(part, part, zs[:, 2 * i:2 * i + 2, :].rearrange("p a b -> p (a b)"), ALU.mult)\
                               .then_inc(ev["og_ready"], 1)

                for name in MIX:
                    step_dve(name)

                for n in range(NB):
                    for i in range(4):
                        dve.wait_ge(ev["gates_sig"], 2 * n + i // 2 + 1)
                        g = (gate_lo[:, 8 * n + 2 * i:8 * n + 2 * i + 2, :] if n < 2 else gate_hi[:, 2 * i:2 * i + 2, :])
                        o = arrived(dve, f"br{n}_{i}")
                        m = merged[:, 2 * i:2 * i + 2, :]
                        if n == 0:
                            dve.tensor_tensor(m, halves(o[:, :]), g, ALU.mult).then_inc(free(f"br{n}_{i}"), 1)
                        else:
                            dve.tensor_tensor(brtmp[:, i % 2, :], o[:, :], g.rearrange("p a b -> p (a b)"), ALU.mult)\
                               .then_inc(free(f"br{n}_{i}"), 1)
                            landed(dve, f"br{n}_{i}")
                            ins = dve.tensor_tensor(m, m, halves(brtmp[:, i % 2, :]), ALU.add)
                            if n == 1:
                                link(ins)
                            else:
                                ins.then_inc(ev["merged_ready"], 1)

                def norm(which):
                    for t in range(TT):
                        dve.wait_ge(ev["ln_sum"], 2 * which + t + 1)
                        dve.tensor_scalar(lnst[:, 2 + t:3 + t], lnst[:, t:t + 1], -1.0 / D, None, ALU.mult).then_inc(ev["ln_negmean"], 1)
                        dve.wait_ge(ev["ln_rstd"], 2 * which + t + 1)
                        link(dve.tensor_scalar(res[:, t, :], res[:, t, :], lnst[:, 2 + t:3 + t], lnst[:, 6 + t:7 + t],
                                               ALU.add, ALU.mult))
                        dve.wait_ge(ev["lnp_loaded"], 16 * (which + 1))
                        link(dve.tensor_tensor(res[:, t, :], res[:, t, :], lnp[:, 0, :], ALU.mult))
                        dve.tensor_tensor(x_tok[:, t, :], res[:, t, :], lnp[:, 1, :], ALU.add).then_inc(ev["x_normed"], 1)

                for i in range(2):
                    for t in range(TT):
                        c = slice(512 * i, 512 * i + 512)
                        o = arrived(dve, f"wo{i}_{t}")
                        dve.scalar_tensor_tensor(res[:, t, c], x_tok[:, t, c], ALPHA, o[:, :], ALU.mult, ALU.add)\
                           .then_inc(free(f"wo{i}_{t}"), 1)
                norm(0)
                turned("xb", 1)
                turned("xb", 3)

                landed(dve, "rt")
                score = rtt[:, 0, 0:32]
                sel, flag, tmp = rtt[:, 1, 0:32], rtt[:, 2, 0:32], rtt[:, 3, 0:32]
                big, big2 = rtt[:, 4, :], rtt[:, 5, :]
                gsc, gfl, den = rtt[:, 6, 0:8], rtt[:, 6, 8:16], rtt[:, 6, 16:18]
                rb = rowb[:, L * 16:L * 16 + E].unsqueeze(1).broadcast_to([P, TT, E])
                link(dve.tensor_tensor(halves(sel), halves(score), rb, ALU.add))

                def best(values, n, limit, out_flag):
                    vj = values.rearrange("p (g e) -> p g e", e=4).unsqueeze(2).broadcast_to([P, n, 4, 4])
                    vi = values.rearrange("p (g e) -> p g e", e=4).unsqueeze(3).broadcast_to([P, n, 4, 4])
                    b1 = big[:, 0:16 * n].rearrange("p (g i j) -> p g i j", i=4, j=4)
                    b2 = big2[:, 0:16 * n].rearrange("p (g i j) -> p g i j", i=4, j=4)
                    dve.tensor_tensor(b1, vj, vi, ALU.is_gt)
                    link(dve.tensor_tensor(b2, vj, vi, ALU.is_equal))
                    b2r = big2[:, 0:16 * n].rearrange("p (g m) -> p g m", m=16)
                    link(dve.tensor_tensor(b2r, b2r, misc(12, n=16).unsqueeze(1).broadcast_to([P, n, 16]), ALU.mult))
                    link(dve.tensor_tensor(big[:, 0:16 * n], big[:, 0:16 * n], big2[:, 0:16 * n], ALU.add))
                    link(dve.tensor_reduce(tmp[:, 0:4 * n], big[:, 0:16 * n].rearrange("p (m j) -> p m j", j=4), AX.X, ALU.add))
                    link(dve.tensor_scalar(out_flag, tmp[:, 0:4 * n], limit - 0.5, None, ALU.is_lt))

                best(sel, 8, 2, flag)
                link(dve.tensor_tensor(tmp, sel, flag, ALU.mult))
                link(dve.tensor_reduce(gsc, tmp.rearrange("p (g e) -> p g e", e=4), AX.X, ALU.add))
                best(gsc, 2, 1, gfl)
                link(dve.tensor_tensor(flag.rearrange("p (g e) -> p g e", e=4), flag.rearrange("p (g e) -> p g e", e=4),
                                       gfl.unsqueeze(2).broadcast_to([P, 8, 4]), ALU.mult))
                link(dve.tensor_tensor(tmp, flag, score, ALU.mult))
                link(dve.tensor_reduce(den, halves(tmp), AX.X, ALU.add))
                link(dve.reciprocal(den, den))
                link(dve.tensor_tensor(comb[:, :, :], halves(tmp), den.unsqueeze(2).broadcast_to([P, TT, E]), ALU.mult))
                dve.wait_ge(ev["y_zero"], 1)

                with dve.Fori(0, E) as e:
                    for t in range(TT):
                        landed_e(dve, e, f"G{t}")
                        o = arrived_e(dve, e, f"U{t}")
                        dve.tensor_tensor(hh[:, t, 0:512], o[:, :], hs[:, t, 0:512], ALU.mult).then_inc(free_e(f"U{t}"), 1)
                    for t in range(TT):
                        for i in range(2):
                            o = arrived_e(dve, e, f"D{t}_{i}")
                            b, k = EXPERT[f"D{t}_{i}"]
                            dve.wait_ge(drained[b], e * PER_EXPERT[b] + (BEFORE[b] + k - 1))
                            part = y[:, t, 512 * i:512 * i + 512]
                            dve.scalar_tensor_tensor(part, o[:, :], comb[:, t, bass.ds(e, 1)], part, ALU.mult, ALU.add)\
                               .then_inc(free_e(f"D{t}_{i}"), 1)
                for t in range(TT):
                    for b in (6, 7):
                        dve.wait_ge(drained[b], BEFORE[b] + 2 * E)
                    dve.scalar_tensor_tensor(res[:, t, :], x_tok[:, t, :], ALPHA, y[:, t, :], ALU.mult, ALU.add)\
                       .then_inc(ev["ln_in"], 1)
                norm(1)
                dve.drain().then_inc(layer_done, 1)
                dve.wait_ge(layer_go, l + 1)

        @block.gpsimd
        def _(pool):
            with pool.Fori(0, L) as l:
                pool.memset(pre[:, :, 0:3], 0.0).then_inc(ev["pad_zero"], 1)
                pool.wait_ge(ev["pad_zero"], 1)
                pool.wait_ge(ev["kr_turned"], 1)
                pool.tensor_copy(mk[64:96, :, :], kr[64:96, 1, :].unsqueeze(1).broadcast_to([32, H, T])).then_inc(ev["kr_ready"], 1)
                pool.wait_ge(ev["kr_ready"], 1)
                pool.wait_ge(ev["decay_exp"], 1)
                pool.tensor_tensor(DEC[:, :, :], DEC[:, :, :], tri_bd.unsqueeze(1).broadcast_to([P, 8, P]), ALU.mult)\
                    .then_inc(ev["decay_ready"], 1)
                pool.wait_ge(ev["decay_ready"], 1)
                landed(pool, "fF")
                pool.tensor_copy(fq[64:80, :, :], fe[64:80, 0, :].unsqueeze(1).broadcast_to([16, H, T])).then_inc(ev["fext_ready"], 1)
                pool.wait_ge(ev["fext_ready"], 1)
                pool.tensor_tensor(fk[64:80, :, :], fe[64:80, 1, :].unsqueeze(1).broadcast_to([16, H, T]),
                                   cst[64:80, C_MISC + 4:C_MISC + 12].unsqueeze(2).broadcast_to([16, H, T]), ALU.mult)\
                    .then_inc(ev["fext_ready"], 1)
                pool.wait_ge(ev["fext_ready"], 2)
                landed(pool, "kk0")
                landed(pool, "kk1")
                for n in range(1, len(LEVELS)):
                    if n > 1:
                        arrived(pool, f"t1_{LEVELS[n - 1]}_1")
                    pool.tensor_tensor(CT[:, :, :], LT, level(n).unsqueeze(1).broadcast_to([P, 8, P]), ALU.mult)\
                        .then_inc(ev["ct_ready"], 1)
                    if n == 1:
                        arrived(pool, "kq1")
                        landed(pool, "gcb0")
                        landed(pool, "gcb1")
                        for t in range(TT):
                            q = cv[:, 0:4, t * P:(t + 1) * P]
                            ins = pool.tensor_tensor(q, q, EGC[:, 4 * t:4 * t + 4, :], ALU.mult)
                        ins.then_inc(ev["qd_ready"], 1)
                pool.wait_ge(ev["x_normed"], 2)
                pool.memset(y, 0.0).then_inc(ev["y_zero"], 1)
                pool.drain()
                pool.wait_ge(layer_done, l * 3 + 3)
                pool.sem_inc(layer_seen, 1)
                for s in filled + drained + list(ev.values()) + [act_chain, dve_chain]:
                    pool.sem_clear(s)
                pool.sem_inc(layer_go, 1)


def kernel(x, positions, w_in, mla_q_norm, mla_w_uq, mla_kv_norm, mla_w_ukv, gdn_conv, gdn_a_log, gdn_dt_bias,
           gdn_out_norm, fox_f_bias, w_branch, w_out, ln1_g, ln1_b, router_w, router_bias,
           exp_w_gate, exp_w_up, exp_w_down, ln2_g, ln2_b):
    import concourse.bacc as _bacc
    from concourse.bass_utils import run_bass_kernel_spmd as _run

    def arr(a):
        return np.ascontiguousarray(a)

    rows = []
    for l in range(L):
        rows += [arr(mla_q_norm[l]).reshape(2, P), arr(mla_kv_norm[l]).reshape(1, P), arr(gdn_out_norm[l]).reshape(1, P),
                 arr(gdn_conv[l]).reshape(CONV * 12, P)]
    row_params = np.concatenate([np.concatenate([arr(gdn_a_log[l]), arr(gdn_dt_bias[l]), arr(fox_f_bias[l])]) for l in range(L)]
                                + [arr(router_bias)])
    ln_params = np.concatenate([np.stack([arr(g[l]), arr(b[l])])[None] for l in range(L)
                                for g, b in ((ln1_g, ln1_b), (ln2_g, ln2_b))])
    arrays = {
        "x": arr(x).reshape(T, D), "positions": arr(positions).reshape(T), "w_in": arr(w_in), "w_uq": arr(mla_w_uq),
        "w_ukv": arr(mla_w_ukv), "w_branch": arr(w_branch), "w_out": arr(w_out),
        "w_gate": arr(exp_w_gate).reshape(L * E, D, F), "w_up": arr(exp_w_up).reshape(L * E, D, F),
        "w_down": arr(exp_w_down).reshape(L * E, F, D), "router_w": arr(router_w), "param_rows": np.concatenate(rows),
        "row_params": row_params, "ln_params": ln_params, "consts": constants(),
    }
    nc = _bacc.Bacc("TRN2", target_bir_lowering=False, num_devices=1, dynamic_dma_scratch_size=1024)
    args = {n: nc.dram_tensor(f"in_{n}", a.shape, mybir.dt.from_np(a.dtype), kind="ExternalInput").ap() for n, a in arrays.items()}
    o = nc.dram_tensor("out", (T, D), F32, kind="ExternalOutput").ap()
    build(nc, *args.values(), o)
    r = _run(nc, [{f"in_{n}": a for n, a in arrays.items()}], core_ids=[0])
    return np.asarray(r.results[0]["out"]).reshape(1, T, D)
```

```python
from contextlib import ExitStack

import concourse.bass as bass
import numpy as np
from concourse import mybir

F32 = mybir.dt.float32
I32 = mybir.dt.int32
ALU = mybir.AluOpType
ACT = mybir.ActivationFunctionType
AX = mybir.AxisListType

P = 128
D, T, L = 1024, 256, 2
TT = T // P
DK = D // P
Q_RANK, KV_RANK, ROPE, NOPE, HV = 256, 128, 32, 64, 64
H = 8
QH = NOPE + ROPE
FXH = 64 + 16
GH, GC = 4, 64
CONV = 4
E, F = 16, 512
CAP = 64
BW, NB = 512, 3
ALPHA = float((2 * L) ** 0.25)
EPS = 1e-6
MLA_SCALE, FOX_SCALE, GDN_SCALE = QH ** -0.5, 64 ** -0.5, 128 ** -0.5
D_IN = 7088
NEG = -1e30

W_COLS = 520
LOADS = [("in", 0, 416), ("in", 416, 512), ("in", 928, 512), ("in", 1440, 512), ("in", 1952, 520),
         ("in", 2472, 512), ("in", 2984, 512), ("in", 3496, 520), ("uq", 0, 768), ("ukv", 0, 1024)]
LOADS += [("in", 4016 + 512 * i, 512) for i in range(6)]
LOADS += [("branch", n, 1024) for n in range(NB)]
LOADS += [("out", 512 * i, 512) for i in range(2)]
NSLOT = 3
PRE = len(LOADS)
assert PRE % NSLOT == 0
PAIRS = E // 2
USES = PRE // NSLOT + PAIRS
J_UQ, J_UKV, J_GATE, J_BR, J_OUT = 8, 9, 10, 16, 19

C_ID, C_TRIBD, C_ONES, C_ONESBD, C_TRI, C_LVL = 0, 128, 256, 384, 512, 640
LEVELS = (1, 2, 4, 8, 16, 32)
C_CAUS = C_LVL + 128 * len(LEVELS)
C_ROT = C_CAUS + 384
C_SLOT = C_ROT + 128
C_MISC = C_SLOT + P
C_END = C_MISC + 32
PR = 2 + 1 + 1 + CONV * 12
R_QN, R_KVN, R_ON, R_CONV = 0, 2, 3, 4


def constants():
    c = np.zeros((P, C_END), np.float32)
    i, j = np.arange(P)[:, None], np.arange(P)[None, :]
    same = i // GC == j // GC
    c[:, C_ID:C_ID + P] = i == j
    c[:, C_TRIBD:C_TRIBD + P] = same & (i <= j)
    c[:, C_ONES:C_ONES + P] = 1
    c[:, C_ONESBD:C_ONESBD + P] = same
    c[:, C_TRI:C_TRI + P] = i <= j
    for n, s in enumerate(LEVELS):
        c[:, C_LVL + P * n:C_LVL + P * n + P] = (i // (2 * s) == j // (2 * s)) & (i % (2 * s) < s) & (j % (2 * s) >= s)
    causal = np.where(j <= i, 0.0, NEG)
    c[:, C_CAUS:C_CAUS + P] = causal
    c[:, C_CAUS + 2 * P:C_CAUS + 3 * P] = causal
    half = ROPE // 2
    a = np.arange(half)
    c[NOPE + half + a, C_ROT + NOPE + a] = 1
    c[NOPE + a, C_ROT + NOPE + half + a] = 1
    freq = np.float32(10000.0) ** (-a.astype(np.float32) / np.float32(half))
    c[NOPE:NOPE + half, C_MISC] = freq
    c[NOPE + half:NOPE + ROPE, C_MISC] = freq
    c[NOPE:NOPE + half, C_MISC + 1] = -1
    c[NOPE + half:NOPE + ROPE, C_MISC + 1] = 1
    c[64:72, C_MISC + 2] = 1
    c[72:80, C_MISC + 3] = 1
    for r in range(16):
        c[64 + r, C_MISC + 4 + r % 8] = 1
    ii, jj = np.arange(4)[:, None], np.arange(4)[None, :]
    c[:, C_MISC + 12:C_MISC + 28] = (jj < ii).reshape(1, 16)
    c[:, C_SLOT:C_SLOT + P] = np.arange(P) % CAP
    c[:, C_MISC + 28] = np.pi / 2
    c[:, C_MISC + 29] = EPS
    c[:, C_MISC + 30] = np.log(GDN_SCALE)
    return c


PT_LAG = 3


def interleaved():
    groups = [["gn0", "gn1", "gn2", "gn3"], ["gcc"], ["gcb0", "gcb1"], ["gbt0", "gbt1"], ["kk0", "kk1"],
              ["kq0", "kq1"], ["tk0", "tk1"], ["tv0", "tv1"], ["tx0", "tx1"]]
    for s in LEVELS[1:]:
        groups.append([f"t1_{s}_0", f"t1_{s}_1"])
        groups.append(([f"xd_{s}_0", f"xd_{s}_1"] if s < LEVELS[-1] else []) + [f"yd_{s}_0", f"yd_{s}_1"])
    groups.append(["wt0", "wt1"])
    for n in range(4):
        groups.append([f"vn{n}"])
        groups.append([f"ot{n}"] + ([f"su{n}"] if n < 3 else []))
    groups.append(["gr0", "gr1"])
    att = []
    for a in range(2 * H + PT_LAG + 1):
        step = []
        if a < 2 * H:
            step.append(f"S{a}")
        if 0 <= a - PT_LAG < 2 * H:
            step.append(f"PT{a - PT_LAG}")
        if 0 <= a - PT_LAG - 1 < 2 * H:
            step.append(f"O{a - PT_LAG - 1}")
        att.append(step)
    gates = [[f"gate{c}"] for c in range(24)]
    out = []
    n = max(len(groups), len(att), len(gates))
    late = []
    for i in range(n):
        for seq in (groups, att, gates):
            for step in seq[i * len(seq) // n:(i + 1) * len(seq) // n]:
                if seq is gates and int(step[0][4:]) >= 16 and f"yd_{LEVELS[-1]}_1" not in out:
                    late.append(step)
                else:
                    while late and seq is gates:
                        out += late.pop(0)
                    out += step
    assert not late
    return out


MIX = interleaved()
FRONT = [f"xa{i}" for i in range(4)] + ["cq", "ckv"] + [f"gp{i}" for i in range(6)] + ["gz0", "gz1", "gab"] + \
    ["fq0", "fq1", "fk0", "fk1", "fv0", "fv1", "ff", "crms"] + [f"mq{i}" for i in range(4)] + \
    [f"mr{i}" for i in range(4)] + ["mkr"] + [f"mk{i}" for i in range(4)] + ["mv0", "mv1", "fF"]
BACK = [f"br{n}_{j}" for n in range(NB) for j in range(4)] + [f"wo{h}_{t}" for h in range(2) for t in range(TT)] + \
    [f"xb{i}" for i in range(4)] + ["rt", "rp"]
NBANK = 8
FIXED = {"XG0": 0, "XT0": 3, "Y0": 4, "Y1": 5, "Y2": 6, "Y3": 7}
BANK_ORDER = FRONT + MIX + BACK
BANK, BEFORE = {}, [0] * NBANK
for _i, _name in enumerate(BANK_ORDER + list(FIXED)):
    _b = FIXED.get(_name, _i % NBANK)
    BANK[_name] = (_b, BEFORE[_b])
    BEFORE[_b] += 1
EXPERT = {"GU": (2, 0), "XG": (0, 0), "HG": (1, 0), "XT": (3, 0), "DN": (0, 1)}
PER_EXPERT = [2, 1, 1, 1]
AFTER = [BEFORE[b] + E * (PER_EXPERT[b] if b < 4 else 0) for b in range(NBANK)]
DENSE = {"G0": (0, 0), "U0": (1, 0), "G1": (2, 0), "U1": (3, 0), "HT0": (4, 0), "HT1": (5, 0),
         "D0_0": (6, 0), "D0_1": (7, 0), "D1_0": (6, 1), "D1_1": (7, 1)}
PER_DENSE = [1, 1, 1, 1, 1, 1, 2, 2]

EVENTS = """rows_ready pad_zero conv_ready silu_ready crstd_ready cn_ready small_neg small_ln gexp_ready small_ready
beta_ready fext_ready mq_ready kr_turned kr_ready gsq_ready grstd_ready qk_ready gb_ready bb_ready
tok_diff tok_exp decay_diff decay_min decay_exp decay_ready  qd_ready y_first ct_ready
osq_ready orstd_ready og_ready p_exp p_ready gates_sig merged_ready ln_in ln_sum ln_negmean ln_sq ln_rstd x_normed
route_mask slots_ready moe_zero g_made gw_made silu_gate dense_done_sp lnp_loaded""".split()


def build(nc, x, positions, w_in, w_uq, w_ukv, w_branch, w_out, w_gate, w_up, w_down, router_w,
          param_rows, row_params, ln_params, consts, out):
    ctx = ExitStack()
    with ctx:
        def sb(name, shape, dt=F32):
            return ctx.enter_context(nc.sbuf_tensor(name, shape, dt))

        def sem(name):
            return ctx.enter_context(nc.semaphore(name))

        W = sb("W", [P, NSLOT, DK * W_COLS])
        cst = sb("cst", [P, C_END])
        x_tok = sb("x_tok", [P, TT, D])
        xT = sb("xT", [P, DK, T])
        gate_lo = sb("gate_lo", [P, 16, T])
        oT = sb("oT", [P, NB, 4, T])
        mq = sb("mq", [P, H, T])
        mk = sb("mk", [P, H, T])
        mv = sb("mv", [P, TT, 512])
        fq = sb("fq", [P, H, T])
        fk = sb("fk", [P, H, T])
        fv = sb("fv", [P, TT, 512])
        kr = sb("kr", [P, 2, T])
        rtmp = sb("rtmp", [P, 2, T])
        fe = sb("fe", [P, 2, T])
        rope_c = sb("rope_c", [P, T])
        rope_s = sb("rope_s", [P, T])
        zs = sb("zs", [P, 4, T])
        gdn_mem = sb("gdn_mem", [P, 12 * (T + 4) + 12 * T + 7 * 1024])
        vn = sb("vn", [P, 512])
        state = sb("state", [P, 4, P])
        sm = sb("sm", [P, 4, 384])
        pt = sb("pt", [P, 2, 384])
        pcols_all = sb("pcols_all", [P, L * PR])
        prow = sb("prow", [P, P])
        pc = sb("pc", [P, PR])
        rowb = sb("rowb", [P, L * 16 + E])
        rl = sb("rl", [P, 16])
        rw = sb("rw", [P, DK, E])
        small = sb("small", [P, 6, TT, 16])
        gcc = sb("gcc", [P, TT, 8])
        tex = sb("tex", [P, 4, TT, 4])
        att = sb("att", [P, 4, 32])
        lnst = sb("lnst", [P, 8])
        over_flag = sb("over_flag", [P, 1], I32)

        carved = [0]

        def carve(a, b):
            lo = carved[0]
            carved[0] += a * b
            return gdn_mem[:, lo:lo + a * b].rearrange("p (a b) -> p a b", b=b)

        pre = carve(12, T + 4)
        cv = carve(12, T)
        gA, gR, DEC, EGC, CT = carve(16, P), carve(16, P), carve(8, P), carve(8, P), carve(8, P)

        def slot_mem(s, rows, n):
            flat = W[:, s, 0:rows * n] if s < NSLOT else gdn_mem[:, (s - NSLOT) * DK * F:(s - NSLOT) * DK * F + rows * n]
            return flat.rearrange("p (k n) -> p k n", n=n)

        c_raw = DEC[:, 0:6, :].rearrange("p (a b) c -> p a (b c)", b=2)
        c_sq = EGC[:, 0:6, :].rearrange("p (a b) c -> p a (b c)", b=2)
        c_n = gA[:, 0:6, :].rearrange("p (a b) c -> p a (b c)", b=2)
        c_rstd = CT[:, 0:4, :].rearrange("p (a b) c -> p a (b c)", b=2)
        gsq = gA[:, :, :].rearrange("p (a b) c -> p a (b c)", b=2)
        grstd = gR[:, :, :].rearrange("p (a b) c -> p a (b c)", b=2)
        LT, AT = gA[:, 0:8, :], gA[:, 8:16, :]
        RK, WT = gR[:, 0:8, :], gR[:, 8:16, :]
        gB, bB = CT, WT
        preflat = gdn_mem[:, 0:12 * (T + 4)]
        Y, X, T1 = [preflat[:, 1024 * i:1024 * i + 1024].rearrange("p (a b) -> p a b", b=P) for i in range(3)]
        gate_hi = preflat[:, 1024:3072].rearrange("p (a b) -> p a b", b=T)
        KD = cv[:, 4:8, :].rearrange("p a (b c) -> p (a b) c", c=P)
        RV = cv[:, 8:12, :].rearrange("p a (b c) -> p (a b) c", c=P)
        merged = mq
        brtmp = mk[:, 0:4, :].rearrange("p (a b) c -> p a (b c)", b=2)
        res = fq[:, :, :].rearrange("p (t a) c -> p t (a c)", t=TT)
        lnp = fk[:, :, :].rearrange("p (t a) c -> p t (a c)", t=TT)
        gflat = gate_lo[:, :, :].rearrange("p a b -> p (a b)")
        xg, xgT, hs, hh, hg, oe = [gflat[:, 512 * i:512 * i + 512] for i in range(6)]
        G = gflat[:, 3072:3072 + TT * CAP].rearrange("p (t c) -> p t c", t=TT)
        Gw = gflat[:, 3200:3200 + TT * P].rearrange("p (t c) -> p t c", t=TT)
        dense_s = gflat[:, 0:1024].rearrange("p (t c) -> p t c", t=TT)
        dense_h = gflat[:, 1024:2048].rearrange("p (t c) -> p t c", t=TT)
        hT = mv[:, :, :].rearrange("p t (a c) -> p t a c", c=P)
        smflat = sm[:, :, :].rearrange("p a b -> p (a b)")
        rtt = smflat[:, 0:1024].rearrange("p (a b) -> p a b", b=P)
        slot = smflat[:, 1024:1024 + TT * (E + 1)].rearrange("p (t e) -> p t e", t=TT)
        comb = smflat[:, 1088:1088 + TT * (E + 1)].rearrange("p (t e) -> p t e", t=TT)
        comb_over = smflat[:, 1152:1152 + TT * E].rearrange("p (t e) -> p t e", t=TT)
        over = smflat[:, 1216:1218]

        ident = cst[:, C_ID:C_ID + P]
        tri_bd = cst[:, C_TRIBD:C_TRIBD + P]
        ones = cst[:, C_ONES:C_ONES + P]
        ones_bd = cst[:, C_ONESBD:C_ONESBD + P]
        tri = cst[:, C_TRI:C_TRI + P]
        causal = cst[:, C_CAUS:C_CAUS + 384]

        def level(n):
            return cst[:, C_LVL + P * n:C_LVL + P * n + P]

        def misc(i, lo=0, hi=P, n=1):
            return cst[lo:hi, C_MISC + i:C_MISC + i + n]

        bank = [ctx.enter_context(nc.psum_tensor(f"bank{i}", [P, 512], F32)) for i in range(NBANK)]

        filled = [sem(f"filled{i}") for i in range(NBANK)]
        drained = [sem(f"drained{i}") for i in range(NBANK)]
        ev = {name: sem(name) for name in EVENTS}
        act_chain, dve_chain = sem("act_chain"), sem("dve_chain")
        w_loaded = [sem(f"w_loaded{i}") for i in range(2 * NSLOT)]
        w_free = [sem(f"w_free{i}") for i in range(2 * NSLOT)]
        gdn_mem_free, gdn_mem_seen = sem("gdn_mem_free"), sem("gdn_mem_seen")
        consts_loaded, x_loaded = sem("consts_loaded"), sem("x_loaded")
        rows_turned, pcols_ready = sem("rows_turned"), sem("pcols_ready")
        rope_chain, rope_in, rope_sin, rope_ready = sem("rope_chain"), sem("rope_in"), sem("rope_sin"), sem("rope_ready")
        dve_start = sem("dve_start")
        over_known, over_seen = sem("over_known"), sem("over_seen")
        dense_loaded = [sem(f"dense_loaded{i}") for i in range(NSLOT)]
        dense_free = [sem(f"dense_free{i}") for i in range(NSLOT)]
        layer_done, layer_seen, layer_go, stored = sem("layer_done"), sem("layer_seen"), sem("layer_go"), sem("stored")

        def view(name):
            return bank[BANK[name][0]]

        def claim(pe, name):
            b, k = BANK[name]
            if k:
                pe.wait_ge(drained[b], k)
            return bank[b]

        def full(name):
            return filled[BANK[name][0]]

        def free(name):
            return drained[BANK[name][0]]

        def arrived(eng, name):
            b, k = BANK[name]
            eng.wait_ge(filled[b], k + 1)
            return bank[b]

        def landed(eng, name):
            b, k = BANK[name]
            eng.wait_ge(drained[b], k + 1)

        def gate_tile(c):
            return gate_lo[:, c, :] if c < 16 else gate_hi[:, c - 16, :]

        def arrived_e(eng, e, name):
            b, k = EXPERT[name]
            eng.wait_ge(filled[b], e * PER_EXPERT[b] + (BEFORE[b] + k + 1))
            return bank[b]

        def landed_e(eng, e, name):
            b, k = EXPERT[name]
            eng.wait_ge(drained[b], e * PER_EXPERT[b] + (BEFORE[b] + k + 1))

        def full_e(name):
            return filled[EXPERT[name][0]]

        def free_e(name):
            return drained[EXPERT[name][0]]

        def arrived_d(eng, e, name):
            b, k = DENSE[name]
            eng.wait_ge(filled[b], e * PER_DENSE[b] + (AFTER[b] + k + 1))
            return bank[b]

        def landed_d(eng, e, name):
            b, k = DENSE[name]
            eng.wait_ge(drained[b], e * PER_DENSE[b] + (AFTER[b] + k + 1))

        def overflow(eng, l):
            eng.wait_ge(over_known, l + 1)
            eng.sem_inc(over_seen, 1)
            return eng.value_load(over_flag[0:1, 0:1], min_val=0, max_val=1)

        block = ctx.enter_context(nc.Block())

        N_CONST = 5

        @block.sync
        def _(sp):
            sp.dma_start(cst[:, :], consts).then_inc(consts_loaded, 16)
            sp.dma_start(x_tok[:, :, :], x.rearrange("(t p) d -> p t d", p=P)).then_inc(x_loaded, 16)
            sp.dma_start(prow[0:L * PR, :], param_rows).then_inc(consts_loaded, 16)
            sp.dma_start(rowb[:, :], row_params.partition_broadcast(P)).then_inc(consts_loaded, 16)
            sp.dma_start(rw[:, :, :], router_w.rearrange("(k p) e -> p k e", p=P)).then_inc(consts_loaded, 16)
            sp.dma_start(kr[64:96, 0, :].bitcast(I32), positions.partition_broadcast(32)).then_inc(consts_loaded, 16)
            for s in (0, 1, 3, 4, 5):
                sp.sem_inc(w_free[s], 1)
            with sp.Fori(0, L) as l:
                for j, (kind, c0, n) in enumerate(LOADS):
                    s, k = j % NSLOT, j // NSLOT
                    if kind == "in":
                        src = w_in[bass.ds(l, 1), :, c0:c0 + n].rearrange("l (k p) n -> p (l k) n", p=P)
                    elif kind == "uq":
                        src = w_uq[bass.ds(l, 1), :, :].rearrange("l (k p) n -> p (l k) n", p=P)
                    elif kind == "ukv":
                        src = w_ukv[bass.ds(l, 1), :, :].rearrange("l (k p) n -> p (l k) n", p=P)
                    elif kind == "branch":
                        src = w_branch[bass.ds(l, 1), c0, :, :].rearrange("l (k p) n -> p (l k) n", p=P)
                    else:
                        src = w_out[bass.ds(l, 1), :, c0:c0 + n].rearrange("l (k p) n -> p (l k) n", p=P)
                    rows = src.shape[1]
                    dst = W[:, s, 0:rows * n].rearrange("p (k n) -> p k n", n=n)
                    sp.wait_ge(w_free[s], l * USES + (k + 1))
                    sp.dma_start(dst, src).then_inc(w_loaded[s], 16)
                sp.wait_ge(gdn_mem_free, l + 1)
                sp.sem_inc(gdn_mem_seen, 1)
                with sp.Fori(0, PAIRS) as i:
                    for odd in range(2):
                        for m, (wt, n) in enumerate(((w_gate, F), (w_up, F), (w_down, D))):
                            s = m if odd else m + NSLOT
                            src = wt[bass.ds(l * E + i * 2 + odd, 1), :, :].rearrange("e (k p) n -> p (e k) n", p=P)
                            if odd:
                                sp.wait_ge(w_free[s], l * USES + i + (PRE // NSLOT + 1))
                            else:
                                sp.wait_ge(w_free[s], l * PAIRS + i + 1)
                            sp.dma_start(slot_mem(s, src.shape[1], n), src).then_inc(w_loaded[s], 16)
                with sp.If(overflow(sp, l)):
                    with sp.Fori(0, E) as e:
                        for s, (wt, n) in enumerate(((w_gate, F), (w_up, F), (w_down, D))):
                            src = wt[bass.ds(l * E + e, 1), :, :].rearrange("e (k p) n -> p (e k) n", p=P)
                            dst = W[:, s, 0:src.shape[1] * n].rearrange("p (k n) -> p k n", n=n)
                            sp.wait_ge(dense_free[s], e + 1)
                            sp.dma_start(dst, src).then_inc(dense_loaded[s], 16)
                    for s in range(2):
                        sp.wait_ge(dense_free[s], E + 1)
                    sp.sem_inc(ev["dense_done_sp"], 1)
            sp.wait_ge(layer_go, L)
            sp.dma_start(out.rearrange("(t p) d -> p t d", p=P), x_tok[:, :, :]).then_inc(stored, 16)
            sp.wait_ge(stored, 16)

        @block.tensor
        def _(pe):
            def group(o, pairs, release=None):
                for i, (a, b) in enumerate(pairs):
                    mm = pe.matmul(o, a, b, start=i == 0, stop=i == len(pairs) - 1)
                    if i == 0 and release is not None:
                        mm.then_inc(w_free[release], 1)
                return mm

            def turn(o, src, release=None):
                mm = pe.transpose(o, src, ident)
                if release is not None:
                    mm.then_inc(w_free[release], 1)
                return mm

            pe.wait_ge(consts_loaded, 16 * N_CONST)
            pe.transpose(bank[7][:, 0:L * PR], prow[0:L * PR, :], cst[0:L * PR, 0:L * PR]).then_inc(rows_turned, 1)
            pe.wait_ge(x_loaded, 16)
            pe.wait_ge(pcols_ready, 1)

            with pe.Fori(0, L) as l:
                def weights(j, n):
                    s = j % NSLOT
                    pe.wait_ge(w_loaded[s], l * (16 * USES) + 16 * (j // NSLOT + 1))
                    rows = {J_UQ: 2, J_UKV: 1}.get(j, 4 if J_BR <= j < J_OUT else DK)
                    return W[:, s, 0:rows * n].rearrange("p (k n) -> p k n", n=n)

                def turn_x(kind, first):
                    for i in range(4):
                        t, k0 = i // 2, 4 * (i % 2)
                        o = claim(pe, f"{kind}{i}")
                        for k in range(k0, k0 + 4):
                            mm = turn(o[:, (k - k0) * P:(k - k0 + 1) * P], x_tok[:, t, k * P:(k + 1) * P],
                                      first if i == 0 and k == 0 else None)
                        mm.then_inc(full(f"{kind}{i}"), 1)

                turn_x("xa", 2)
                for i in range(4):
                    landed(pe, f"xa{i}")

                def project(o, w, c, m, release=None):
                    return group(o, [(w[:, k, c:c + m], xT[:, k, :]) for k in range(DK)], release)

                def project_tok(o, w, c, n, t, release=None):
                    return group(o, [(xT[:, k, t * P:(t + 1) * P], w[:, k, c:c + n]) for k in range(DK)], release)

                w = weights(0, 416)
                o = claim(pe, "cq")
                project(o[:, 0:T], w, 0, P)
                project(o[:, T:2 * T], w, P, P).then_inc(full("cq"), 1)
                o = claim(pe, "ckv")
                project(o[:, 0:T], w, 2 * P, P)
                project(o[64:96, T:2 * T], w, 3 * P, ROPE).then_inc(full("ckv"), 1)
                for i in range(6):
                    j = 1 + i // 2
                    w = weights(j, 512)
                    o = claim(pe, f"gp{i}")
                    for c in range(2):
                        mm = project(o[:, c * T:(c + 1) * T], w, ((2 * i + c) % 4) * P, P,
                                     (j - 1) % NSLOT if i % 2 == 0 and c == 0 else None)
                    mm.then_inc(full(f"gp{i}"), 1)
                w = weights(4, 520)
                for i in range(2):
                    o = claim(pe, f"gz{i}")
                    for c in range(2):
                        mm = project(o[:, c * T:(c + 1) * T], w, (2 * i + c) * P, P, 3 % NSLOT if i == c == 0 else None)
                    mm.then_inc(full(f"gz{i}"), 1)
                o = claim(pe, "gab")
                for t in range(TT):
                    mm = project_tok(o[:, 8 * t:8 * t + 8], w, 512, 8, t)
                mm.then_inc(full("gab"), 1)
                for j, kind in ((5, "fq"), (6, "fk")):
                    w = weights(j, 512)
                    for i in range(2):
                        o = claim(pe, f"{kind}{i}")
                        for c in range(2):
                            mm = project(o[:, c * T:(c + 1) * T], w, (2 * i + c) * P, P,
                                         (j - 1) % NSLOT if i == c == 0 else None)
                        mm.then_inc(full(f"{kind}{i}"), 1)
                w = weights(7, 520)
                for t in range(TT):
                    o = claim(pe, f"fv{t}")
                    project_tok(o[:, :], w, 0, 512, t, 6 % NSLOT if t == 0 else None).then_inc(full(f"fv{t}"), 1)
                o = claim(pe, "ff")
                for t in range(TT):
                    mm = project_tok(o[:, 8 * t:8 * t + 8], w, 512, 8, t)
                mm.then_inc(full("ff"), 1)
                landed(pe, "cq")
                landed(pe, "ckv")
                o = claim(pe, "crms")
                group(o[:, 0:T], [(ones, c_sq[:, 0, :]), (ones, c_sq[:, 1, :])], 7 % NSLOT)
                group(o[:, T:2 * T], [(ones, c_sq[:, 2, :])]).then_inc(full("crms"), 1)
                w = weights(J_UQ, 768)
                pe.wait_ge(ev["cn_ready"], 3)
                for i in range(4):
                    o = claim(pe, f"mq{i}")
                    for c in range(2):
                        h = 2 * i + c
                        mm = group(o[0:QH, c * T:(c + 1) * T], [(w[:, k, h * QH:(h + 1) * QH], c_n[:, k, :]) for k in range(2)])
                    mm.then_inc(full(f"mq{i}"), 1)
                for i in range(4):
                    landed(pe, f"mq{i}")
                    o = claim(pe, f"mr{i}")
                    pe.matmul(o[0:QH, :], cst[0:QH, C_ROT:C_ROT + QH],
                              mq[0:QH, 2 * i:2 * i + 2, :].rearrange("p a b -> p (a b)"),
                              start=True, stop=True).then_inc(full(f"mr{i}"), 1)
                o = claim(pe, "mkr")
                pe.matmul(o[64:96, 0:T], cst[64:96, C_ROT + 64:C_ROT + 96], kr[64:96, 0, :],
                          start=True, stop=True).then_inc(full("mkr"), 1)
                w = weights(J_UKV, 1024)
                for i in range(4):
                    o = claim(pe, f"mk{i}")
                    for c in range(2):
                        h = 2 * i + c
                        mm = group(o[0:NOPE, c * T:(c + 1) * T], [(w[:, 0, h * P:h * P + NOPE], c_n[:, 2, :])],
                                   J_UQ % NSLOT if h == 0 else None)
                    mm.then_inc(full(f"mk{i}"), 1)
                wv = w[:, 0, :].rearrange("p (h c) -> p h c", c=P)[:, :, NOPE:P]
                for t in range(TT):
                    o = claim(pe, f"mv{t}")
                    pe.matmul(o[:, :].rearrange("p (h c) -> p h c", c=HV), c_n[:, 2, t * P:(t + 1) * P], wv,
                              start=True, stop=True).then_inc(full(f"mv{t}"), 1)
                pe.wait_ge(ev["small_ready"], 1)
                o = claim(pe, "fF")
                lf = small[:, 5, :, :]
                pe.matmul(o[64:80, 0:P], lf[:, 0, :], tri, start=True, stop=True).then_inc(w_free[J_UKV % NSLOT], 1)
                group(o[64:80, P:T], [(lf[:, 0, :], ones), (lf[:, 1, :], tri)]).then_inc(full("fF"), 1)

                def step_pe(name):
                    o = claim(pe, name)
                    if name.startswith("gate"):
                        c = int(name[4:])
                        j = J_GATE + c // 4
                        w = weights(j, 512)
                        mm = project(o[:, 0:T], w, (c % 4) * P, P,
                                     (j - 1) % NSLOT if c % 4 == 0 and c > 0 else None)
                    elif name[0] == "S" and name[1:].isdigit():
                        a = int(name[1:])
                        h = a % H
                        if a < H:
                            pe.wait_ge(ev["mq_ready"], h // 2 + 1)
                            landed(pe, f"mk{h // 2}")
                            if a == 0:
                                pe.wait_ge(ev["kr_ready"], 1)
                            q, k = mq[0:QH, h, :], mk[0:QH, h, :]
                        else:
                            if a == H:
                                for i in range(2):
                                    landed(pe, f"fq{i}")
                                    landed(pe, f"fk{i}")
                                pe.wait_ge(ev["fext_ready"], 2)
                            q, k = fq[0:FXH, h, :], fk[0:FXH, h, :]
                        pe.matmul(o[:, 0:P], q[:, 0:P], k[:, 0:P], start=True, stop=True)
                        mm = pe.matmul(o[:, P:P + T], q[:, P:T], k[:, 0:T], start=True, stop=True)
                    elif name.startswith("PT"):
                        a = int(name[2:])
                        pe.wait_ge(ev["p_ready"], a + 1)
                        for i in range(3):
                            mm = turn(o[:, i * P:(i + 1) * P], sm[:, a % 4, i * P:(i + 1) * P])
                    elif name[0] == "O":
                        a = int(name[1:])
                        h = a % H
                        landed(pe, f"PT{a}")
                        if a % H == 0:
                            for t in range(TT):
                                landed(pe, f"mv{t}" if a < H else f"fv{t}")
                        v = (mv if a < H else fv)[:, :, h * HV:(h + 1) * HV]
                        r = 64 * (h % 2)
                        p = pt[:, a % 2, :]
                        pe.matmul(o[r:r + 64, 0:T], v[:, 0, :], p[:, 0:T], start=True, stop=False)
                        mm = pe.matmul(o[r:r + 64, P:T], v[:, 1, :], p[:, T:T + P], start=False, stop=True)
                    elif name.startswith("gn"):
                        i = int(name[2:])
                        pe.wait_ge(ev["gsq_ready"], i // 2 + 1)
                        mm = pe.matmul(o[:, :], ones, gsq[:, 2 * i:2 * i + 2, :].rearrange("p a b -> p (a b)"),
                                       start=True, stop=True)
                    elif name == "gcc":
                        g = small[:, 4, :, 0:4]
                        pe.wait_ge(ev["small_ready"], 1)
                        for t in range(TT):
                            pe.matmul(o[:, 8 * t:8 * t + 4], tri_bd, g[:, t, :], start=True, stop=True)
                            mm = pe.matmul(o[:, 8 * t + 4:8 * t + 8], ones_bd, g[:, t, :], start=True, stop=True)
                    elif name.startswith("gcb") or name.startswith("gbt"):
                        t = int(name[3:])
                        src, by = (gB, tri_bd) if name.startswith("gcb") else (bB, ident)
                        pe.wait_ge(ev["gb_ready" if name.startswith("gcb") else "bb_ready"], 1)
                        for h in range(GH):
                            mm = pe.matmul(o[:, h * P:(h + 1) * P], src[:, 4 * t + h, :], by, start=True, stop=True)
                    elif name[:2] in ("kk", "kq"):
                        t = int(name[2:])
                        if name == "kk0":
                            pe.wait_ge(ev["qk_ready"], 4)
                        for h in range(GH):
                            k = cv[:, 4 + h, t * P:(t + 1) * P]
                            mm = pe.matmul(o[:, h * P:(h + 1) * P], k,
                                           k if name[:2] == "kk" else cv[:, h, t * P:(t + 1) * P], start=True, stop=True)
                    elif name[:2] in ("tk", "tv"):
                        t = int(name[2:])
                        base = 4 if name[:2] == "tk" else 8
                        for h in range(GH):
                            mm = turn(o[:, h * P:(h + 1) * P], cv[:, base + h, t * P:(t + 1) * P])
                    elif name.startswith("tx"):
                        t = int(name[2:])
                        pe.wait_ge(ev["y_first"], 1)
                        for h in range(GH):
                            mm = turn(o[:, h * P:(h + 1) * P], Y[:, 4 * t + h, :])
                    elif name.startswith("t1_"):
                        _, s, t = name.split("_")
                        n, t = LEVELS.index(int(s)), int(t)
                        pe.wait_ge(ev["ct_ready"], n)
                        landed(pe, f"tx{t}" if n == 1 else f"xd_{LEVELS[n - 1]}_{t}")
                        for h in range(GH):
                            mm = pe.matmul(o[:, h * P:(h + 1) * P], CT[:, 4 * t + h, :], X[:, 4 * t + h, :], start=True, stop=True)
                    elif name[:3] in ("xd_", "yd_"):
                        _, s, t = name.split("_")
                        n, t = LEVELS.index(int(s)), int(t)
                        landed(pe, f"t1_{s}_{t}")
                        if n > 1:
                            landed(pe, f"yd_{LEVELS[n - 1]}_{t}")
                        for h in range(GH):
                            p = 4 * t + h
                            a, b = (Y, T1) if name[0] == "x" else (T1, Y)
                            mm = pe.matmul(o[:, h * P:(h + 1) * P], a[:, p, :], b[:, p, :], start=True, stop=True)
                    elif name.startswith("wt"):
                        t = int(name[2:])
                        landed(pe, f"yd_{LEVELS[-1]}_{t}")
                        landed(pe, "tk1")
                        landed(pe, "tk0")
                        for h in range(GH):
                            p = 4 * t + h
                            mm = pe.matmul(o[:, h * P:(h + 1) * P], RK[:, p, :], Y[:, p, :], start=True, stop=True)
                    elif name.startswith("vn"):
                        n = int(name[2:])
                        t, r = n // 2, 64 * (n % 2)
                        if n == 0:
                            landed(pe, "tv0")
                            landed(pe, "tv1")
                        else:
                            landed(pe, f"wt{t}")
                            landed(pe, f"su{n - 1}")
                        for h in range(GH):
                            p = 4 * t + h
                            dst = o[r:r + 64, h * P:(h + 1) * P]
                            mm = pe.matmul(dst, Y[:, p, r:r + 64], RV[:, p, :], start=True, stop=n == 0)
                            if n:
                                mm = pe.matmul(dst, WT[:, p, r:r + 64], state[:, h, :], start=False, stop=True)
                    elif name.startswith("ot"):
                        n = int(name[2:])
                        t, r = n // 2, 64 * (n % 2)
                        landed(pe, f"vn{n}")
                        if n == 0:
                            landed(pe, "kq0")
                            landed(pe, "kq1")
                            pe.wait_ge(ev["qd_ready"], 1)
                        for h in range(GH):
                            p = 4 * t + h
                            dst = o[:, h * 64:(h + 1) * 64]
                            if n:
                                pe.matmul(dst, state[:, h, :], cv[:, h, t * P + r:t * P + r + 64], start=True, stop=False)
                            mm = pe.matmul(dst, vn[r:r + 64, h * P:(h + 1) * P], AT[r:r + 64, p, r:r + 64],
                                           start=n == 0, stop=True)
                    elif name.startswith("su"):
                        n = int(name[2:])
                        t, r = n // 2, 64 * (n % 2)
                        for h in range(GH):
                            mm = pe.matmul(o[:, h * P:(h + 1) * P], KD[r:r + 64, 4 * t + h, :],
                                           vn[r:r + 64, h * P:(h + 1) * P], start=True, stop=True)
                    elif name.startswith("gr"):
                        i = int(name[2:])
                        pe.wait_ge(ev["osq_ready"], 1)
                        mm = pe.matmul(o[:, :], ones, EGC[:, 4 * i:4 * i + 4, :].rearrange("p a b -> p (a b)"),
                                       start=True, stop=True)
                    mm.then_inc(full(name), 1)

                for name in MIX:
                    step_pe(name)

                for n in range(NB):
                    j = J_BR + n
                    w = weights(j, 1024)
                    if n == 1:
                        pe.wait_ge(ev["og_ready"], 2)
                    else:
                        for a in range(H):
                            landed(pe, f"O{a + (H if n else 0)}")
                    for i in range(4):
                        o = claim(pe, f"br{n}_{i}")
                        for c in range(2):
                            m = 2 * i + c
                            mm = group(o[:, c * T:(c + 1) * T], [(w[:, k, m * P:(m + 1) * P], oT[:, n, k, :]) for k in range(4)],
                                       (j - 1) % NSLOT if m == 0 else None)
                        mm.then_inc(full(f"br{n}_{i}"), 1)
                pe.wait_ge(ev["merged_ready"], 4)
                for i in range(2):
                    w = weights(J_OUT + i, 512)
                    for t in range(TT):
                        o = claim(pe, f"wo{i}_{t}")
                        group(o[:, :], [(merged[:, k, t * P:(t + 1) * P], w[:, k, :]) for k in range(DK)],
                              (J_OUT + i - 1) % NSLOT if t == 0 else None).then_inc(full(f"wo{i}_{t}"), 1)
                pe.wait_ge(ev["x_normed"], 2)
                turn_x("xb", None)
                for i in range(4):
                    landed(pe, f"xb{i}")
                o = claim(pe, "rt")
                for t in range(TT):
                    mm = group(o[:, t * E:(t + 1) * E], [(xT[:, k, t * P:(t + 1) * P], rw[:, k, :]) for k in range(DK)])
                mm.then_inc(full("rt"), 1)

                pe.wait_ge(ev["route_mask"], 1)
                o = claim(pe, "rp")
                mask = rtt[:, 2, 0:2 * E]
                group(o[:, 0:E], [(tri, mask[:, 0:E])])
                group(o[:, E:2 * E], [(ones, mask[:, 0:E]), (tri, mask[:, E:2 * E])])
                group(o[:, 2 * E:3 * E], [(ones, mask[:, 0:E]), (ones, mask[:, E:2 * E])]).then_inc(full("rp"), 1)

                def gather(o):
                    for t in range(TT):
                        for half in range(2):
                            mm = pe.matmul(o[64 * half:64 * half + 64, :], G[:, t, :], x_tok[:, t, 512 * half:512 * half + 512],
                                           start=t == 0, stop=t == TT - 1)
                    return mm

                def turn_gathered(o):
                    for c in range(4):
                        mm = turn(o[:, c * P:(c + 1) * P], xg[:, c * P:(c + 1) * P])
                    return mm

                def scatter(release=(None, None)):
                    done = []
                    for t in range(TT):
                        for half in range(2):
                            r = 64 * half
                            mm = pe.matmul(bank[4 + 2 * t + half][:, :], hg[r:r + 64, T + t * P:T + (t + 1) * P],
                                           oe[r:r + 64, :], start=False, stop=True, skip_group_check=True)
                            if t == 0 and release[half] is not None:
                                mm.then_inc(w_free[release[half]], 1)
                            done.append(mm)
                    return done

                pe.wait_ge(ev["g_made"], 1)
                gather(claim(pe, "XG0")).then_inc(full("XG0"), 1)
                for i in range(4):
                    o = claim(pe, f"Y{i}")
                    pe.matmul(o[:, 0:64], cst[:, C_CAUS + P:C_CAUS + 2 * P], ident[:, 0:64], start=True, stop=False,
                              skip_group_check=True)
                landed(pe, "XG0")
                turn_gathered(claim(pe, "XT0")).then_inc(full("XT0"), 1)
                pe.wait_ge(ev["moe_zero"], 1)

                def expert(i, odd):
                    e = i * 2 + odd
                    s0 = 0 if odd else NSLOT

                    def claim_e(name):
                        b, k = EXPERT[name]
                        pe.wait_ge(drained[b], e * PER_EXPERT[b] + (BEFORE[b] + k))
                        return bank[b]

                    def weights_e(m, rows, n):
                        if odd:
                            pe.wait_ge(w_loaded[m], l * (16 * USES) + i * 16 + 16 * (PRE // NSLOT + 1))
                        else:
                            pe.wait_ge(w_loaded[s0 + m], l * (16 * PAIRS) + i * 16 + 16)
                        return slot_mem(s0 + m, rows, n)

                    wg = weights_e(0, DK, F)
                    wu = weights_e(1, DK, F)
                    o = claim_e("GU")
                    pe.wait_ge(drained[EXPERT["XT"][0]], e + BEFORE[EXPERT["XT"][0]])
                    for k in range(DK):
                        st = xgT[:, (k % 4) * P + 64 * (k // 4):(k % 4) * P + 64 * (k // 4) + 64]
                        mm = pe.matmul(o[0:64, :], st, wg[:, k, :], start=k == 0, stop=k == DK - 1)
                        if k == 0:
                            mm.then_inc(w_free[5 if odd else 2], 1)
                        mm = pe.matmul(o[64:128, :], st, wu[:, k, :], start=k == 0, stop=k == DK - 1)
                    mm.then_inc(full_e("GU"), 1)
                    pe.wait_ge(drained[0], e * 2 + BEFORE[0])
                    pe.wait_ge(drained[1], e + BEFORE[1])
                    scatter((s0, s0 + 1))
                    o = claim_e("XG")
                    pe.wait_ge(ev["g_made"], e + 2)
                    gather(o).then_inc(full_e("XG"), 1)
                    landed_e(pe, e, "GU")
                    pe.wait_ge(ev["gw_made"], e + 1)
                    o = claim_e("HG")
                    for t in range(TT):
                        turn(o[:, T + t * P:T + (t + 1) * P], Gw[:, t, :])
                    for k in range(4):
                        mm = pe.transpose(o[:, k * CAP:(k + 1) * CAP], hh[0:CAP, k * P:(k + 1) * P], cst[0:CAP, C_ID:C_ID + CAP])
                    mm.then_inc(full_e("HG"), 1)
                    o = claim_e("XT")
                    landed_e(pe, e, "XG")
                    turn_gathered(o).then_inc(full_e("XT"), 1)
                    o = claim_e("DN")
                    landed_e(pe, e, "HG")
                    w = weights_e(2, 4, D)
                    for k in range(4):
                        for half in range(2):
                            mm = pe.matmul(o[64 * half:64 * half + 64, :], hg[:, k * CAP:(k + 1) * CAP],
                                           w[:, k, 512 * half:512 * half + 512], start=k == 0, stop=k == 3)
                    mm.then_inc(full_e("DN"), 1)
                with pe.Fori(0, PAIRS) as i:
                    expert(i, 0)
                    expert(i, 1)
                landed_e(pe, E - 1, "DN")
                landed_e(pe, E - 1, "HG")
                for i, mm in enumerate(scatter()):
                    mm.then_inc(full(f"Y{i}"), 1)

                with pe.If(overflow(pe, l)):
                    pe.drain().then_inc(dense_free[0], 1)
                    pe.sem_inc(dense_free[1], 1)
                    with pe.Fori(0, E) as e:
                        def claim_d(name):
                            b, k = DENSE[name]
                            pe.wait_ge(drained[b], e * PER_DENSE[b] + (AFTER[b] + k))
                            return bank[b]

                        def weights_d(s, rows, n):
                            pe.wait_ge(dense_loaded[s], e * 16 + 16)
                            return W[:, s, 0:rows * n].rearrange("p (k n) -> p k n", n=n)

                        for t in range(TT):
                            for s, kind in enumerate("GU"):
                                w = weights_d(s, DK, F)
                                o = claim_d(f"{kind}{t}")
                                release = 2 if (kind, t) == ("G", 0) else 0 if (kind, t) == ("U", 1) else None
                                for k in range(DK):
                                    mm = pe.matmul(o[:, :], xT[:, k, t * P:(t + 1) * P], w[:, k, :], start=k == 0, stop=k == DK - 1)
                                    if k == 0 and release is not None:
                                        mm.then_inc(dense_free[release], 1)
                                mm.then_inc(filled[DENSE[f"{kind}{t}"][0]], 1)
                        for t in range(TT):
                            o = claim_d(f"HT{t}")
                            landed_d(pe, e, f"U{t}")
                            for k in range(4):
                                mm = turn(o[:, k * P:(k + 1) * P], dense_h[:, t, k * P:(k + 1) * P])
                                if t == k == 0:
                                    mm.then_inc(dense_free[1], 1)
                            mm.then_inc(filled[DENSE[f"HT{t}"][0]], 1)
                            w = weights_d(2, 4, D)
                            landed_d(pe, e, f"HT{t}")
                            for i in range(2):
                                o = claim_d(f"D{t}_{i}")
                                group(o[:, :], [(hT[:, t, k, :], w[:, k, i * 512:(i + 1) * 512]) for k in range(4)])\
                                    .then_inc(filled[DENSE[f"D{t}_{i}"][0]], 1)
                    pe.wait_ge(ev["dense_done_sp"], 1)

                pe.drain().then_inc(layer_done, 1)
                pe.wait_ge(layer_go, l + 1)

        eps = misc(29)

        def halves(ap, n=2):
            return ap.rearrange("p (a b) -> p a b", a=n)

        @block.scalar
        def _(act):
            act.wait_ge(rope_in, 1)
            act.activation(rope_s[64:96, :], rtmp[64:96, 0, :], ACT.Sin).then_inc(rope_sin, 1)
            act.activation(rtmp[64:96, 1, :], rtmp[64:96, 0, :], ACT.Abs).then_inc(rope_chain, 1)
            act.wait_ge(rope_chain, 1)
            act.activation(rope_c[64:96, :], rtmp[64:96, 1, :], ACT.Sin, scale=-1.0, bias=misc(28, 64, 96)).then_inc(rope_sin, 1)

            with act.Fori(0, L) as l:
                count = [0]

                def link(ins):
                    count[0] += 1
                    ins.then_inc(act_chain, 1)
                    act.wait_ge(act_chain, count[0])

                def turned(kind, i):
                    t, k0 = i // 2, 4 * (i % 2)
                    o = arrived(act, f"{kind}{i}")
                    act.activation(xT[:, k0:k0 + 4, t * P:(t + 1) * P], halves(o[:, :], 4), ACT.Copy).then_inc(free(f"{kind}{i}"), 1)

                turned("xa", 0)
                turned("xa", 2)
                o = arrived(act, "cq")
                act.activation(c_raw[:, 0:2, :], halves(o[:, :]), ACT.Copy)
                act.activation(c_sq[:, 0:2, :], halves(o[:, :]), ACT.Square).then_inc(free("cq"), 1)
                o = arrived(act, "ckv")
                act.activation(c_raw[:, 2, :], o[:, 0:T], ACT.Copy)
                act.activation(kr[64:96, 0, :], o[64:96, T:2 * T], ACT.Copy)
                act.activation(c_sq[:, 2, :], o[:, 0:T], ACT.Square).then_inc(free("ckv"), 1)
                act.wait_ge(ev["pad_zero"], 1)
                for i in range(6):
                    o = arrived(act, f"gp{i}")
                    act.activation(pre[:, 2 * i:2 * i + 2, 3:3 + T], halves(o[:, :]), ACT.Copy).then_inc(free(f"gp{i}"), 1)
                for i in range(2):
                    o = arrived(act, f"gz{i}")
                    act.activation(zs[:, 2 * i:2 * i + 2, :], halves(o[:, :]), ACT.Silu).then_inc(free(f"gz{i}"), 1)
                for kind, dst, scale in (("fq", fq, FOX_SCALE), ("fk", fk, 1.0)):
                    for i in range(2):
                        o = arrived(act, f"{kind}{i}")
                        for r in range(2):
                            ins = act.activation(dst[0:64, 4 * i + r:4 * i + r + 3:2, :], halves(o[64 * r:64 * r + 64, :]),
                                                 ACT.Copy, scale=scale)
                        ins.then_inc(free(f"{kind}{i}"), 1)
                for t in range(TT):
                    o = arrived(act, f"fv{t}")
                    act.activation(fv[:, t, :], o[:, :], ACT.Copy).then_inc(free(f"fv{t}"), 1)
                for i in range(3):
                    act.wait_ge(ev["conv_ready"], i + 1)
                    act.activation(cv[:, 4 * i:4 * i + 4, :], cv[:, 4 * i:4 * i + 4, :], ACT.Silu).then_inc(ev["silu_ready"], 1)
                act.preload_act_table_set("natural_log_exp_and_others")
                o = arrived(act, "crms")
                act.activation(c_rstd[:, 0, :], o[:, 0:T], ACT.Ln, scale=1.0 / Q_RANK, bias=eps)
                act.activation(c_rstd[:, 1, :], o[:, T:2 * T], ACT.Ln, scale=1.0 / KV_RANK, bias=eps).then_inc(free("crms"), 1)
                landed(act, "crms")
                act.activation(c_rstd[:, 0:2, :], c_rstd[:, 0:2, :], ACT.Exp, scale=-0.5).then_inc(ev["crstd_ready"], 1)
                act.wait_ge(ev["rows_ready"], 1)
                act.activation(rl[:, 0:4], rl[:, 0:4], ACT.Exp).then_inc(ev["gexp_ready"], 1)
                act.wait_ge(ev["small_neg"], 1)
                link(act.activation(small[:, 2, :, :], small[:, 1, :, :], ACT.Exp))
                act.activation(small[:, 3, :, :], small[:, 2, :, :], ACT.Ln, bias=ones[:, 0:1]).then_inc(ev["small_ln"], 1)
                act.wait_ge(ev["small_ready"], 1)
                act.activation(small[:, 4, :, 4:8], small[:, 4, :, 4:8], ACT.Exp).then_inc(ev["beta_ready"], 1)
                for i in range(4):
                    o = arrived(act, f"mq{i}")
                    act.activation(mq[0:QH, 2 * i:2 * i + 2, :], halves(o[0:QH, :]), ACT.Copy).then_inc(free(f"mq{i}"), 1)
                for i in range(4):
                    o = arrived(act, f"mk{i}")
                    act.activation(mk[0:NOPE, 2 * i:2 * i + 2, :], halves(o[0:NOPE, :]), ACT.Copy).then_inc(free(f"mk{i}"), 1)
                for t in range(TT):
                    o = arrived(act, f"mv{t}")
                    act.activation(mv[:, t, :], o[:, :], ACT.Copy).then_inc(free(f"mv{t}"), 1)
                for i in range(2):
                    act.activation(gsq[:, 4 * i:4 * i + 4, :], cv[:, 4 * i:4 * i + 4, :], ACT.Square).then_inc(ev["gsq_ready"], 1)

                def exps(a):
                    landed(act, f"S{a}")
                    for i, (lo, hi) in enumerate(((0, P), (P, P + T))):
                        ins = act.activation(sm[:, a % 4, lo:hi], sm[:, a % 4, lo:hi], ACT.Exp, scale=-1.0,
                                             bias=att[:, 0, 2 * a + i:2 * a + i + 1], accum_out=att[:, 1, 2 * a + i:2 * a + i + 1])
                    ins.then_inc(ev["p_exp"], 1)

                def step_act(name):
                    if name.startswith("gate"):
                        c = int(name[4:])
                        if c == 16:
                            arrived(act, f"yd_{LEVELS[-1]}_1")
                            landed(act, f"xd_{LEVELS[-2]}_1")
                        o = arrived(act, name)
                        act.activation(gate_tile(c), o[:, 0:T], ACT.Copy).then_inc(free(name), 1)
                    elif name[0] == "S" and name[1:].isdigit():
                        if int(name[1:]) > 0:
                            exps(int(name[1:]) - 1)
                    elif name.startswith("PT"):
                        a = int(name[2:])
                        if a == 2 * H - PT_LAG:
                            exps(2 * H - 1)
                        o = arrived(act, name)
                        act.activation(pt[:, a % 2, :], o[:, 0:384], ACT.Copy).then_inc(free(name), 1)
                    elif name.startswith("gn"):
                        i = int(name[2:])
                        o = arrived(act, name)
                        act.activation(grstd[:, 2 * i:2 * i + 2, :], halves(o[:, :]), ACT.Ln, bias=eps).then_inc(free(name), 1)
                        landed(act, name)
                        if i < 2:
                            ins = act.activation(grstd[:, 2 * i:2 * i + 2, :], grstd[:, 2 * i:2 * i + 2, :], ACT.Exp,
                                                 scale=-0.5, bias=misc(30))
                        else:
                            ins = act.activation(grstd[:, 2 * i:2 * i + 2, :], grstd[:, 2 * i:2 * i + 2, :], ACT.Exp, scale=-0.5)
                        ins.then_inc(ev["grstd_ready"], 1)
                    elif name == "gcb0":
                        act.wait_ge(ev["tok_diff"], 1)
                        act.activation(tex[:, 1, :, :], gcc[:, :, 0:4], ACT.Exp)
                        act.activation(tex[:, 2, :, :], tex[:, 0, :, :], ACT.Exp).then_inc(ev["tok_exp"], 1)
                        row_exp(0)
                    elif name == "gcb1":
                        row_exp(1)
                        act.wait_ge(ev["decay_min"], 1)
                        act.activation(DEC[:, :, :], DEC[:, :, :], ACT.Exp).then_inc(ev["decay_exp"], 1)
                    elif name.startswith("tx") or name.startswith("t1_"):
                        t = int(name[-1])
                        o = arrived(act, name)
                        dst = (X if name.startswith("tx") else T1)[:, 4 * t:4 * t + 4, :]
                        act.activation(dst, halves(o[:, :], 4), ACT.Copy).then_inc(free(name), 1)
                    elif name.startswith("wt"):
                        t = int(name[2:])
                        o = arrived(act, name)
                        act.activation(WT[:, 4 * t:4 * t + 4, :], halves(o[:, :], 4), ACT.Copy, scale=-1.0).then_inc(free(name), 1)
                    elif name.startswith("vn"):
                        r = 64 * (int(name[2:]) % 2)
                        o = arrived(act, name)
                        act.activation(vn[r:r + 64, :], o[r:r + 64, :], ACT.Copy).then_inc(free(name), 1)
                    elif name.startswith("gr"):
                        i = int(name[2:])
                        if i == 0:
                            landed(act, "ot3")
                            landed(act, "su2")
                            act.activation(EGC[:, :, :].rearrange("p (a b) c -> p a (b c)", b=2), oT[:, 1, :, :],
                                           ACT.Square).then_inc(ev["osq_ready"], 1)
                        o = arrived(act, name)
                        act.activation(DEC[:, 4 * i:4 * i + 4, :], halves(o[:, :], 4), ACT.Ln, scale=1.0 / P,
                                       bias=eps).then_inc(free(name), 1)
                        landed(act, name)
                        act.activation(DEC[:, 4 * i:4 * i + 4, :], DEC[:, 4 * i:4 * i + 4, :], ACT.Exp,
                                       scale=-0.5).then_inc(ev["orstd_ready"], 1)

                def row_exp(t):
                    act.wait_ge(ev["decay_diff"], t + 1)
                    o = arrived(act, f"gcb{t}")
                    act.activation(EGC[:, 4 * t:4 * t + 4, :], halves(o[:, :], 4), ACT.Exp).then_inc(free(f"gcb{t}"), 1)

                for name in MIX:
                    step_act(name)

                arrived(act, f"S{2 * H - 1}")
                act.dma_start(lnp[:, :, :], ln_params[bass.ds(l * 2, 1), :, :].rearrange("l a d -> (l a) d")
                              .partition_broadcast(P)).then_inc(ev["lnp_loaded"], 16)
                for n in range(NB):
                    g = gate_lo[:, 8 * n:8 * n + 8, :] if n < 2 else gate_hi
                    landed(act, f"gate{8 * n + 7}")
                    for i in range(2):
                        act.activation(g[:, 4 * i:4 * i + 4, :], g[:, 4 * i:4 * i + 4, :], ACT.Sigmoid).then_inc(ev["gates_sig"], 1)
                act.preload_act_table_set("natural_log_exp_and_others")

                def norm_stats(which):
                    for t in range(TT):
                        if which == 0:
                            landed(act, f"wo1_{t}")
                        else:
                            act.wait_ge(ev["ln_in"], t + 1)
                        act.activation(zs[:, :, :].rearrange("p a b -> p (a b)"), res[:, t, :], ACT.Copy,
                                       accum_out=lnst[:, t:t + 1]).then_inc(ev["ln_sum"], 1)
                        act.wait_ge(ev["ln_negmean"], 2 * which + t + 1)
                        act.activation(zs[:, :, :].rearrange("p a b -> p (a b)"), res[:, t, :], ACT.Square,
                                       bias=lnst[:, 2 + t:3 + t], accum_out=lnst[:, 4 + t:5 + t]).then_inc(ev["ln_sq"], 1)
                        act.wait_ge(ev["ln_sq"], 2 * which + t + 1)
                        link(act.activation(lnst[:, 6 + t:7 + t], lnst[:, 4 + t:5 + t], ACT.Ln, scale=1.0 / D, bias=eps))
                        act.activation(lnst[:, 6 + t:7 + t], lnst[:, 6 + t:7 + t], ACT.Exp, scale=-0.5).then_inc(ev["ln_rstd"], 1)

                norm_stats(0)
                act.wait_ge(ev["x_normed"], 2)
                act.dma_start(lnp[:, :, :], ln_params[bass.ds(l * 2 + 1, 1), :, :].rearrange("l a d -> (l a) d")
                              .partition_broadcast(P)).then_inc(ev["lnp_loaded"], 16)
                turned("xb", 0)
                turned("xb", 2)
                o = arrived(act, "rt")
                act.activation(rtt[:, 0, 0:2 * E], o[:, 0:2 * E], ACT.Sigmoid).then_inc(free("rt"), 1)

                o = arrived(act, "XG0")
                act.activation(xg, o[:, :], ACT.Copy).then_inc(free("XG0"), 1)
                with act.Fori(0, E) as e:
                    o = arrived_e(act, e, "GU")
                    act.activation(hs[0:CAP, :], o[0:CAP, :], ACT.Silu).then_inc(ev["silu_gate"], 1)
                    o = arrived_e(act, e, "XG")
                    act.activation(xg, o[:, :], ACT.Copy).then_inc(free_e("XG"), 1)
                    o = arrived_e(act, e, "HG")
                    act.activation(hg, o[:, :], ACT.Copy).then_inc(free_e("HG"), 1)
                with act.If(overflow(act, l)):
                    with act.Fori(0, E) as e:
                        for t in range(TT):
                            o = arrived_d(act, e, f"G{t}")
                            b, k = DENSE[f"U{t}"]
                            act.wait_ge(drained[b], e * PER_DENSE[b] + (AFTER[b] + k))
                            act.activation(dense_s[:, t, :], o[:, :], ACT.Silu).then_inc(drained[DENSE[f"G{t}"][0]], 1)
                        for t in range(TT):
                            o = arrived_d(act, e, f"HT{t}")
                            act.activation(hT[:, t, :, :], halves(o[:, :], 4), ACT.Copy).then_inc(drained[DENSE[f"HT{t}"][0]], 1)
                act.preload_act_table_set("natural_log_exp_and_others")
                norm_stats(1)
                act.drain().then_inc(layer_done, 1)
                act.wait_ge(layer_go, l + 1)

        @block.vector
        def _(dve):
            dve.wait_ge(rows_turned, 1)
            dve.tensor_copy(pcols_all[:, :], bank[7][:, 0:L * PR]).then_inc(pcols_ready, 1)
            dve.wait_ge(consts_loaded, 16 * N_CONST)
            ang, turns, rest = rtmp[64:96, 0, :], rtmp[64:96, 1, :], rope_s[64:96, :]
            start = [0]

            def rope_link(ins):
                start[0] += 1
                ins.then_inc(dve_start, 1)
                dve.wait_ge(dve_start, start[0])

            rope_link(dve.tensor_copy(rest, kr[64:96, 0, :].bitcast(I32)))
            rope_link(dve.tensor_scalar(ang, rest, misc(0, 64, 96), None, ALU.mult))
            magic = 1.5 * 2.0 ** 23
            rope_link(dve.tensor_scalar(rest, ang, 1.0 / (2 * np.pi), magic, ALU.mult, ALU.add))
            rope_link(dve.tensor_scalar(turns, rest, magic, None, ALU.subtract))
            two_pi, parts = 2 * np.pi, []
            for bits in (7, 12):
                q = 2.0 ** (bits - 3)
                parts.append(np.floor(two_pi * q) / q if not parts else np.round((two_pi - sum(parts)) * 2.0 ** 20) / 2.0 ** 20)
            parts.append(two_pi - sum(parts))
            for part in parts:
                rope_link(dve.scalar_tensor_tensor(ang, turns, -float(part), ang, ALU.mult, ALU.add))
            dve.tensor_scalar(ang, ang, 3.1415925, -3.1415925, ALU.min, ALU.max).then_inc(rope_in, 1)
            dve.wait_ge(rope_sin, 2)
            dve.tensor_scalar(rope_s[64:96, :], rope_s[64:96, :], misc(1, 64, 96), None, ALU.mult).then_inc(rope_ready, 1)
            dve.wait_ge(rope_ready, 1)

            with dve.Fori(0, L) as l:
                count = [0]

                def link(ins):
                    count[0] += 1
                    ins.then_inc(dve_chain, 1)
                    dve.wait_ge(dve_chain, count[0])

                dve.tensor_copy(pc[:, :], pcols_all[:, bass.ds(l * PR, PR)])
                link(dve.tensor_copy(rl[:, :], rowb[:, bass.ds(l * 16, 16)]))
                dve.sem_inc(ev["rows_ready"], 1)

                def turned(kind, i):
                    t, k0 = i // 2, 4 * (i % 2)
                    o = arrived(dve, f"{kind}{i}")
                    dve.tensor_copy(xT[:, k0:k0 + 4, t * P:(t + 1) * P], halves(o[:, :], 4)).then_inc(free(f"{kind}{i}"), 1)

                turned("xa", 1)
                turned("xa", 3)

                def conv(i):
                    landed(dve, f"gp{2 * i}")
                    landed(dve, f"gp{2 * i + 1}")
                    for j in range(CONV):
                        for c in range(4 * i, 4 * i + 4):
                            tap = pc[:, R_CONV + 12 * j + c:R_CONV + 12 * j + c + 1]
                            if j == 0:
                                ins = dve.tensor_scalar(cv[:, c, :], pre[:, c, 0:T], tap, None, ALU.mult)
                            else:
                                ins = dve.scalar_tensor_tensor(cv[:, c, :], pre[:, c, j:j + T], tap, cv[:, c, :], ALU.mult, ALU.add)
                        if j < CONV - 1:
                            link(ins)
                    ins.then_inc(ev["conv_ready"], 1)

                for i in range(3):
                    conv(i)
                o = arrived(dve, "gab")[:, 0:16].rearrange("p (t c) -> p t c", t=TT)
                dve.scalar_tensor_tensor(small[:, 0, :, 0:4], o[:, :, 0:4], -1.0,
                                         rl[:, 4:8].unsqueeze(1).broadcast_to([P, TT, 4]), ALU.mult, ALU.subtract)
                dve.tensor_copy(small[:, 0, :, 4:8], o[:, :, 4:8]).then_inc(free("gab"), 1)
                o = arrived(dve, "ff")[:, 0:16].rearrange("p (t c) -> p t c", t=TT)
                dve.tensor_tensor(small[:, 0, :, 8:16], o, rl[:, 8:16].unsqueeze(1).broadcast_to([P, TT, 8]),
                                  ALU.add).then_inc(free("ff"), 1)
                landed(dve, "gab")
                landed(dve, "ff")
                dve.scalar_tensor_tensor(small[:, 1, :, :], small[:, 0, :, :], -1.0, small[:, 0, :, :],
                                         ALU.mult, ALU.min).then_inc(ev["small_neg"], 1)
                dve.wait_ge(ev["crstd_ready"], 1)
                landed(dve, "cq")
                landed(dve, "ckv")
                for i in range(3):
                    dve.scalar_tensor_tensor(c_n[:, i, :], c_raw[:, i, :], pc[:, i:i + 1], c_rstd[:, i // 2, :],
                                             ALU.mult, ALU.mult).then_inc(ev["cn_ready"], 1)
                dve.wait_ge(ev["small_ln"], 1)
                link(dve.scalar_tensor_tensor(small[:, 4, :, :], small[:, 0, :, :], 0.0, small[:, 3, :, :], ALU.min, ALU.subtract))
                dve.tensor_copy(small[:, 5, :, 0:8], small[:, 4, :, 8:16])
                dve.tensor_scalar(small[:, 5, :, 8:16], small[:, 4, :, 8:16], -1.0, None, ALU.mult)
                dve.wait_ge(ev["gexp_ready"], 1)
                dve.tensor_tensor(small[:, 4, :, 0:4], small[:, 4, :, 0:4], rl[:, 0:4].unsqueeze(1).broadcast_to([P, TT, 4]),
                                  ALU.mult).then_inc(ev["small_ready"], 1)
                dve.wait_ge(ev["small_ready"], 1)

                def spread(dst, cols, done):
                    dve.tensor_copy(dst.rearrange("p (t h) c -> p t h c", t=TT),
                                    small[:, 4, :, cols:cols + 4].unsqueeze(3).broadcast_to([P, TT, 4, P])).then_inc(ev[done], 1)

                spread(gB[:, :, :], 0, "gb_ready")
                def both(ap):
                    return ap[64:96, :].unsqueeze(1).broadcast_to([32, 2, T])

                for i in range(4):
                    o = arrived(dve, f"mr{i}")
                    q = mq[64:96, 2 * i:2 * i + 2, :]
                    dve.tensor_tensor(rtmp[64:96, :, :], halves(o[64:96, :]), both(rope_s), ALU.mult).then_inc(free(f"mr{i}"), 1)
                    link(dve.tensor_tensor(q, q, both(rope_c), ALU.mult))
                    dve.tensor_tensor(q, q, rtmp[64:96, :, :], ALU.add).then_inc(ev["mq_ready"], 1)
                    dve.wait_ge(ev["mq_ready"], i + 1)
                o = arrived(dve, "mkr")
                dve.tensor_tensor(rtmp[64:96, 0, :], o[64:96, 0:T], rope_s[64:96, :], ALU.mult).then_inc(free("mkr"), 1)
                link(dve.tensor_tensor(kr[64:96, 1, :], kr[64:96, 0, :], rope_c[64:96, :], ALU.mult))
                dve.tensor_tensor(kr[64:96, 1, :], kr[64:96, 1, :], rtmp[64:96, 0, :], ALU.add).then_inc(ev["kr_turned"], 1)
                o = arrived(dve, "fF")
                dve.tensor_scalar(fe[64:80, 0, :], o[64:80, 0:T], misc(2, 64, 80), misc(3, 64, 80), ALU.mult, ALU.add)
                dve.tensor_scalar(fe[64:80, 1, :], o[64:80, 0:T], misc(3, 64, 80), misc(2, 64, 80), ALU.mult, ALU.add)\
                   .then_inc(free("fF"), 1)

                def rows4(ap):
                    return ap.unsqueeze(2).broadcast_to([P, 4, P])

                def masks4(ap, n=8):
                    return ap.unsqueeze(1).broadcast_to([P, n, P])

                def probabilities(a):
                    dve.wait_ge(ev["p_exp"], a + 1)
                    link(dve.reciprocal(att[:, 2, 2 * a:2 * a + 2], att[:, 1, 2 * a:2 * a + 2]))
                    for i, (lo, hi) in enumerate(((0, P), (P, P + T))):
                        ins = dve.tensor_scalar(sm[:, a % 4, lo:hi], sm[:, a % 4, lo:hi],
                                                att[:, 2, 2 * a + i:2 * a + i + 1], None, ALU.mult)
                    ins.then_inc(ev["p_ready"], 1)

                def step_dve(name):
                    if name[0] == "S" and name[1:].isdigit():
                        a = int(name[1:])
                        if a >= 4:
                            arrived(dve, f"PT{a - 4}")
                        o = arrived(dve, name)
                        scale = MLA_SCALE if a < H else 1.0
                        for i, (lo, hi) in enumerate(((0, P), (P, P + T))):
                            ins = dve.tensor_tensor_reduce(sm[:, a % 4, lo:hi], o[:, lo:hi],
                                                           causal[:, 0:P] if i == 0 else causal[:, P:P + T],
                                                           -scale, 3e38, ALU.add, ALU.min, att[:, 0, 2 * a + i:2 * a + i + 1])
                        ins.then_inc(free(name), 1)
                        if a >= 2:
                            probabilities(a - 2)
                    elif name.startswith("PT"):
                        a = int(name[2:]) + PT_LAG + 1
                        if a - 2 in (2 * H - 2, 2 * H - 1):
                            probabilities(a - 2)
                    elif name[0] == "O":
                        a = int(name[1:])
                        h, r = a % H, 64 * (a % 2)
                        o = arrived(dve, name)
                        dve.tensor_copy(oT[r:r + 64, 0 if a < H else 2, h // 2, :], o[r:r + 64, 0:T]).then_inc(free(name), 1)
                    elif name.startswith("gn"):
                        i = int(name[2:])
                        dve.wait_ge(ev["grstd_ready"], i + 1)
                        q = cv[:, 2 * i:2 * i + 2, :]
                        dve.tensor_tensor(q, q, grstd[:, 2 * i:2 * i + 2, :], ALU.mult).then_inc(ev["qk_ready"], 1)
                        if i == 3:
                            dve.wait_ge(ev["qk_ready"], 4)
                            dve.wait_ge(ev["beta_ready"], 1)
                            spread(bB, 4, "bb_ready")
                    elif name == "gcc":
                        o = arrived(dve, name)
                        dve.tensor_copy(gcc[:, :, :], o[:, 0:16].rearrange("p (t c) -> p t c", t=TT)).then_inc(free(name), 1)
                        landed(dve, name)
                        dve.tensor_tensor(tex[:, 0, :, :], gcc[:, :, 4:8], gcc[:, :, 0:4], ALU.subtract).then_inc(ev["tok_diff"], 1)
                    elif name.startswith("gcb"):
                        t = int(name[3:])
                        o = arrived(dve, name)
                        dve.tensor_tensor(DEC[:, 4 * t:4 * t + 4, :], halves(o[:, :], 4), rows4(gcc[:, t, 0:4]),
                                          ALU.subtract).then_inc(ev["decay_diff"], 1)
                        if t == 1:
                            dve.wait_ge(ev["decay_diff"], 2)
                            dve.tensor_scalar(DEC[:, :, :], DEC[:, :, :], 0.0, None, ALU.min).then_inc(ev["decay_min"], 1)
                            dve.wait_ge(ev["tok_exp"], 1)
                            link(dve.tensor_tensor(tex[:, 3, :, :], tex[:, 1, :, :], small[:, 4, :, 4:8], ALU.mult))
                    elif name.startswith("gbt"):
                        t = int(name[3:])
                        dve.wait_ge(ev["decay_ready"], 1)
                        o = arrived(dve, name)
                        dve.tensor_tensor(LT[:, 4 * t:4 * t + 4, :], halves(o[:, :], 4), DEC[:, 4 * t:4 * t + 4, :],
                                          ALU.mult).then_inc(free(name), 1)
                    elif name.startswith("kk"):
                        t = int(name[2:])
                        landed(dve, f"gbt{t}")
                        o = arrived(dve, name)
                        dve.tensor_tensor(LT[:, 4 * t:4 * t + 4, :], halves(o[:, :], 4), LT[:, 4 * t:4 * t + 4, :],
                                          ALU.mult).then_inc(free(name), 1)
                        if t == 1:
                            landed(dve, "kk0")
                            landed(dve, "kk1")
                            link(dve.tensor_tensor(T1, LT, masks4(level(0)), ALU.mult))
                            dve.tensor_tensor(Y, masks4(ident), T1, ALU.subtract).then_inc(ev["y_first"], 1)
                    elif name.startswith("kq"):
                        t = int(name[2:])
                        o = arrived(dve, name)
                        dve.tensor_tensor(AT[:, 4 * t:4 * t + 4, :], halves(o[:, :], 4), DEC[:, 4 * t:4 * t + 4, :],
                                          ALU.mult).then_inc(free(name), 1)
                    elif name == "tk1" or name == "tv1":
                        arrived(dve, name)
                        for t in range(TT):
                            o = arrived(dve, f"{name[:2]}{t}")
                            if name == "tk1":
                                dve.tensor_tensor(RK[:, 4 * t:4 * t + 4, :], halves(o[:, :], 4), rows4(tex[:, 3, t, :]), ALU.mult)
                                ins = dve.tensor_tensor(KD[:, 4 * t:4 * t + 4, :], halves(o[:, :], 4), rows4(tex[:, 2, t, :]), ALU.mult)
                            else:
                                ins = dve.tensor_tensor(RV[:, 4 * t:4 * t + 4, :], halves(o[:, :], 4),
                                                        rows4(small[:, 4, t, 4:8]), ALU.mult)
                            ins.then_inc(free(f"{name[:2]}{t}"), 1)
                    elif name[:3] in ("xd_", "yd_"):
                        t = int(name[-1])
                        dst = (X if name[0] == "x" else Y)[:, 4 * t:4 * t + 4, :]
                        o = arrived(dve, name)
                        if name.startswith("xd_2_"):
                            landed(dve, f"tx{t}")
                        dve.tensor_tensor(dst, dst, halves(o[:, :], 4), ALU.subtract).then_inc(free(name), 1)
                    elif name.startswith("ot"):
                        n = int(name[2:])
                        o = arrived(dve, name)
                        dve.tensor_copy(oT[:, 1, :, n * GC:(n + 1) * GC], o[:, 0:GH * GC].rearrange("p (h c) -> p h c", c=GC))\
                           .then_inc(free(name), 1)
                        if 0 < n < 3:
                            t, r = n // 2, 64 * (n % 2)
                            last = EGC[:, 4 * t:4 * t + 4, r + 63]
                            link(dve.tensor_tensor(state[:, :, :], state[:, :, :], rows4(last), ALU.mult))
                    elif name.startswith("su"):
                        o = arrived(dve, name)
                        if name == "su0":
                            dve.tensor_copy(state[:, :, :], halves(o[:, :], 4)).then_inc(free(name), 1)
                        else:
                            dve.tensor_tensor(state[:, :, :], state[:, :, :], halves(o[:, :], 4), ALU.add).then_inc(free(name), 1)
                    elif name == "gr1":
                        og = oT[:, 1, :, :].rearrange("p h c -> p (h c)")
                        for i in range(2):
                            dve.wait_ge(ev["orstd_ready"], i + 1)
                            part = og[:, 512 * i:512 * i + 512]
                            link(dve.scalar_tensor_tensor(part, part, pc[:, R_ON:R_ON + 1],
                                                          DEC[:, 4 * i:4 * i + 4, :].rearrange("p a b -> p (a b)"), ALU.mult, ALU.mult))
                            dve.tensor_tensor(part, part, zs[:, 2 * i:2 * i + 2, :].rearrange("p a b -> p (a b)"), ALU.mult)\
                               .then_inc(ev["og_ready"], 1)

                for name in MIX:
                    step_dve(name)

                for n in range(NB):
                    for i in range(4):
                        dve.wait_ge(ev["gates_sig"], 2 * n + i // 2 + 1)
                        g = (gate_lo[:, 8 * n + 2 * i:8 * n + 2 * i + 2, :] if n < 2 else gate_hi[:, 2 * i:2 * i + 2, :])
                        o = arrived(dve, f"br{n}_{i}")
                        m = merged[:, 2 * i:2 * i + 2, :]
                        if n == 0:
                            dve.tensor_tensor(m, halves(o[:, :]), g, ALU.mult).then_inc(free(f"br{n}_{i}"), 1)
                        else:
                            dve.tensor_tensor(brtmp[:, i % 2, :], o[:, :], g.rearrange("p a b -> p (a b)"), ALU.mult)\
                               .then_inc(free(f"br{n}_{i}"), 1)
                            landed(dve, f"br{n}_{i}")
                            ins = dve.tensor_tensor(m, m, halves(brtmp[:, i % 2, :]), ALU.add)
                            if n == 1:
                                link(ins)
                            else:
                                ins.then_inc(ev["merged_ready"], 1)

                dve.wait_ge(ev["merged_ready"], 4)
                dve.sem_inc(gdn_mem_free, 1)

                def norm(which):
                    for t in range(TT):
                        dve.wait_ge(ev["ln_sum"], 2 * which + t + 1)
                        dve.tensor_scalar(lnst[:, 2 + t:3 + t], lnst[:, t:t + 1], -1.0 / D, None, ALU.mult).then_inc(ev["ln_negmean"], 1)
                        dve.wait_ge(ev["ln_rstd"], 2 * which + t + 1)
                        link(dve.tensor_scalar(res[:, t, :], res[:, t, :], lnst[:, 2 + t:3 + t], lnst[:, 6 + t:7 + t],
                                               ALU.add, ALU.mult))
                        dve.wait_ge(ev["lnp_loaded"], 16 * (which + 1))
                        link(dve.tensor_tensor(res[:, t, :], res[:, t, :], lnp[:, 0, :], ALU.mult))
                        dve.tensor_tensor(x_tok[:, t, :], res[:, t, :], lnp[:, 1, :], ALU.add).then_inc(ev["x_normed"], 1)

                for i in range(2):
                    for t in range(TT):
                        c = slice(512 * i, 512 * i + 512)
                        o = arrived(dve, f"wo{i}_{t}")
                        dve.scalar_tensor_tensor(res[:, t, c], x_tok[:, t, c], ALPHA, o[:, :], ALU.mult, ALU.add)\
                           .then_inc(free(f"wo{i}_{t}"), 1)
                norm(0)
                turned("xb", 1)
                turned("xb", 3)

                landed(dve, "rt")
                score = rtt[:, 0, 0:32]
                sel, flag, tmp = rtt[:, 1, 0:32], rtt[:, 2, 0:32], rtt[:, 3, 0:32]
                big, big2 = rtt[:, 4, :], rtt[:, 5, :]
                gsc, gfl, den = rtt[:, 6, 0:8], rtt[:, 6, 8:16], rtt[:, 6, 16:18]
                rb = rowb[:, L * 16:L * 16 + E].unsqueeze(1).broadcast_to([P, TT, E])
                link(dve.tensor_tensor(halves(sel), halves(score), rb, ALU.add))

                def best(values, n, limit, out_flag):
                    vj = values.rearrange("p (g e) -> p g e", e=4).unsqueeze(2).broadcast_to([P, n, 4, 4])
                    vi = values.rearrange("p (g e) -> p g e", e=4).unsqueeze(3).broadcast_to([P, n, 4, 4])
                    b1 = big[:, 0:16 * n].rearrange("p (g i j) -> p g i j", i=4, j=4)
                    b2 = big2[:, 0:16 * n].rearrange("p (g i j) -> p g i j", i=4, j=4)
                    dve.tensor_tensor(b1, vj, vi, ALU.is_gt)
                    link(dve.tensor_tensor(b2, vj, vi, ALU.is_equal))
                    b2r = big2[:, 0:16 * n].rearrange("p (g m) -> p g m", m=16)
                    link(dve.tensor_tensor(b2r, b2r, misc(12, n=16).unsqueeze(1).broadcast_to([P, n, 16]), ALU.mult))
                    link(dve.tensor_tensor(big[:, 0:16 * n], big[:, 0:16 * n], big2[:, 0:16 * n], ALU.add))
                    link(dve.tensor_reduce(tmp[:, 0:4 * n], big[:, 0:16 * n].rearrange("p (m j) -> p m j", j=4), AX.X, ALU.add))
                    link(dve.tensor_scalar(out_flag, tmp[:, 0:4 * n], limit - 0.5, None, ALU.is_lt))

                best(sel, 8, 2, flag)
                link(dve.tensor_tensor(tmp, sel, flag, ALU.mult))
                link(dve.tensor_reduce(gsc, tmp.rearrange("p (g e) -> p g e", e=4), AX.X, ALU.add))
                best(gsc, 2, 1, gfl)
                dve.tensor_tensor(flag.rearrange("p (g e) -> p g e", e=4), flag.rearrange("p (g e) -> p g e", e=4),
                                  gfl.unsqueeze(2).broadcast_to([P, 8, 4]), ALU.mult).then_inc(ev["route_mask"], 1)
                dve.wait_ge(ev["route_mask"], 1)
                dve.memset(slot[:, :, E:E + 1], -1.0)
                dve.memset(comb[:, :, E:E + 1], 0.0)
                link(dve.tensor_tensor(tmp, flag, score, ALU.mult))
                link(dve.tensor_reduce(den, halves(tmp), AX.X, ALU.add))
                link(dve.reciprocal(den, den))
                link(dve.tensor_tensor(comb[:, :, 0:E], halves(tmp), den.unsqueeze(2).broadcast_to([P, TT, E]), ALU.mult))
                o = arrived(dve, "rp")
                link(dve.tensor_tensor(tmp, o[:, 0:2 * E], flag, ALU.mult))
                dve.tensor_reduce(over[:, 0:1], o[:, 2 * E:3 * E], AX.X, ALU.max).then_inc(free("rp"), 1)
                link(dve.tensor_scalar(slot[:, :, 0:E], halves(tmp), -1.0, None, ALU.add))
                landed(dve, "rp")
                dve.tensor_scalar(over_flag[:, :], over[:, 0:1], CAP + 0.5, None, ALU.is_gt).then_inc(over_known, 1)
                link(dve.tensor_scalar(comb_over[:, :, :], slot[:, :, 0:E], CAP - 0.5, None, ALU.is_gt))
                link(dve.tensor_tensor(comb_over[:, :, :], comb_over[:, :, :], comb[:, :, 0:E], ALU.mult))

                def gather_matrix(e):
                    for t in range(TT):
                        ins = dve.tensor_scalar(G[:, t, :], cst[:, C_SLOT:C_SLOT + CAP], e_col(slot, t, e), None, ALU.is_equal)
                    ins.then_inc(ev["g_made"], 1)

                def e_col(tile, t, e):
                    return tile[:, t, e:e + 1] if isinstance(e, int) else tile[:, t, bass.ds(e, 1)]

                gather_matrix(0)
                dve.memset(oe, 0.0)
                dve.memset(hg, 0.0).then_inc(ev["moe_zero"], 1)
                o = arrived(dve, "XT0")
                dve.tensor_copy(xgT, o[:, :]).then_inc(free("XT0"), 1)

                with dve.Fori(0, E) as e:
                    arrived_e(dve, e, "GU")
                    gather_matrix(e + 1)
                    for t in range(TT):
                        ins = dve.tensor_scalar(Gw[:, t, :], cst[:, C_SLOT:C_SLOT + P], slot[:, t, bass.ds(e, 1)],
                                                comb[:, t, bass.ds(e, 1)], ALU.is_equal, ALU.mult)
                    ins.then_inc(ev["gw_made"], 1)
                    dve.wait_ge(ev["silu_gate"], e + 1)
                    dve.tensor_tensor(hh[0:CAP, :], bank[EXPERT["GU"][0]][64:128, :], hs[0:CAP, :], ALU.mult).then_inc(free_e("GU"), 1)
                    o = arrived_e(dve, e, "XT")
                    dve.tensor_copy(xgT, o[:, :]).then_inc(free_e("XT"), 1)
                    o = arrived_e(dve, e, "DN")
                    dve.tensor_copy(oe, o[:, :]).then_inc(free_e("DN"), 1)
                for t in range(TT):
                    for i in range(2):
                        o = arrived(dve, f"Y{2 * t + i}")
                        c = slice(512 * i, 512 * i + 512)
                        dve.scalar_tensor_tensor(res[:, t, c], x_tok[:, t, c], ALPHA, o[:, :], ALU.mult, ALU.add)\
                           .then_inc(free(f"Y{2 * t + i}"), 1)
                for i in range(4):
                    landed(dve, f"Y{i}")
                with dve.If(overflow(dve, l)):
                    with dve.Fori(0, E) as e:
                        for t in range(TT):
                            landed_d(dve, e, f"G{t}")
                            o = arrived_d(dve, e, f"U{t}")
                            dve.tensor_tensor(dense_h[:, t, :], o[:, :], dense_s[:, t, :], ALU.mult)\
                               .then_inc(drained[DENSE[f"U{t}"][0]], 1)
                        for t in range(TT):
                            for i in range(2):
                                o = arrived_d(dve, e, f"D{t}_{i}")
                                b, k = DENSE[f"D{t}_{i}"]
                                dve.wait_ge(drained[b], e * PER_DENSE[b] + (AFTER[b] + k - 1))
                                part = res[:, t, 512 * i:512 * i + 512]
                                dve.scalar_tensor_tensor(part, o[:, :], comb_over[:, t, bass.ds(e, 1)], part, ALU.mult, ALU.add)\
                                   .then_inc(drained[b], 1)
                    for b in (6, 7):
                        dve.wait_ge(drained[b], AFTER[b] + 2 * E)
                dve.sem_inc(ev["ln_in"], 2)
                norm(1)
                dve.drain().then_inc(layer_done, 1)
                dve.wait_ge(layer_go, l + 1)

        @block.gpsimd
        def _(pool):
            with pool.Fori(0, L) as l:
                pool.memset(pre[:, :, 0:3], 0.0).then_inc(ev["pad_zero"], 1)
                pool.wait_ge(ev["pad_zero"], 1)
                pool.wait_ge(ev["kr_turned"], 1)
                pool.tensor_copy(mk[64:96, :, :], kr[64:96, 1, :].unsqueeze(1).broadcast_to([32, H, T])).then_inc(ev["kr_ready"], 1)
                pool.wait_ge(ev["kr_ready"], 1)
                pool.wait_ge(ev["decay_exp"], 1)
                pool.tensor_tensor(DEC[:, :, :], DEC[:, :, :], tri_bd.unsqueeze(1).broadcast_to([P, 8, P]), ALU.mult)\
                    .then_inc(ev["decay_ready"], 1)
                pool.wait_ge(ev["decay_ready"], 1)
                landed(pool, "fF")
                pool.tensor_copy(fq[64:80, :, :], fe[64:80, 0, :].unsqueeze(1).broadcast_to([16, H, T])).then_inc(ev["fext_ready"], 1)
                pool.wait_ge(ev["fext_ready"], 1)
                pool.tensor_tensor(fk[64:80, :, :], fe[64:80, 1, :].unsqueeze(1).broadcast_to([16, H, T]),
                                   cst[64:80, C_MISC + 4:C_MISC + 12].unsqueeze(2).broadcast_to([16, H, T]), ALU.mult)\
                    .then_inc(ev["fext_ready"], 1)
                pool.wait_ge(ev["fext_ready"], 2)
                landed(pool, "kk0")
                landed(pool, "kk1")
                for n in range(1, len(LEVELS)):
                    if n > 1:
                        arrived(pool, f"t1_{LEVELS[n - 1]}_1")
                    pool.tensor_tensor(CT[:, :, :], LT, level(n).unsqueeze(1).broadcast_to([P, 8, P]), ALU.mult)\
                        .then_inc(ev["ct_ready"], 1)
                    if n == 1:
                        arrived(pool, "kq1")
                        landed(pool, "gcb0")
                        landed(pool, "gcb1")
                        for t in range(TT):
                            q = cv[:, 0:4, t * P:(t + 1) * P]
                            ins = pool.tensor_tensor(q, q, EGC[:, 4 * t:4 * t + 4, :], ALU.mult)
                        ins.then_inc(ev["qd_ready"], 1)
                pool.drain()
                pool.wait_ge(layer_done, l * 3 + 3)
                pool.sem_inc(layer_seen, 1)
                for s in filled + drained + list(ev.values()) + [act_chain, dve_chain] + dense_loaded + dense_free:
                    pool.sem_clear(s)
                pool.sem_inc(layer_go, 1)


def kernel(x, positions, w_in, mla_q_norm, mla_w_uq, mla_kv_norm, mla_w_ukv, gdn_conv, gdn_a_log, gdn_dt_bias,
           gdn_out_norm, fox_f_bias, w_branch, w_out, ln1_g, ln1_b, router_w, router_bias,
           exp_w_gate, exp_w_up, exp_w_down, ln2_g, ln2_b):
    import concourse.bacc as _bacc
    from concourse.bass_utils import run_bass_kernel_spmd as _run

    def arr(a):
        return np.ascontiguousarray(a)

    rows = []
    for l in range(L):
        rows += [arr(mla_q_norm[l]).reshape(2, P), arr(mla_kv_norm[l]).reshape(1, P), arr(gdn_out_norm[l]).reshape(1, P),
                 arr(gdn_conv[l]).reshape(CONV * 12, P)]
    row_params = np.concatenate([np.concatenate([arr(gdn_a_log[l]), arr(gdn_dt_bias[l]), arr(fox_f_bias[l])]) for l in range(L)]
                                + [arr(router_bias)])
    ln_params = np.concatenate([np.stack([arr(g[l]), arr(b[l])])[None] for l in range(L)
                                for g, b in ((ln1_g, ln1_b), (ln2_g, ln2_b))])
    arrays = {
        "x": arr(x).reshape(T, D), "positions": arr(positions).reshape(T), "w_in": arr(w_in), "w_uq": arr(mla_w_uq),
        "w_ukv": arr(mla_w_ukv), "w_branch": arr(w_branch), "w_out": arr(w_out),
        "w_gate": arr(exp_w_gate).reshape(L * E, D, F), "w_up": arr(exp_w_up).reshape(L * E, D, F),
        "w_down": arr(exp_w_down).reshape(L * E, F, D), "router_w": arr(router_w), "param_rows": np.concatenate(rows),
        "row_params": row_params, "ln_params": ln_params, "consts": constants(),
    }
    nc = _bacc.Bacc("TRN2", target_bir_lowering=False, num_devices=1, dynamic_dma_scratch_size=1024)
    args = {n: nc.dram_tensor(f"in_{n}", a.shape, mybir.dt.from_np(a.dtype), kind="ExternalInput").ap() for n, a in arrays.items()}
    o = nc.dram_tensor("out", (T, D), F32, kind="ExternalOutput").ap()
    build(nc, *args.values(), o)
    r = _run(nc, [{f"in_{n}": a for n, a in arrays.items()}], core_ids=[0])
    return np.asarray(r.results[0]["out"]).reshape(1, T, D)
```

```python
from contextlib import ExitStack

import concourse.bass as bass
import numpy as np
from concourse import mybir

F32 = mybir.dt.float32
F32R = mybir.dt.float32r
I32 = mybir.dt.int32
ALU = mybir.AluOpType
ACT = mybir.ActivationFunctionType
AX = mybir.AxisListType

P = 128
D, T, L = 1024, 256, 2
TT = T // P
DK = D // P
Q_RANK, KV_RANK, ROPE, NOPE, HV = 256, 128, 32, 64, 64
H = 8
QH = NOPE + ROPE
FXH = 64 + 16
GH, GC = 4, 64
CONV = 4
E, F = 16, 512
CAP = 64
NB = 3
BK = 512 // P
ALPHA = float((2 * L) ** 0.25)
EPS = 1e-6
MLA_SCALE, FOX_SCALE, GDN_SCALE = QH ** -0.5, 64 ** -0.5, 128 ** -0.5
NEG = -1e30

W_COLS = 520
LOADS = [("in", 0, 416), ("in", 416, 512), ("in", 928, 512), ("in", 1440, 512), ("in", 1952, 520),
         ("in", 2472, 512), ("in", 2984, 512), ("in", 3496, 520), ("uq", 0, 768), ("ukv", 0, 1024)]
LOADS += [("in", 4016 + 512 * i, 512) for i in range(6)]
LOADS += [("branch", n, 1024) for n in range(NB)]
LOADS += [("out", 512 * i, 512) for i in range(2)]
NSLOT = 3
PRE = len(LOADS)
assert PRE % NSLOT == 0
PAIRS = E // 2
USES = PRE // NSLOT + PAIRS
FREED = [USES, USES, USES + 1]
J_UQ, J_UKV, J_GATE, J_BR, J_OUT = 8, 9, 10, 16, 19
N_FRONT = 8

def w_cols(j):
    return LOADS[j][2]


def w_rows(j):
    return BK if J_BR <= j < J_OUT else DK


PIECES = []
for _j in list(range(N_FRONT)) + list(range(J_GATE, J_OUT)):
    _n = w_cols(_j)
    PIECES += [(_j, c, P) for c in range(0, _n - _n % P, P)]
    PIECES += [(_j, _n - _n % P, _n % P)] if _n % P else []
PIECE = {(j, c): i for i, (j, c, n) in enumerate(PIECES)}


def hi_place(i):
    j, c, n = PIECES[i]
    if j < N_FRONT and n == P:
        return {f"front{c // P}"}
    if j < J_BR:
        return {0, 1} if j >= N_FRONT and c // P % 2 == 0 else {2, 3}
    return {c // P % 4}


HI_BEFORE = {}
for _i in range(len(PIECES)):
    HI_BEFORE[_i] = max((k for k in range(_i) if hi_place(k) & hi_place(_i)), default=None)

C_ID, C_TRIBD, C_ONES, C_ONESBD, C_TRI, C_LVL = 0, 128, 256, 384, 512, 640
LEVELS = (1, 2, 4, 8, 16, 32)
C_CAUS = C_LVL + 128 * len(LEVELS)
C_ROT = C_CAUS + 384
C_SLOT = C_ROT + 128
C_MISC = C_SLOT + CAP
C_END = C_MISC + 32
PR = 2 + 1 + 1 + CONV * 12
R_QN, R_KVN, R_ON, R_CONV = 0, 2, 3, 4


def constants():
    c = np.zeros((P, C_END), np.float32)
    i, j = np.arange(P)[:, None], np.arange(P)[None, :]
    same = i // GC == j // GC
    c[:, C_ID:C_ID + P] = i == j
    c[:, C_TRIBD:C_TRIBD + P] = same & (i <= j)
    c[:, C_ONES:C_ONES + P] = 1
    c[:, C_ONESBD:C_ONESBD + P] = same
    c[:, C_TRI:C_TRI + P] = i <= j
    for n, s in enumerate(LEVELS):
        c[:, C_LVL + P * n:C_LVL + P * n + P] = (i // (2 * s) == j // (2 * s)) & (i % (2 * s) < s) & (j % (2 * s) >= s)
    causal = np.where(j <= i, 0.0, NEG)
    c[:, C_CAUS:C_CAUS + P] = causal
    c[:, C_CAUS + 2 * P:C_CAUS + 3 * P] = causal
    half = ROPE // 2
    a = np.arange(half)
    c[NOPE + half + a, C_ROT + NOPE + a] = 1
    c[NOPE + a, C_ROT + NOPE + half + a] = 1
    freq = np.float32(10000.0) ** (-a.astype(np.float32) / np.float32(half))
    c[NOPE:NOPE + half, C_MISC] = freq
    c[NOPE + half:NOPE + ROPE, C_MISC] = freq
    c[NOPE:NOPE + half, C_MISC + 1] = -1
    c[NOPE + half:NOPE + ROPE, C_MISC + 1] = 1
    c[64:72, C_MISC + 2] = 1
    c[72:80, C_MISC + 3] = 1
    for r in range(16):
        c[64 + r, C_MISC + 4 + r % 8] = 1
    ii, jj = np.arange(4)[:, None], np.arange(4)[None, :]
    c[:, C_MISC + 12:C_MISC + 28] = (jj < ii).reshape(1, 16)
    c[:, C_SLOT:C_SLOT + CAP] = np.arange(CAP)
    c[:, C_MISC + 28] = np.pi / 2
    c[:, C_MISC + 29] = EPS
    c[:, C_MISC + 30] = np.log(GDN_SCALE)
    return c


PT_LAG = 3


def interleaved():
    groups = [["gn0", "gn1", "gn2", "gn3"], ["gcc"], ["gcb0", "gcb1"], ["gbt0", "gbt1"], ["kk0", "kk1"],
              ["kq0", "kq1"], ["tk0", "tk1"], ["tv0", "tv1"], ["tx0", "tx1"]]
    for s in LEVELS[1:]:
        groups.append([f"t1_{s}_0", f"t1_{s}_1"])
        groups.append(([f"xd_{s}_0", f"xd_{s}_1"] if s < LEVELS[-1] else []) + [f"yd_{s}_0", f"yd_{s}_1"])
    groups.append(["wt0", "wt1"])
    for n in range(4):
        groups.append([f"vn{n}"])
        groups.append([f"ot{n}"] + ([f"su{n}"] if n < 3 else []))
    groups.append(["gr0", "gr1"])
    att = []
    for a in range(2 * H + PT_LAG + 1):
        step = []
        if a < 2 * H:
            step.append(f"S{a}")
        if 0 <= a - PT_LAG < 2 * H:
            step.append(f"PT{a - PT_LAG}")
        if 0 <= a - PT_LAG - 1 < 2 * H:
            step.append(f"O{a - PT_LAG - 1}")
        att.append(step)
    gates = [[f"gate{c}"] for c in range(24)]
    out = []
    n = max(len(groups), len(att), len(gates))
    late = []
    for i in range(n):
        for seq in (groups, att, gates):
            for step in seq[i * len(seq) // n:(i + 1) * len(seq) // n]:
                if seq is gates and int(step[0][4:]) >= 16 and f"yd_{LEVELS[-1]}_1" not in out:
                    late.append(step)
                else:
                    while late and seq is gates:
                        out += late.pop(0)
                    out += step
    assert not late
    out.remove("gate23")
    out.insert(out.index("gr0"), "gate23")
    return out


MIX = interleaved()
FRONT = [f"xa{i}" for i in range(4)] + ["cq", "ckv"] + [f"gp{i}" for i in range(6)] + ["gz0", "gz1", "abT"] + \
    ["fq0", "gab", "fq1", "fk0", "fk1", "crms", "fv0", "fv1", "fT"] + [f"mq{i}" for i in range(4)] + ["ff"] + \
    [f"mr{i}" for i in range(4)] + ["mkr"] + [f"mk{i}" for i in range(4)] + ["mv0", "mv1", "fF"]
BACK = [f"br{n}_{j}" for n in range(NB) for j in range(4)] + ["wo0_0", "wo1_0", "wo0_1", "xb0", "xb1", "wo1_1", "rt", "xb2", "xb3", "rp"]
NBANK = 8
FIXED = {"XG0": 0, "XG1": 1, "XT0": 0, "XT1": 1, "Y0": 4, "Y1": 5, "Y2": 6, "Y3": 7}
BANK_ORDER = FRONT + MIX + BACK
BANK, BEFORE = {}, [0] * NBANK
for _i, _name in enumerate(BANK_ORDER + list(FIXED)):
    _b = FIXED.get(_name, _i % NBANK)
    BANK[_name] = (_b, BEFORE[_b])
    BEFORE[_b] += 1
PAIR = {"GU0": (2, 0), "HG0": (3, 0), "DN0": (3, 1), "GU1": (2, 1), "XG0": (0, 0), "XG1": (1, 0), "HG1": (3, 2),
        "XT0": (0, 1), "XT1": (1, 1), "DN1": (3, 3)}
PER_PAIR = [2, 2, 2, 4]
AFTER = [BEFORE[b] + PAIRS * (PER_PAIR[b] if b < 4 else 0) for b in range(NBANK)]
DENSE = {"G0": (0, 0), "U0": (1, 0), "G1": (2, 0), "U1": (3, 0), "HT0": (4, 0), "HT1": (5, 0),
         "D0_0": (6, 0), "D0_1": (7, 0), "D1_0": (6, 1), "D1_1": (7, 1)}
PER_DENSE = [1, 1, 1, 1, 1, 1, 2, 2]

EVENTS = """oh_made o_mla_lo ol_made xh_ready hi_made lo_made hi_used rows_ready pad_zero conv_ready silu_ready crstd_ready cn_ready
small_neg small_ln gexp_ready small_ready beta_ready fext_ready mq_ready kr_turned kr_ready gsq_ready
grstd_ready qk_ready gb_ready bb_ready tok_diff tok_exp decay_diff decay_min decay_exp decay_ready qd_ready
y_first ct_ready osq_ready orstd_ready og_ready p_exp p_ready gates_sig merged_ready ln_var ln_rstd ln_scaled
ln_b_mult x_normed_a x_normed_b route_mask xt_hi_made xt_lo_made moe_zero g_made gw_made silu_gate
dense_done_sp lnp_loaded""".split()


def build(nc, x, positions, w_in, w_uq, w_ukv, w_branch, w_out, w_gate, w_up, w_down, router_w,
          param_rows, row_params, ln_params, consts, out):
    ctx = ExitStack()
    with ctx:
        def sb(name, shape, dt=F32):
            return ctx.enter_context(nc.sbuf_tensor(name, shape, dt))

        def sem(name):
            return ctx.enter_context(nc.semaphore(name))

        with nc.sbuf_tensor("W", [P, NSLOT, DK * W_COLS], F32) as W, nc.sbuf_tensor("xT", [P, DK, T], F32) as xT, \
                nc.sbuf_tensor("gate_lo", [P, 16, T], F32) as gate_lo:
            pass
        W_lo = sb("W_lo", [P, NSLOT, DK * W_COLS], F32R)
        xh = sb("xh", [P, DK, T], F32R)
        hi_front = sb("hi_front", [P, DK, 4 * P], F32R)
        cst = sb("cst", [P, C_END])
        x_tok = sb("x_tok", [P, TT, D])
        xl = sb("xl", [P, DK, T], F32R)
        w_hi = sb("w_hi", [P, 2, DK, P], F32R)
        o_mla = sb("o_mla", [P, 4, T])
        mq = sb("mq", [P, H, T])
        mk = sb("mk", [P, H, T])
        mv = sb("mv", [P, TT, 512])
        fq = sb("fq", [P, H, T])
        fk = sb("fk", [P, H, T])
        fv = sb("fv", [P, TT, 512])
        kr = sb("kr", [P, 2, T])
        rtmp = sb("rtmp", [P, 2, T])
        rope_c = sb("rope_c", [P, T])
        rope_s = sb("rope_s", [P, T])
        zs = sb("zs", [P, 4, T])
        gdn_mem = sb("gdn_mem", [P, 12 * (T + 4) + 12 * T + 7 * 1024])
        sm = sb("sm", [P, 4, 384])
        pt = sb("pt", [P, 2, 384])
        pcols_all = sb("pcols_all", [P, L * PR])
        pc = sb("pc", [P, PR])
        rowb = sb("rowb", [P, L * 16 + E])
        rl = sb("rl", [P, 16])
        rw = sb("rw", [P, DK, E])
        small = sb("small", [P, 6, TT, 16])
        gcc = sb("gcc", [P, TT, 8])
        tex = sb("tex", [P, 4, TT, 4])
        att = sb("att", [P, 3, 32])
        lnst = sb("lnst", [P, 8])
        over_flag = sb("over_flag", [P, 1], I32)

        carved = [0]

        def carve(a, b):
            lo = carved[0]
            carved[0] += a * b
            return gdn_mem[:, lo:lo + a * b].rearrange("p (a b) -> p a b", b=b)

        pre = carve(12, T + 4)
        cv = carve(12, T)
        gA, gR, DEC, EGC, CT = carve(16, P), carve(16, P), carve(8, P), carve(8, P), carve(8, P)

        def slot_mem(s, rows, n):
            flat = W[:, s, 0:rows * n] if s < NSLOT else gdn_mem[:, (s - NSLOT) * DK * F:(s - NSLOT) * DK * F + rows * n]
            return flat.rearrange("p (k n) -> p k n", n=n)

        c_raw = DEC[:, 0:6, :].rearrange("p (a b) c -> p a (b c)", b=2)
        c_sq = EGC[:, 0:6, :].rearrange("p (a b) c -> p a (b c)", b=2)
        c_n = gA[:, 0:6, :].rearrange("p (a b) c -> p a (b c)", b=2)
        c_rstd = CT[:, 0:4, :].rearrange("p (a b) c -> p a (b c)", b=2)
        gsq = gA[:, :, :].rearrange("p (a b) c -> p a (b c)", b=2)
        grstd = gR[:, :, :].rearrange("p (a b) c -> p a (b c)", b=2)
        LT, AT = gA[:, 0:8, :], gA[:, 8:16, :]
        RK, WT = gR[:, 0:8, :], gR[:, 8:16, :]
        gB, bB = CT, WT
        preflat = gdn_mem[:, 0:12 * (T + 4)]
        Y, X, T1 = [preflat[:, 1024 * i:1024 * i + 1024].rearrange("p (a b) -> p a b", b=P) for i in range(3)]
        gate_hi = preflat[:, 1024:3072].rearrange("p (a b) -> p a b", b=T)
        KD = cv[:, 4:8, :].rearrange("p a (b c) -> p (a b) c", c=P)
        RV = cv[:, 8:12, :].rearrange("p a (b c) -> p (a b) c", c=P)
        fe = rtmp
        prow = sm[:, 0, 0:P]
        bnst = zs[:, 0, 0:24].rearrange("p (t a b) -> p t a b", t=TT, a=2)
        abT, fT = sm[0:8, 0, 0:T], sm[0:8, 1, 0:T]
        vn = mq[:, 0:2, :].rearrange("p a b -> p (a b)")
        state = mq[:, 2:4, :].rearrange("p a (b c) -> p (a b) c", c=P)
        oT = [o_mla, mk[:, 4:8, :], mv[:, :, :].rearrange("p t (a c) -> p (t a) c", c=T)]
        merged = mq
        brtmp = mk[:, 0:4, :].rearrange("p (a b) c -> p a (b c)", b=2)
        res = fq[:, :, :].rearrange("p (t a) c -> p t (a c)", t=TT)
        lnp = fk[:, :, :].rearrange("p (t a) c -> p t (a c)", t=TT)
        gflat = gate_lo[:, :, :].rearrange("p a b -> p (a b)")
        xg = gflat[:, 0:D]
        xgT = gflat[:, D:2 * D].rearrange("p (k c) -> p k c", c=P)
        hs, hh = gflat[:, 2048:2560], gflat[:, 2560:3072]
        hT_pair = gflat[:, 3072:3328]
        scat = gflat[:, 3328:3584]
        hT_scat = gflat[:, 3072:3584]
        Gw = gflat[:, 3584:3840].rearrange("p (t c) -> p t c", t=TT)
        G = hi_front[:, 7, 256:512].rearrange("p (t c) -> p t c", t=TT)
        xt_hi = w_hi[:, :, :, :].rearrange("p t k n -> p t (k n)")
        xt_lo = xl[:, :, :].rearrange("p (t k) n -> p t (k n)", t=TT)
        oe = mq[:, 0:4, :].rearrange("p a b -> p (a b)")
        dense_s = gflat[:, 0:1024].rearrange("p (t c) -> p t c", t=TT)
        dense_h = gflat[:, 1024:2048].rearrange("p (t c) -> p t c", t=TT)
        hT = mv[:, :, :].rearrange("p t (a c) -> p t a c", c=P)
        smflat = sm[:, :, :].rearrange("p a b -> p (a b)")
        rtt = smflat[:, 0:1024].rearrange("p (a b) -> p a b", b=P)
        slot = smflat[:, 1024:1024 + TT * (E + 2)].rearrange("p (t e) -> p t e", t=TT)
        comb = smflat[:, 1088:1088 + TT * (E + 2)].rearrange("p (t e) -> p t e", t=TT)
        comb_over = smflat[:, 1152:1152 + TT * E].rearrange("p (t e) -> p t e", t=TT)
        over = smflat[:, 1216:1218]

        ident = cst[:, C_ID:C_ID + P]
        tri_bd = cst[:, C_TRIBD:C_TRIBD + P]
        ones = cst[:, C_ONES:C_ONES + P]
        ones_bd = cst[:, C_ONESBD:C_ONESBD + P]
        tri = cst[:, C_TRI:C_TRI + P]
        causal = cst[:, C_CAUS:C_CAUS + 384]

        def level(n):
            return cst[:, C_LVL + P * n:C_LVL + P * n + P]

        def misc(i, lo=0, hi=P, n=1):
            return cst[lo:hi, C_MISC + i:C_MISC + i + n]

        bank = [ctx.enter_context(nc.psum_tensor(f"bank{i}", [P, 512], F32)) for i in range(NBANK)]

        filled = [sem(f"filled{i}") for i in range(NBANK)]
        drained = [sem(f"drained{i}") for i in range(NBANK)]
        ev = {name: sem(name) for name in EVENTS}
        act_chain, dve_chain = sem("act_chain"), sem("dve_chain")
        dense_loaded = [sem(f"dense_loaded{i}") for i in range(NSLOT)]
        dense_free = [sem(f"dense_free{i}") for i in range(NSLOT)]
        of_a_layer = sorted(s.num for s in filled + drained + list(ev.values()) + [act_chain, dve_chain] + dense_loaded + dense_free)
        assert of_a_layer == list(range(of_a_layer[0], of_a_layer[0] + len(of_a_layer)))
        w_loaded = [sem(f"w_loaded{i}") for i in range(2 * NSLOT)]
        w_free = [sem(f"w_free{i}") for i in range(2 * NSLOT)]
        gdn_mem_free, gdn_mem_seen = sem("gdn_mem_free"), sem("gdn_mem_seen")
        first_loaded, consts_loaded, x_loaded = sem("first_loaded"), sem("consts_loaded"), sem("x_loaded")
        rows_turned, pcols_ready = sem("rows_turned"), sem("pcols_ready")
        rope_chain, rope_in, rope_sin, rope_ready = sem("rope_chain"), sem("rope_in"), sem("rope_sin"), sem("rope_ready")
        dve_start = sem("dve_start")
        load_seen, turn_seen = sem("load_seen"), sem("turn_seen")
        over_known, over_seen = sem("over_known"), sem("over_seen")
        layer_done, layer_seen, layer_go, stored = sem("layer_done"), sem("layer_seen"), sem("layer_go"), sem("stored")

        def hi_half(i):
            j, c, n = PIECES[i]
            place = hi_place(i)
            if j < N_FRONT and n == P:
                return hi_front[:, :, c:c + n]
            q = min(place)
            return w_hi[:, q // 2, 4 * (q % 2):4 * (q % 2) + w_rows(j), 0:n]

        def piece_of_w(i):
            j, c, n = PIECES[i]
            return slot_mem(j % NSLOT, w_rows(j), w_cols(j))[:, :, c:c + n]

        def lo_half(i, cols=None):
            j, c, n = PIECES[i]
            return W_lo[:, j % NSLOT, 0:w_rows(j) * w_cols(j)].rearrange("p (k n) -> p k n", k=w_rows(j))[:, :, c:c + (cols or n)]

        def branch_halves(n):
            return xh[:, BK * (n % 2):BK * (n % 2) + BK, :], xl[:, BK * (n % 2):BK * (n % 2) + BK, :]

        def view(name):
            return bank[BANK[name][0]]

        def claim(pe, name):
            b, k = BANK[name]
            if k:
                pe.wait_ge(drained[b], k)
            return bank[b]

        def full(name):
            return filled[BANK[name][0]]

        def free(name):
            return drained[BANK[name][0]]

        def arrived(eng, name):
            b, k = BANK[name]
            eng.wait_ge(filled[b], k + 1)
            return bank[b]

        def landed(eng, name):
            b, k = BANK[name]
            eng.wait_ge(drained[b], k + 1)

        def gate_tile(c):
            return gate_lo[:, c, :] if c < 16 else gate_hi[:, c - 16, :]

        def claim_p(pe, i, name):
            b, k = PAIR[name]
            pe.wait_ge(drained[b], i * PER_PAIR[b] + (BEFORE[b] + k))
            return bank[b]

        def arrived_p(eng, i, name):
            b, k = PAIR[name]
            eng.wait_ge(filled[b], i * PER_PAIR[b] + (BEFORE[b] + k + 1))
            return bank[b]

        def landed_p(eng, i, name):
            b, k = PAIR[name]
            eng.wait_ge(drained[b], i * PER_PAIR[b] + (BEFORE[b] + k + 1))

        def full_p(name):
            return filled[PAIR[name][0]]

        def free_p(name):
            return drained[PAIR[name][0]]

        def arrived_d(eng, e, name):
            b, k = DENSE[name]
            eng.wait_ge(filled[b], e * PER_DENSE[b] + (AFTER[b] + k + 1))
            return bank[b]

        def landed_d(eng, e, name):
            b, k = DENSE[name]
            eng.wait_ge(drained[b], e * PER_DENSE[b] + (AFTER[b] + k + 1))

        def overflow(eng, l):
            eng.wait_ge(over_known, l + 1)
            eng.sem_inc(over_seen, 1)
            return eng.value_load(over_flag[0:1, 0:1], min_val=0, max_val=1)

        block = ctx.enter_context(nc.Block())

        N_FIRST, N_CONST = 5, 2

        @block.sync
        def _(sp):
            sp.dma_start(cst[:, C_ID:C_ID + P], consts[:, C_ID:C_ID + P]).then_inc(first_loaded, 16)
            sp.dma_start(cst[:, C_MISC:C_END], consts[:, C_MISC:C_END]).then_inc(first_loaded, 16)
            sp.dma_start(kr[64:96, 0, :].bitcast(I32), positions.partition_broadcast(32)).then_inc(first_loaded, 16)
            sp.dma_start(prow[0:L * PR, :], param_rows).then_inc(first_loaded, 16)
            sp.dma_start(rowb[:, :], row_params.partition_broadcast(P)).then_inc(first_loaded, 16)
            sp.dma_start(x_tok[:, :, :], x.rearrange("(t p) d -> p t d", p=P)).then_inc(x_loaded, 16)
            sp.dma_start(cst[:, C_ID + P:C_MISC], consts[:, C_ID + P:C_MISC]).then_inc(consts_loaded, 16)
            sp.dma_start(rw[:, :, :], router_w.rearrange("(k p) e -> p k e", p=P)).then_inc(consts_loaded, 16)
            for s in (0, 1, 3, 4, 5):
                sp.sem_inc(w_free[s], 1)
            with sp.Fori(0, L) as l:
                for j, (kind, c0, n) in enumerate(LOADS):
                    s, k = j % NSLOT, j // NSLOT
                    if kind == "in":
                        src = w_in[bass.ds(l, 1), :, c0:c0 + n].rearrange("l (k p) n -> p (l k) n", p=P)
                    elif kind == "uq":
                        src = w_uq[bass.ds(l, 1), :, :].rearrange("l (k p) n -> p (l k) n", p=P)
                    elif kind == "ukv":
                        src = w_ukv[bass.ds(l, 1), :, :].rearrange("l (k p) n -> p (l k) n", p=P)
                    elif kind == "branch":
                        src = w_branch[bass.ds(l, 1), c0, :, :].rearrange("l (k p) n -> p (l k) n", p=P)
                    else:
                        src = w_out[bass.ds(l, 1), :, c0:c0 + n].rearrange("l (k p) n -> p (l k) n", p=P)
                    rows = src.shape[1]
                    dst = W[:, s, 0:rows * n].rearrange("p (k n) -> p k n", n=n)
                    sp.wait_ge(w_free[s], l * FREED[s] + (k + 1))
                    sp.dma_start(dst, src).then_inc(w_loaded[s], 16)
                sp.wait_ge(gdn_mem_free, l + 1)
                sp.sem_inc(gdn_mem_seen, 1)
                def load_pair(i, first):
                    for odd in range(2):
                        for m, (wt, n) in enumerate(((w_gate, F), (w_up, F), (w_down, D))):
                            s = m if odd else m + NSLOT
                            src = wt[bass.ds(l * E + i * 2 + odd, 1), :, :].rearrange("e (k p) n -> p (e k) n", p=P)
                            if odd:
                                extra = m == 2 and not first
                                sp.wait_ge(w_free[s], l * FREED[m] + i + (PRE // NSLOT + 1 + extra))
                            else:
                                sp.wait_ge(w_free[s], l * PAIRS + i + 1)
                            sp.dma_start(slot_mem(s, src.shape[1], n), src).then_inc(w_loaded[s], 16)

                load_pair(0, True)
                with sp.Fori(1, PAIRS) as i:
                    load_pair(i, False)
                with sp.If(overflow(sp, l)):
                    with sp.Fori(0, E) as e:
                        for s, (wt, n) in enumerate(((w_gate, F), (w_up, F), (w_down, D))):
                            src = wt[bass.ds(l * E + e, 1), :, :].rearrange("e (k p) n -> p (e k) n", p=P)
                            dst = W[:, s, 0:src.shape[1] * n].rearrange("p (k n) -> p k n", n=n)
                            sp.wait_ge(dense_free[s], e + 1)
                            sp.dma_start(dst, src).then_inc(dense_loaded[s], 16)
                    for s in range(2):
                        sp.wait_ge(dense_free[s], E + 1)
                    sp.sem_inc(ev["dense_done_sp"], 1)
            sp.wait_ge(layer_go, L)
            sp.dma_start(out.rearrange("(t p) d -> p t d", p=P), x_tok[:, :, :]).then_inc(stored, 16)
            sp.wait_ge(stored, 16)

        @block.tensor
        def _(pe):
            def group(o, pairs, release=None):
                for i, (a, b) in enumerate(pairs):
                    mm = pe.matmul(o, a, b, start=i == 0, stop=i == len(pairs) - 1)
                    if i == 0 and release is not None:
                        mm.then_inc(w_free[release], 1)
                return mm

            def turn(o, src, release=None):
                mm = pe.transpose(o, src, ident)
                if release is not None:
                    mm.then_inc(w_free[release], 1)
                return mm

            pe.wait_ge(first_loaded, 16 * N_FIRST)
            pe.transpose(bank[7][:, 0:L * PR], prow[0:L * PR, :], cst[0:L * PR, 0:L * PR]).then_inc(rows_turned, 1)
            pe.wait_ge(x_loaded, 16)
            pe.wait_ge(pcols_ready, 1)

            with pe.Fori(0, L) as l:
                def weights(j, n):
                    s = j % NSLOT
                    pe.wait_ge(w_loaded[s], l * (16 * USES) + 16 * (j // NSLOT + 1))
                    rows = {J_UQ: 2, J_UKV: 1}.get(j, 4 if J_BR <= j < J_OUT else DK)
                    return W[:, s, 0:rows * n].rearrange("p (k n) -> p k n", n=n)

                def turn_x(kind, first, only=None):
                    tiles = range(4) if only is None else (2 * only, 2 * only + 1)
                    for i in tiles:
                        t, k0 = i // 2, 4 * (i % 2)
                        o = claim(pe, f"{kind}{i}")
                        if kind == "xb":
                            pe.wait_ge(ev["x_normed_b" if i % 2 else "x_normed_a"], t + 1)
                        for k in range(k0, k0 + 4):
                            mm = turn(o[:, (k - k0) * P:(k - k0 + 1) * P], x_tok[:, t, k * P:(k + 1) * P],
                                      first if i == tiles[0] and k == 0 else None)
                        mm.then_inc(full(f"{kind}{i}"), 1)

                turn_x("xa", 2)
                pe.wait_ge(consts_loaded, 16 * N_CONST)
                pe.wait_ge(ev["xh_ready"], 4)

                def product(o, i, release=None):
                    j, c, _ = PIECES[i]
                    hi, lo = hi_half(i), lo_half(i)
                    a_hi, a_lo = branch_halves(j - J_BR) if j >= J_BR else (xh, xl)
                    pe.wait_ge(ev["hi_made"], i + 1)
                    for k in range(w_rows(j)):
                        mm = pe.matmul(o, hi[:, k, :], a_hi[:, k, :], start=k == 0, stop=False)
                        if k == 0 and release is not None:
                            mm.then_inc(w_free[release], 1)
                    if i == 0:
                        for b in range(4):
                            landed(pe, f"xa{b}")
                    elif j == J_BR and c == 0:
                        pe.wait_ge(ev["o_mla_lo"], 1)
                    elif j > J_BR and c == 0:
                        pe.wait_ge(ev["ol_made"], j - J_BR)
                    for k in range(w_rows(j)):
                        mm = pe.matmul(o, hi[:, k, :], a_lo[:, k, :], start=False, stop=False)
                    mm.then_inc(ev["hi_used"], 1)
                    pe.wait_ge(ev["lo_made"], i + 1)
                    for k in range(w_rows(j)):
                        mm = pe.matmul(o, lo[:, k, :], a_hi[:, k, :], start=False, stop=k == w_rows(j) - 1)
                    return mm

                def pair(name, i, release=None):
                    o = claim(pe, name)
                    product(o[:, 0:T], i, release)
                    product(o[:, T:2 * T], i + 1).then_inc(full(name), 1)

                pair("cq", 0)
                o = claim(pe, "ckv")
                product(o[:, 0:T], 2)
                product(o[0:ROPE, T:2 * T], 3).then_inc(full("ckv"), 1)
                for i in range(6):
                    j = 1 + i // 2
                    pair(f"gp{i}", PIECE[j, 2 * P * (i % 2)], (j - 1) % NSLOT if i % 2 == 0 else None)
                for i in range(2):
                    pair(f"gz{i}", PIECE[4, 2 * P * i], 3 % NSLOT if i == 0 else None)
                o = claim(pe, "abT")
                product(o[0:8, 0:T], PIECE[4, 512]).then_inc(full("abT"), 1)

                def turn_small(name, src, turned_from):
                    landed(pe, turned_from)
                    o = claim(pe, name)
                    for t in range(TT):
                        mm = pe.transpose(o[:, 8 * t:8 * t + 8], src[:, t * P:(t + 1) * P], cst[0:8, C_ID:C_ID + 8])
                    mm.then_inc(full(name), 1)

                pair("fq0", PIECE[5, 0], 4 % NSLOT)
                turn_small("gab", abT, "abT")
                pair("fq1", PIECE[5, 2 * P])
                for i in range(2):
                    pair(f"fk{i}", PIECE[6, 2 * P * i], 5 % NSLOT if i == 0 else None)
                landed(pe, "cq")
                landed(pe, "ckv")
                o = claim(pe, "crms")
                group(o[:, 0:T], [(ones, c_sq[:, 0, :]), (ones, c_sq[:, 1, :])], 6 % NSLOT)
                group(o[:, T:2 * T], [(ones, c_sq[:, 2, :])]).then_inc(full("crms"), 1)
                first = PIECE[7, 0]
                whi, wlo = hi_front, lo_half(first, 512)
                pe.wait_ge(ev["hi_made"], first + 4)
                for t in range(TT):
                    o = claim(pe, f"fv{t}")
                    tok = slice(t * P, (t + 1) * P)
                    for k in range(DK):
                        mm = pe.matmul(o[:, :], xh[:, k, tok], whi[:, k, :], start=k == 0, stop=False)
                        mm = pe.matmul(o[:, :], xl[:, k, tok], whi[:, k, :], start=False, stop=False)
                    if t == 1:
                        mm.then_inc(ev["hi_used"], 4)
                    pe.wait_ge(ev["lo_made"], first + 4)
                    for k in range(DK):
                        mm = pe.matmul(o[:, :], xh[:, k, tok], wlo[:, k, :], start=False, stop=k == DK - 1)
                    mm.then_inc(full(f"fv{t}"), 1)
                o = claim(pe, "fT")
                product(o[0:8, 0:T], PIECE[7, 512]).then_inc(full("fT"), 1)
                w = weights(J_UQ, 768)
                pe.wait_ge(ev["cn_ready"], 3)
                for i in range(4):
                    o = claim(pe, f"mq{i}")
                    for c in range(2):
                        h = 2 * i + c
                        mm = group(o[0:QH, c * T:(c + 1) * T], [(w[:, k, h * QH:(h + 1) * QH], c_n[:, k, :]) for k in range(2)],
                                   7 % NSLOT if h == 0 else None)
                    mm.then_inc(full(f"mq{i}"), 1)
                turn_small("ff", fT, "fT")
                for i in range(4):
                    landed(pe, f"mq{i}")
                    o = claim(pe, f"mr{i}")
                    pe.matmul(o[0:QH, :], cst[0:QH, C_ROT:C_ROT + QH],
                              mq[0:QH, 2 * i:2 * i + 2, :].rearrange("p a b -> p (a b)"),
                              start=True, stop=True).then_inc(full(f"mr{i}"), 1)
                o = claim(pe, "mkr")
                pe.matmul(o[64:96, 0:T], cst[64:96, C_ROT + 64:C_ROT + 96], kr[64:96, 0, :],
                          start=True, stop=True).then_inc(full("mkr"), 1)
                w = weights(J_UKV, 1024)
                for i in range(4):
                    o = claim(pe, f"mk{i}")
                    for c in range(2):
                        h = 2 * i + c
                        mm = group(o[0:NOPE, c * T:(c + 1) * T], [(w[:, 0, h * P:h * P + NOPE], c_n[:, 2, :])],
                                   J_UQ % NSLOT if h == 0 else None)
                    mm.then_inc(full(f"mk{i}"), 1)
                wv = w[:, 0, :].rearrange("p (h c) -> p h c", c=P)[:, :, NOPE:P]
                for t in range(TT):
                    o = claim(pe, f"mv{t}")
                    pe.matmul(o[:, :].rearrange("p (h c) -> p h c", c=HV), c_n[:, 2, t * P:(t + 1) * P], wv,
                              start=True, stop=True).then_inc(full(f"mv{t}"), 1)
                pe.wait_ge(ev["small_ready"], 1)
                o = claim(pe, "fF")
                lf = small[:, 5, :, :]
                pe.matmul(o[64:80, 0:P], lf[:, 0, :], tri, start=True, stop=True).then_inc(w_free[J_UKV % NSLOT], 1)
                group(o[64:80, P:T], [(lf[:, 0, :], ones), (lf[:, 1, :], tri)]).then_inc(full("fF"), 1)

                def step_pe(name):
                    o = claim(pe, name)
                    if name.startswith("gate"):
                        c = int(name[4:])
                        j = J_GATE + c // 4
                        mm = product(o[:, 0:T], PIECE[j, (c % 4) * P], (j - 1) % NSLOT if c % 4 == 0 and c > 0 else None)
                    elif name[0] == "S" and name[1:].isdigit():
                        a = int(name[1:])
                        h = a % H
                        if a < H:
                            pe.wait_ge(ev["mq_ready"], h // 2 + 1)
                            landed(pe, f"mk{h // 2}")
                            if a == 0:
                                pe.wait_ge(ev["kr_ready"], 1)
                            q, k = mq[0:QH, h, :], mk[0:QH, h, :]
                        else:
                            if a == H:
                                for i in range(2):
                                    landed(pe, f"fq{i}")
                                    landed(pe, f"fk{i}")
                                pe.wait_ge(ev["fext_ready"], 2)
                            q, k = fq[0:FXH, h, :], fk[0:FXH, h, :]
                        pe.matmul(o[:, 0:P], q[:, 0:P], k[:, 0:P], start=True, stop=True)
                        mm = pe.matmul(o[:, P:P + T], q[:, P:T], k[:, 0:T], start=True, stop=True)
                    elif name.startswith("PT"):
                        a = int(name[2:])
                        pe.wait_ge(ev["p_ready"], a + 1)
                        for i in range(3):
                            mm = turn(o[:, i * P:(i + 1) * P], sm[:, a % 4, i * P:(i + 1) * P])
                    elif name[0] == "O":
                        a = int(name[1:])
                        h = a % H
                        landed(pe, f"PT{a}")
                        if a % H == 0:
                            for t in range(TT):
                                landed(pe, f"mv{t}" if a < H else f"fv{t}")
                        v = (mv if a < H else fv)[:, :, h * HV:(h + 1) * HV]
                        r = 64 * (h % 2)
                        p = pt[:, a % 2, :]
                        pe.matmul(o[r:r + 64, 0:T], v[:, 0, :], p[:, 0:T], start=True, stop=False)
                        mm = pe.matmul(o[r:r + 64, P:T], v[:, 1, :], p[:, T:T + P], start=False, stop=True)
                    elif name.startswith("gn"):
                        i = int(name[2:])
                        pe.wait_ge(ev["gsq_ready"], i // 2 + 1)
                        mm = pe.matmul(o[:, :], ones, gsq[:, 2 * i:2 * i + 2, :].rearrange("p a b -> p (a b)"),
                                       start=True, stop=True)
                    elif name == "gcc":
                        g = small[:, 4, :, 0:4]
                        pe.wait_ge(ev["small_ready"], 1)
                        for t in range(TT):
                            pe.matmul(o[:, 8 * t:8 * t + 4], tri_bd, g[:, t, :], start=True, stop=True)
                            mm = pe.matmul(o[:, 8 * t + 4:8 * t + 8], ones_bd, g[:, t, :], start=True, stop=True)
                    elif name.startswith("gcb") or name.startswith("gbt"):
                        t = int(name[3:])
                        src, by = (gB, tri_bd) if name.startswith("gcb") else (bB, ident)
                        pe.wait_ge(ev["gb_ready" if name.startswith("gcb") else "bb_ready"], 1)
                        for h in range(GH):
                            mm = pe.matmul(o[:, h * P:(h + 1) * P], src[:, 4 * t + h, :], by, start=True, stop=True)
                    elif name[:2] in ("kk", "kq"):
                        t = int(name[2:])
                        if name == "kk0":
                            pe.wait_ge(ev["qk_ready"], 4)
                        for h in range(GH):
                            k = cv[:, 4 + h, t * P:(t + 1) * P]
                            mm = pe.matmul(o[:, h * P:(h + 1) * P], k,
                                           k if name[:2] == "kk" else cv[:, h, t * P:(t + 1) * P], start=True, stop=True)
                    elif name[:2] in ("tk", "tv"):
                        t = int(name[2:])
                        base = 4 if name[:2] == "tk" else 8
                        for h in range(GH):
                            mm = turn(o[:, h * P:(h + 1) * P], cv[:, base + h, t * P:(t + 1) * P])
                    elif name.startswith("tx"):
                        t = int(name[2:])
                        pe.wait_ge(ev["y_first"], 1)
                        for h in range(GH):
                            mm = turn(o[:, h * P:(h + 1) * P], Y[:, 4 * t + h, :])
                    elif name.startswith("t1_"):
                        _, s, t = name.split("_")
                        n, t = LEVELS.index(int(s)), int(t)
                        pe.wait_ge(ev["ct_ready"], n)
                        landed(pe, f"tx{t}" if n == 1 else f"xd_{LEVELS[n - 1]}_{t}")
                        for h in range(GH):
                            mm = pe.matmul(o[:, h * P:(h + 1) * P], CT[:, 4 * t + h, :], X[:, 4 * t + h, :], start=True, stop=True)
                    elif name[:3] in ("xd_", "yd_"):
                        _, s, t = name.split("_")
                        n, t = LEVELS.index(int(s)), int(t)
                        landed(pe, f"t1_{s}_{t}")
                        if n > 1:
                            landed(pe, f"yd_{LEVELS[n - 1]}_{t}")
                        for h in range(GH):
                            p = 4 * t + h
                            a, b = (Y, T1) if name[0] == "x" else (T1, Y)
                            mm = pe.matmul(o[:, h * P:(h + 1) * P], a[:, p, :], b[:, p, :], start=True, stop=True)
                    elif name.startswith("wt"):
                        t = int(name[2:])
                        landed(pe, f"yd_{LEVELS[-1]}_{t}")
                        landed(pe, "tk1")
                        landed(pe, "tk0")
                        for h in range(GH):
                            p = 4 * t + h
                            mm = pe.matmul(o[:, h * P:(h + 1) * P], RK[:, p, :], Y[:, p, :], start=True, stop=True)
                    elif name.startswith("vn"):
                        n = int(name[2:])
                        t, r = n // 2, 64 * (n % 2)
                        if n == 0:
                            landed(pe, "tv0")
                            landed(pe, "tv1")
                        else:
                            landed(pe, f"wt{t}")
                            landed(pe, f"su{n - 1}")
                        for h in range(GH):
                            p = 4 * t + h
                            dst = o[r:r + 64, h * P:(h + 1) * P]
                            mm = pe.matmul(dst, Y[:, p, r:r + 64], RV[:, p, :], start=True, stop=n == 0)
                            if n:
                                mm = pe.matmul(dst, WT[:, p, r:r + 64], state[:, h, :], start=False, stop=True)
                    elif name.startswith("ot"):
                        n = int(name[2:])
                        t, r = n // 2, 64 * (n % 2)
                        landed(pe, f"vn{n}")
                        if n == 0:
                            landed(pe, "kq0")
                            landed(pe, "kq1")
                            pe.wait_ge(ev["qd_ready"], 1)
                        for h in range(GH):
                            p = 4 * t + h
                            dst = o[:, h * 64:(h + 1) * 64]
                            if n:
                                pe.matmul(dst, state[:, h, :], cv[:, h, t * P + r:t * P + r + 64], start=True, stop=False)
                            mm = pe.matmul(dst, vn[r:r + 64, h * P:(h + 1) * P], AT[r:r + 64, p, r:r + 64],
                                           start=n == 0, stop=True)
                    elif name.startswith("su"):
                        n = int(name[2:])
                        t, r = n // 2, 64 * (n % 2)
                        for h in range(GH):
                            mm = pe.matmul(o[:, h * P:(h + 1) * P], KD[r:r + 64, 4 * t + h, :],
                                           vn[r:r + 64, h * P:(h + 1) * P], start=True, stop=True)
                    elif name.startswith("gr"):
                        i = int(name[2:])
                        pe.wait_ge(ev["osq_ready"], 1)
                        mm = pe.matmul(o[:, :], ones, EGC[:, 4 * i:4 * i + 4, :].rearrange("p a b -> p (a b)"),
                                       start=True, stop=True)
                    mm.then_inc(full(name), 1)

                for name in MIX:
                    step_pe(name)

                for n in range(NB):
                    pe.wait_ge(ev["oh_made"], n + 1)
                    for i in range(4):
                        pair(f"br{n}_{i}", PIECE[J_BR + n, 2 * P * i], (J_BR + n - 1) % NSLOT if i == 0 else None)
                pe.wait_ge(ev["merged_ready"], 4)

                def project_out(i, t, release):
                    w = weights(J_OUT + i, 512)
                    o = claim(pe, f"wo{i}_{t}")
                    group(o[:, :], [(merged[:, k, t * P:(t + 1) * P], w[:, k, :]) for k in range(DK)],
                          release).then_inc(full(f"wo{i}_{t}"), 1)

                def route(t):
                    for i in range(2):
                        landed(pe, f"xb{2 * t + i}")
                    return group(view("rt")[:, t * E:(t + 1) * E], [(xT[:, k, t * P:(t + 1) * P], rw[:, k, :]) for k in range(DK)])

                project_out(0, 0, (J_OUT - 1) % NSLOT)
                project_out(1, 0, None)
                project_out(0, 1, None)
                turn_x("xb", J_OUT % NSLOT, 0)
                project_out(1, 1, None)
                claim(pe, "rt")
                route(0)
                turn_x("xb", (J_OUT + 1) % NSLOT, 1)
                route(1).then_inc(full("rt"), 1)

                pe.wait_ge(ev["route_mask"], 1)
                o = claim(pe, "rp")
                mask = rtt[:, 2, 0:2 * E]
                group(o[:, 0:E], [(tri, mask[:, 0:E])])
                group(o[:, E:2 * E], [(ones, mask[:, 0:E]), (tri, mask[:, E:2 * E])])
                group(o[:, 2 * E:3 * E], [(ones, mask[:, 0:E]), (ones, mask[:, E:2 * E])]).then_inc(full("rp"), 1)

                def gather(names, release=(None, None)):
                    for half, (o, done) in enumerate(names):
                        c = slice(512 * half, 512 * half + 512)
                        for t in range(TT):
                            mm = pe.matmul(o[:, :], G[:, t, :], xt_hi[:, t, c], start=t == 0, stop=False)
                            if t == 0 and release[half] is not None:
                                mm.then_inc(w_free[release[half]], 1)
                            mm = pe.matmul(o[:, :], G[:, t, :], xt_lo[:, t, c], start=False, stop=t == TT - 1)
                        mm.then_inc(done, 1)

                def turn_gathered(o, half):
                    for c in range(4):
                        mm = turn(o[:, c * P:(c + 1) * P], xg[:, 512 * half + c * P:512 * half + (c + 1) * P])
                    return mm

                def scatter(release=(None, None)):
                    done = []
                    for t in range(TT):
                        for half in range(2):
                            mm = pe.matmul(bank[4 + 2 * t + half][:, :], scat[:, t * P:(t + 1) * P],
                                           oe[:, 512 * half:512 * half + 512], start=False, stop=True, skip_group_check=True)
                            if t == 0 and release[half] is not None:
                                mm.then_inc(w_free[release[half]], 1)
                            done.append(mm)
                    return done

                for i in range(4):
                    o = claim(pe, f"Y{i}")
                    pe.matmul(o[:, 0:64], cst[:, C_CAUS + P:C_CAUS + 2 * P], ident[:, 0:64], start=True, stop=False,
                              skip_group_check=True)
                pe.wait_ge(ev["g_made"], 1)
                pe.wait_ge(ev["xt_lo_made"], 2)
                gather([(claim(pe, f"XG{half}"), full(f"XG{half}")) for half in range(2)])
                for half in range(2):
                    landed(pe, f"XG{half}")
                    turn_gathered(claim(pe, f"XT{half}"), half).then_inc(full(f"XT{half}"), 1)
                pe.wait_ge(ev["moe_zero"], 1)

                def expert(i, odd):
                    s0 = 0 if odd else NSLOT

                    def weights_e(m, rows, n):
                        if odd:
                            pe.wait_ge(w_loaded[m], l * (16 * USES) + i * 16 + 16 * (PRE // NSLOT + 1))
                        else:
                            pe.wait_ge(w_loaded[s0 + m], l * (16 * PAIRS) + i * 16 + 16)
                        return slot_mem(s0 + m, rows, n)

                    wg = weights_e(0, DK, F)
                    wu = weights_e(1, DK, F)
                    o = claim_p(pe, i, f"GU{odd}")
                    if not odd:
                        for b in range(2):
                            pe.wait_ge(drained[b], i * PER_PAIR[b] + BEFORE[b])
                    for k in range(DK):
                        st = xgT[:, k, CAP * odd:CAP * odd + CAP]
                        mm = pe.matmul(o[0:64, :], st, wg[:, k, :], start=k == 0, stop=k == DK - 1)
                        if k == 0:
                            mm.then_inc(w_free[5 if odd else 2], 1)
                        mm = pe.matmul(o[64:128, :], st, wu[:, k, :], start=k == 0, stop=k == DK - 1)
                    mm.then_inc(full_p(f"GU{odd}"), 1)
                    if odd:
                        pe.wait_ge(ev["g_made"], i + 2)
                        gather([(claim_p(pe, i, f"XG{half}"), full_p(f"XG{half}")) for half in range(2)], (s0, s0 + 1))
                    else:
                        pe.wait_ge(drained[3], i * PER_PAIR[3] + BEFORE[3])
                        scatter((s0, s0 + 1))
                    landed_p(pe, i, f"GU{odd}")
                    o = claim_p(pe, i, f"HG{odd}")
                    if odd:
                        pe.wait_ge(ev["gw_made"], i + 1)
                        for t in range(TT):
                            turn(o[:, T + t * P:T + (t + 1) * P], Gw[:, t, :])
                    else:
                        pe.sem_inc(turn_seen, 1)
                    for k in range(4):
                        mm = pe.transpose(o[:, k * CAP:(k + 1) * CAP], hh[0:CAP, k * P:(k + 1) * P], cst[0:CAP, C_ID:C_ID + CAP])
                    mm.then_inc(full_p(f"HG{odd}"), 1)
                    if odd:
                        for half in range(2):
                            landed_p(pe, i, f"XG{half}")
                            turn_gathered(bank[PAIR[f"XT{half}"][0]], half).then_inc(full_p(f"XT{half}"), 1)
                    landed_p(pe, i, f"HG{odd}")
                    o = bank[PAIR[f"DN{odd}"][0]]
                    w = weights_e(2, 4, D)
                    for k in range(4):
                        for half in range(2):
                            mm = pe.matmul(o[64 * half:64 * half + 64, :], hT_pair[:, k * CAP:(k + 1) * CAP],
                                           w[:, k, 512 * half:512 * half + 512], start=k == 0, stop=k == 3)
                    mm.then_inc(full_p(f"DN{odd}"), 1)
                with pe.Fori(0, PAIRS) as i:
                    expert(i, 0)
                    expert(i, 1)
                landed_p(pe, PAIRS - 1, "DN1")
                for i, mm in enumerate(scatter()):
                    mm.then_inc(full(f"Y{i}"), 1)

                with pe.If(overflow(pe, l)):
                    pe.drain().then_inc(dense_free[0], 1)
                    pe.sem_inc(dense_free[1], 1)
                    with pe.Fori(0, E) as e:
                        def claim_d(name):
                            b, k = DENSE[name]
                            pe.wait_ge(drained[b], e * PER_DENSE[b] + (AFTER[b] + k))
                            return bank[b]

                        def weights_d(s, rows, n):
                            pe.wait_ge(dense_loaded[s], e * 16 + 16)
                            return W[:, s, 0:rows * n].rearrange("p (k n) -> p k n", n=n)

                        for t in range(TT):
                            for s, kind in enumerate("GU"):
                                w = weights_d(s, DK, F)
                                o = claim_d(f"{kind}{t}")
                                release = 2 if (kind, t) == ("G", 0) else 0 if (kind, t) == ("U", 1) else None
                                for k in range(DK):
                                    mm = pe.matmul(o[:, :], xT[:, k, t * P:(t + 1) * P], w[:, k, :], start=k == 0, stop=k == DK - 1)
                                    if k == 0 and release is not None:
                                        mm.then_inc(dense_free[release], 1)
                                mm.then_inc(filled[DENSE[f"{kind}{t}"][0]], 1)
                        for t in range(TT):
                            o = claim_d(f"HT{t}")
                            landed_d(pe, e, f"U{t}")
                            for k in range(4):
                                mm = turn(o[:, k * P:(k + 1) * P], dense_h[:, t, k * P:(k + 1) * P])
                                if t == k == 0:
                                    mm.then_inc(dense_free[1], 1)
                            mm.then_inc(filled[DENSE[f"HT{t}"][0]], 1)
                            w = weights_d(2, 4, D)
                            landed_d(pe, e, f"HT{t}")
                            for i in range(2):
                                o = claim_d(f"D{t}_{i}")
                                group(o[:, :], [(hT[:, t, k, :], w[:, k, i * 512:(i + 1) * 512]) for k in range(4)])\
                                    .then_inc(filled[DENSE[f"D{t}_{i}"][0]], 1)
                    pe.wait_ge(ev["dense_done_sp"], 1)

                pe.drain().then_inc(layer_done, 1)
                pe.wait_ge(layer_go, l + 1)

        eps = misc(29)

        def rstd(t):
            return lnst[:, 4 * t + 2:4 * t + 3]

        def halves(ap, n=2):
            return ap.rearrange("p (a b) -> p a b", a=n)

        @block.scalar
        def _(act):
            act.wait_ge(rope_in, 1)
            act.activation(rope_s[64:96, :], rtmp[64:96, 0, :], ACT.Sin).then_inc(rope_sin, 1)
            act.activation(rtmp[64:96, 1, :], rtmp[64:96, 0, :], ACT.Abs).then_inc(rope_chain, 1)
            act.wait_ge(rope_chain, 1)
            act.activation(rope_c[64:96, :], rtmp[64:96, 1, :], ACT.Sin, scale=-1.0, bias=misc(28, 64, 96)).then_inc(rope_sin, 1)

            with act.Fori(0, L) as l:
                count = [0]

                def link(ins):
                    count[0] += 1
                    ins.then_inc(act_chain, 1)
                    act.wait_ge(act_chain, count[0])

                def turned(kind, i):
                    t, k0 = i // 2, 4 * (i % 2)
                    o = arrived(act, f"{kind}{i}")
                    act.activation(xT[:, k0:k0 + 4, t * P:(t + 1) * P], halves(o[:, :], 4), ACT.Copy).then_inc(free(f"{kind}{i}"), 1)

                def make_hi(*pieces):
                    for i in pieces:
                        j, c, n = PIECES[i]
                        if c == 0:
                            act.wait_ge(w_loaded[j % NSLOT], l * (16 * USES) + 16 * (j // NSLOT + 1))
                            act.sem_inc(load_seen, 1)
                        if HI_BEFORE[i] is not None:
                            act.wait_ge(ev["hi_used"], HI_BEFORE[i] + 1)
                            act.wait_ge(ev["lo_made"], HI_BEFORE[i] + 1)
                        act.activation(hi_half(i), piece_of_w(i), ACT.Copy).then_inc(ev["hi_made"], 1)

                for i in range(4):
                    t, k0 = i // 2, 4 * (i % 2)
                    o = arrived(act, f"xa{i}")
                    act.activation(xh[:, k0:k0 + 4, t * P:(t + 1) * P], halves(o[:, :], 4), ACT.Copy)\
                       .then_inc(ev["xh_ready"], 1)
                make_hi(0, 1, 2, 3)
                act.wait_ge(consts_loaded, 16 * N_CONST)
                o = arrived(act, "cq")
                act.activation(c_raw[:, 0:2, :], halves(o[:, :]), ACT.Copy)
                act.activation(c_sq[:, 0:2, :], halves(o[:, :]), ACT.Square).then_inc(free("cq"), 1)
                make_hi(PIECE[1, 0], PIECE[1, P])
                o = arrived(act, "ckv")
                act.activation(c_raw[:, 2, :], o[:, 0:T], ACT.Copy)
                act.activation(kr[64:96, 0, :], o[0:ROPE, T:2 * T], ACT.Copy)
                act.activation(c_sq[:, 2, :], o[:, 0:T], ACT.Square).then_inc(free("ckv"), 1)
                make_hi(PIECE[1, 2 * P], PIECE[1, 3 * P])
                act.wait_ge(ev["pad_zero"], 1)
                for i in range(6):
                    o = arrived(act, f"gp{i}")
                    act.activation(pre[:, 2 * i:2 * i + 2, 3:3 + T], halves(o[:, :]), ACT.Copy).then_inc(free(f"gp{i}"), 1)
                    first = PIECE[2 + i // 2, 2 * P * (i % 2)]
                    make_hi(first, first + 1)
                make_hi(PIECE[4, 512])
                for i in range(2):
                    o = arrived(act, f"gz{i}")
                    act.activation(zs[:, 2 * i:2 * i + 2, :], halves(o[:, :]), ACT.Silu).then_inc(free(f"gz{i}"), 1)
                    make_hi(PIECE[5, 2 * P * i], PIECE[5, 2 * P * i + P])
                o = arrived(act, "abT")
                act.activation(abT, o[0:8, 0:T], ACT.Copy).then_inc(free("abT"), 1)
                for kind, dst, scale, j in (("fq", fq, FOX_SCALE, 6), ("fk", fk, 1.0, 7)):
                    for i in range(2):
                        o = arrived(act, f"{kind}{i}")
                        for r in range(2):
                            ins = act.activation(dst[0:64, 4 * i + r:4 * i + r + 3:2, :], halves(o[64 * r:64 * r + 64, :]),
                                                 ACT.Copy, scale=scale)
                        ins.then_inc(free(f"{kind}{i}"), 1)
                        make_hi(PIECE[j, 2 * P * i], PIECE[j, 2 * P * i + P])
                make_hi(PIECE[7, 512])
                for i in range(3):
                    act.wait_ge(ev["conv_ready"], i + 1)
                    act.activation(cv[:, 4 * i:4 * i + 4, :], cv[:, 4 * i:4 * i + 4, :], ACT.Silu).then_inc(ev["silu_ready"], 1)
                act.preload_act_table_set("natural_log_exp_and_others")
                o = arrived(act, "crms")
                act.activation(c_rstd[:, 0, :], o[:, 0:T], ACT.Ln, scale=1.0 / Q_RANK, bias=eps)
                act.activation(c_rstd[:, 1, :], o[:, T:2 * T], ACT.Ln, scale=1.0 / KV_RANK, bias=eps).then_inc(free("crms"), 1)
                landed(act, "crms")
                act.activation(c_rstd[:, 0:2, :], c_rstd[:, 0:2, :], ACT.Exp, scale=-0.5).then_inc(ev["crstd_ready"], 1)
                for t in range(TT):
                    o = arrived(act, f"fv{t}")
                    act.activation(fv[:, t, :], o[:, :], ACT.Copy).then_inc(free(f"fv{t}"), 1)
                o = arrived(act, "fT")
                act.activation(fT, o[0:8, 0:T], ACT.Copy).then_inc(free("fT"), 1)
                for i in range(4):
                    o = arrived(act, f"mq{i}")
                    act.activation(mq[0:QH, 2 * i:2 * i + 2, :], halves(o[0:QH, :]), ACT.Copy).then_inc(free(f"mq{i}"), 1)
                act.wait_ge(ev["rows_ready"], 1)
                act.activation(rl[:, 0:4], rl[:, 0:4], ACT.Exp).then_inc(ev["gexp_ready"], 1)
                act.wait_ge(ev["small_neg"], 1)
                link(act.activation(small[:, 2, :, :], small[:, 1, :, :], ACT.Exp))
                act.activation(small[:, 3, :, :], small[:, 2, :, :], ACT.Ln, bias=ones[:, 0:1]).then_inc(ev["small_ln"], 1)
                act.wait_ge(ev["small_ready"], 1)
                act.activation(small[:, 4, :, 4:8], small[:, 4, :, 4:8], ACT.Exp).then_inc(ev["beta_ready"], 1)
                for i in range(4):
                    o = arrived(act, f"mk{i}")
                    act.activation(mk[0:NOPE, 2 * i:2 * i + 2, :], halves(o[0:NOPE, :]), ACT.Copy).then_inc(free(f"mk{i}"), 1)
                for t in range(TT):
                    o = arrived(act, f"mv{t}")
                    act.activation(mv[:, t, :], o[:, :], ACT.Copy).then_inc(free(f"mv{t}"), 1)
                make_hi(PIECE[J_GATE, 0], PIECE[J_GATE, P])
                for i in range(2):
                    act.activation(gsq[:, 4 * i:4 * i + 4, :], cv[:, 4 * i:4 * i + 4, :], ACT.Square).then_inc(ev["gsq_ready"], 1)

                def exps(a):
                    landed(act, f"S{a}")
                    for i, (lo, hi) in enumerate(((0, P), (P, P + T))):
                        ins = act.activation(sm[:, a % 4, lo:hi], sm[:, a % 4, lo:hi], ACT.Exp, scale=-1.0,
                                             bias=att[:, 0, 2 * a + i:2 * a + i + 1], accum_out=att[:, 1, 2 * a + i:2 * a + i + 1])
                    ins.then_inc(ev["p_exp"], 1)

                def output_hi(n):
                    if n == 0:
                        arrived(act, "gate23")
                    elif n == 2:
                        arrived(act, "br0_3")
                    if n == 1:
                        act.wait_ge(ev["og_ready"], 2)
                    else:
                        for a in range(H):
                            landed(act, f"O{a + (H if n else 0)}")
                    act.activation(branch_halves(n)[0], oT[n][:, :, :], ACT.Copy).then_inc(ev["oh_made"], 1)

                def step_act(name):
                    if name.startswith("gate"):
                        c = int(name[4:])
                        if c == 16:
                            arrived(act, f"yd_{LEVELS[-1]}_1")
                            landed(act, f"xd_{LEVELS[-2]}_1")
                        o = arrived(act, name)
                        act.activation(gate_tile(c), o[:, 0:T], ACT.Copy).then_inc(free(name), 1)
                        if c + 2 < 24:
                            make_hi(PIECE[J_GATE, 0] + c + 2)
                        elif c == 22:
                            landed(act, "ot3")
                            landed(act, "su2")
                            act.activation(EGC[:, :, :].rearrange("p (a b) c -> p a (b c)", b=2), oT[1],
                                           ACT.Square).then_inc(ev["osq_ready"], 1)
                    elif name[0] == "S" and name[1:].isdigit():
                        if int(name[1:]) > 0:
                            exps(int(name[1:]) - 1)
                    elif name.startswith("PT"):
                        a = int(name[2:])
                        if a == 2 * H - PT_LAG:
                            exps(2 * H - 1)
                        o = arrived(act, name)
                        act.activation(pt[:, a % 2, :], o[:, 0:384], ACT.Copy).then_inc(free(name), 1)
                    elif name.startswith("gn"):
                        i = int(name[2:])
                        o = arrived(act, name)
                        act.activation(grstd[:, 2 * i:2 * i + 2, :], halves(o[:, :]), ACT.Ln, bias=eps).then_inc(free(name), 1)
                        landed(act, name)
                        if i < 2:
                            ins = act.activation(grstd[:, 2 * i:2 * i + 2, :], grstd[:, 2 * i:2 * i + 2, :], ACT.Exp,
                                                 scale=-0.5, bias=misc(30))
                        else:
                            ins = act.activation(grstd[:, 2 * i:2 * i + 2, :], grstd[:, 2 * i:2 * i + 2, :], ACT.Exp, scale=-0.5)
                        ins.then_inc(ev["grstd_ready"], 1)
                    elif name == "gcb0":
                        act.wait_ge(ev["tok_diff"], 1)
                        act.activation(tex[:, 1, :, :], gcc[:, :, 0:4], ACT.Exp)
                        act.activation(tex[:, 2, :, :], tex[:, 0, :, :], ACT.Exp).then_inc(ev["tok_exp"], 1)
                        row_exp(0)
                    elif name == "gcb1":
                        row_exp(1)
                        act.wait_ge(ev["decay_min"], 1)
                        act.activation(DEC[:, :, :], DEC[:, :, :], ACT.Exp).then_inc(ev["decay_exp"], 1)
                    elif name.startswith("tx") or name.startswith("t1_"):
                        t = int(name[-1])
                        o = arrived(act, name)
                        dst = (X if name.startswith("tx") else T1)[:, 4 * t:4 * t + 4, :]
                        act.activation(dst, halves(o[:, :], 4), ACT.Copy).then_inc(free(name), 1)
                    elif name.startswith("wt"):
                        t = int(name[2:])
                        o = arrived(act, name)
                        act.activation(WT[:, 4 * t:4 * t + 4, :], halves(o[:, :], 4), ACT.Copy, scale=-1.0).then_inc(free(name), 1)
                    elif name.startswith("vn"):
                        r = 64 * (int(name[2:]) % 2)
                        o = arrived(act, name)
                        act.activation(vn[r:r + 64, :], o[r:r + 64, :], ACT.Copy).then_inc(free(name), 1)
                    elif name.startswith("gr"):
                        i = int(name[2:])
                        if i == 0:
                            output_hi(0)
                            make_hi(*range(PIECE[J_BR, 0], PIECE[J_BR, 4 * P]))
                        o = arrived(act, name)
                        act.activation(DEC[:, 4 * i:4 * i + 4, :], halves(o[:, :], 4), ACT.Ln, scale=1.0 / P,
                                       bias=eps).then_inc(free(name), 1)
                        landed(act, name)
                        act.activation(DEC[:, 4 * i:4 * i + 4, :], DEC[:, 4 * i:4 * i + 4, :], ACT.Exp,
                                       scale=-0.5).then_inc(ev["orstd_ready"], 1)

                def row_exp(t):
                    act.wait_ge(ev["decay_diff"], t + 1)
                    o = arrived(act, f"gcb{t}")
                    act.activation(EGC[:, 4 * t:4 * t + 4, :], halves(o[:, :], 4), ACT.Exp).then_inc(free(f"gcb{t}"), 1)

                for name in MIX:
                    step_act(name)

                arrived(act, f"S{2 * H - 1}")
                act.dma_start(lnp[:, :, :], ln_params[bass.ds(l * 2, 1), :, :].rearrange("l a d -> (l a) d")
                              .partition_broadcast(P)).then_inc(ev["lnp_loaded"], 16)

                def sigmoid(n, i):
                    g = gate_lo[:, 8 * n:8 * n + 8, :] if n < 2 else gate_hi
                    landed(act, f"gate{8 * n + 7}")
                    act.activation(g[:, 4 * i:4 * i + 4, :], g[:, 4 * i:4 * i + 4, :], ACT.Sigmoid).then_inc(ev["gates_sig"], 1)

                first = PIECE[J_BR, 0]
                sigmoid(0, 0)
                sigmoid(0, 1)
                for n in range(NB):
                    for m in range(8):
                        if first + 8 * n + m + 4 < len(PIECES):
                            make_hi(first + 8 * n + m + 4)
                        if n + 1 < NB and m in (1, 3):
                            sigmoid(n + 1, m // 2)
                        if n + 1 < NB and m == 5:
                            output_hi(n + 1)
                act.preload_act_table_set("natural_log_exp_and_others")

                def norm_rstd(which, t):
                    act.wait_ge(ev["ln_var"], 2 * which + t + 1)
                    link(act.activation(rstd(t), lnst[:, 4 * t + 1:4 * t + 2], ACT.Ln, bias=eps))
                    act.activation(rstd(t), rstd(t), ACT.Exp, scale=-0.5).then_inc(ev["ln_rstd"], 1)

                for t in range(TT):
                    norm_rstd(0, t)
                    act.wait_ge(ev["x_normed_a"], t + 1)
                    act.wait_ge(ev["x_normed_b"], t + 1)
                    if t == 1:
                        act.dma_start(lnp[:, :, :], ln_params[bass.ds(l * 2 + 1, 1), :, :].rearrange("l a d -> (l a) d")
                                      .partition_broadcast(P)).then_inc(ev["lnp_loaded"], 16)
                    turned("xb", 2 * t)
                    act.activation(xt_hi[:, t, :], x_tok[:, t, :], ACT.Copy).then_inc(ev["xt_hi_made"], 1)
                o = arrived(act, "rt")
                act.activation(rtt[:, 0, 0:2 * E], o[:, 0:2 * E], ACT.Sigmoid).then_inc(free("rt"), 1)

                for half in range(2):
                    o = arrived(act, f"XG{half}")
                    act.activation(xg[:, 512 * half:512 * half + 512], o[:, :], ACT.Copy).then_inc(free(f"XG{half}"), 1)
                with act.Fori(0, PAIRS) as i:
                    for odd in range(2):
                        o = arrived_p(act, i, f"GU{odd}")
                        act.activation(hs[0:CAP, :], o[0:CAP, :], ACT.Silu).then_inc(ev["silu_gate"], 1)
                        if odd:
                            for half in range(2):
                                o = arrived_p(act, i, f"XG{half}")
                                act.activation(xg[:, 512 * half:512 * half + 512], o[:, :], ACT.Copy).then_inc(free_p(f"XG{half}"), 1)
                        o = arrived_p(act, i, f"HG{odd}")
                        dst = hT_scat if odd else hT_pair
                        act.activation(dst, o[:, 0:dst.shape[1]], ACT.Copy).then_inc(free_p(f"HG{odd}"), 1)
                with act.If(overflow(act, l)):
                    with act.Fori(0, E) as e:
                        for t in range(TT):
                            o = arrived_d(act, e, f"G{t}")
                            b, k = DENSE[f"U{t}"]
                            act.wait_ge(drained[b], e * PER_DENSE[b] + (AFTER[b] + k))
                            act.activation(dense_s[:, t, :], o[:, :], ACT.Silu).then_inc(drained[DENSE[f"G{t}"][0]], 1)
                        for t in range(TT):
                            o = arrived_d(act, e, f"HT{t}")
                            act.activation(hT[:, t, :, :], halves(o[:, :], 4), ACT.Copy).then_inc(drained[DENSE[f"HT{t}"][0]], 1)
                act.preload_act_table_set("natural_log_exp_and_others")
                for t in range(TT):
                    norm_rstd(1, t)
                act.drain().then_inc(layer_done, 1)
                act.wait_ge(layer_go, l + 1)

        @block.vector
        def _(dve):
            dve.wait_ge(rows_turned, 1)
            dve.tensor_copy(pcols_all[:, :], bank[7][:, 0:L * PR]).then_inc(pcols_ready, 1)
            dve.wait_ge(first_loaded, 16 * N_FIRST)
            ang, turns, rest = rtmp[64:96, 0, :], rtmp[64:96, 1, :], rope_s[64:96, :]
            start = [0]

            def rope_link(ins):
                start[0] += 1
                ins.then_inc(dve_start, 1)
                dve.wait_ge(dve_start, start[0])

            rope_link(dve.tensor_copy(rest, kr[64:96, 0, :].bitcast(I32)))
            rope_link(dve.tensor_scalar(ang, rest, misc(0, 64, 96), None, ALU.mult))
            magic = 1.5 * 2.0 ** 23
            rope_link(dve.tensor_scalar(rest, ang, 1.0 / (2 * np.pi), magic, ALU.mult, ALU.add))
            rope_link(dve.tensor_scalar(turns, rest, magic, None, ALU.subtract))
            two_pi, parts = 2 * np.pi, []
            for bits in (7, 12):
                q = 2.0 ** (bits - 3)
                parts.append(np.floor(two_pi * q) / q if not parts else np.round((two_pi - sum(parts)) * 2.0 ** 20) / 2.0 ** 20)
            parts.append(two_pi - sum(parts))
            for part in parts:
                rope_link(dve.scalar_tensor_tensor(ang, turns, -float(part), ang, ALU.mult, ALU.add))
            dve.tensor_scalar(ang, ang, 3.1415925, -3.1415925, ALU.min, ALU.max).then_inc(rope_in, 1)
            dve.wait_ge(rope_sin, 2)
            dve.tensor_scalar(rope_s[64:96, :], rope_s[64:96, :], misc(1, 64, 96), None, ALU.mult).then_inc(rope_ready, 1)
            dve.wait_ge(rope_ready, 1)

            with dve.Fori(0, L) as l:
                count = [0]

                def link(ins):
                    count[0] += 1
                    ins.then_inc(dve_chain, 1)
                    dve.wait_ge(dve_chain, count[0])

                dve.tensor_copy(pc[:, :], pcols_all[:, bass.ds(l * PR, PR)])
                link(dve.tensor_copy(rl[:, :], rowb[:, bass.ds(l * 16, 16)]))
                dve.sem_inc(ev["rows_ready"], 1)

                def turned(kind, i):
                    t, k0 = i // 2, 4 * (i % 2)
                    o = arrived(dve, f"{kind}{i}")
                    dve.tensor_copy(xT[:, k0:k0 + 4, t * P:(t + 1) * P], halves(o[:, :], 4)).then_inc(free(f"{kind}{i}"), 1)

                for i in range(4):
                    t, k0 = i // 2, 4 * (i % 2)
                    dve.wait_ge(ev["xh_ready"], i + 1)
                    o = arrived(dve, f"xa{i}")
                    part = (slice(None), slice(k0, k0 + 4), slice(t * P, (t + 1) * P))
                    dve.tensor_tensor(xl[part], halves(o[:, :], 4), xh[part].bitcast(F32), ALU.subtract).then_inc(free(f"xa{i}"), 1)

                def make_lo(*pieces):
                    for i in pieces:
                        dve.wait_ge(ev["hi_made"], i + 1)
                        dve.tensor_tensor(lo_half(i), piece_of_w(i), hi_half(i).bitcast(F32), ALU.subtract).then_inc(ev["lo_made"], 1)

                def conv(i, j):
                    if j == 0:
                        landed(dve, f"gp{2 * i}")
                        landed(dve, f"gp{2 * i + 1}")
                    for c in range(4 * i, 4 * i + 4):
                        tap = pc[:, R_CONV + 12 * j + c:R_CONV + 12 * j + c + 1]
                        if j == 0:
                            ins = dve.tensor_scalar(cv[:, c, :], pre[:, c, 0:T], tap, None, ALU.mult)
                        else:
                            ins = dve.scalar_tensor_tensor(cv[:, c, :], pre[:, c, j:j + T], tap, cv[:, c, :], ALU.mult, ALU.add)
                    if j < CONV - 1:
                        link(ins)
                    else:
                        ins.then_inc(ev["conv_ready"], 1)

                dve.wait_ge(consts_loaded, 16 * N_CONST)
                make_lo(*range(PIECE[3, 0]))
                for i in range(3):
                    for j in range(CONV):
                        make_lo(PIECE[3 + i, j * P])
                        conv(i, j)
                    if i == 1:
                        make_lo(PIECE[4, 512])
                o = arrived(dve, "gab")[:, 0:16].rearrange("p (t c) -> p t c", t=TT)
                dve.scalar_tensor_tensor(small[:, 0, :, 0:4], o[:, :, 0:4], -1.0,
                                         rl[:, 4:8].unsqueeze(1).broadcast_to([P, TT, 4]), ALU.mult, ALU.subtract)
                dve.tensor_copy(small[:, 0, :, 4:8], o[:, :, 4:8]).then_inc(free("gab"), 1)
                make_lo(*range(PIECE[6, 0], PIECE[7, 512]))
                dve.wait_ge(ev["crstd_ready"], 1)
                landed(dve, "cq")
                landed(dve, "ckv")
                for i in range(3):
                    dve.scalar_tensor_tensor(c_n[:, i, :], c_raw[:, i, :], pc[:, i:i + 1], c_rstd[:, i // 2, :],
                                             ALU.mult, ALU.mult).then_inc(ev["cn_ready"], 1)
                make_lo(PIECE[7, 512])
                o = arrived(dve, "ff")[:, 0:16].rearrange("p (t c) -> p t c", t=TT)
                dve.tensor_tensor(small[:, 0, :, 8:16], o, rl[:, 8:16].unsqueeze(1).broadcast_to([P, TT, 8]),
                                  ALU.add).then_inc(free("ff"), 1)
                landed(dve, "gab")
                landed(dve, "ff")
                dve.scalar_tensor_tensor(small[:, 1, :, :], small[:, 0, :, :], -1.0, small[:, 0, :, :],
                                         ALU.mult, ALU.min).then_inc(ev["small_neg"], 1)
                dve.wait_ge(ev["small_ln"], 1)
                link(dve.scalar_tensor_tensor(small[:, 4, :, :], small[:, 0, :, :], 0.0, small[:, 3, :, :], ALU.min, ALU.subtract))
                dve.tensor_copy(small[:, 5, :, 0:8], small[:, 4, :, 8:16])
                dve.tensor_scalar(small[:, 5, :, 8:16], small[:, 4, :, 8:16], -1.0, None, ALU.mult)
                dve.wait_ge(ev["gexp_ready"], 1)
                dve.tensor_tensor(small[:, 4, :, 0:4], small[:, 4, :, 0:4], rl[:, 0:4].unsqueeze(1).broadcast_to([P, TT, 4]),
                                  ALU.mult).then_inc(ev["small_ready"], 1)
                dve.wait_ge(ev["small_ready"], 1)

                def spread(dst, cols, done):
                    dve.tensor_copy(dst.rearrange("p (t h) c -> p t h c", t=TT),
                                    small[:, 4, :, cols:cols + 4].unsqueeze(3).broadcast_to([P, TT, 4, P])).then_inc(ev[done], 1)

                spread(gB[:, :, :], 0, "gb_ready")
                def both(ap):
                    return ap[64:96, :].unsqueeze(1).broadcast_to([32, 2, T])

                for i in range(4):
                    o = arrived(dve, f"mr{i}")
                    q = mq[64:96, 2 * i:2 * i + 2, :]
                    dve.tensor_tensor(rtmp[64:96, :, :], halves(o[64:96, :]), both(rope_s), ALU.mult).then_inc(free(f"mr{i}"), 1)
                    link(dve.tensor_tensor(q, q, both(rope_c), ALU.mult))
                    dve.tensor_tensor(q, q, rtmp[64:96, :, :], ALU.add).then_inc(ev["mq_ready"], 1)
                    dve.wait_ge(ev["mq_ready"], i + 1)
                o = arrived(dve, "mkr")
                dve.tensor_tensor(rtmp[64:96, 0, :], o[64:96, 0:T], rope_s[64:96, :], ALU.mult).then_inc(free("mkr"), 1)
                link(dve.tensor_tensor(kr[64:96, 1, :], kr[64:96, 0, :], rope_c[64:96, :], ALU.mult))
                dve.tensor_tensor(kr[64:96, 1, :], kr[64:96, 1, :], rtmp[64:96, 0, :], ALU.add).then_inc(ev["kr_turned"], 1)
                dve.wait_ge(ev["kr_turned"], 1)
                o = arrived(dve, "fF")
                dve.tensor_scalar(fe[64:80, 0, :], o[64:80, 0:T], misc(2, 64, 80), misc(3, 64, 80), ALU.mult, ALU.add)
                dve.tensor_scalar(fe[64:80, 1, :], o[64:80, 0:T], misc(3, 64, 80), misc(2, 64, 80), ALU.mult, ALU.add)\
                   .then_inc(free("fF"), 1)

                make_lo(PIECE[J_GATE, 0])

                def rows4(ap):
                    return ap.unsqueeze(2).broadcast_to([P, 4, P])

                def masks4(ap, n=8):
                    return ap.unsqueeze(1).broadcast_to([P, n, P])

                def probabilities(a):
                    dve.wait_ge(ev["p_exp"], a + 1)
                    link(dve.reciprocal(att[:, 2, 2 * a:2 * a + 2], att[:, 1, 2 * a:2 * a + 2]))
                    for i, (lo, hi) in enumerate(((0, P), (P, P + T))):
                        ins = dve.tensor_scalar(sm[:, a % 4, lo:hi], sm[:, a % 4, lo:hi],
                                                att[:, 2, 2 * a + i:2 * a + i + 1], None, ALU.mult)
                    ins.then_inc(ev["p_ready"], 1)

                def step_dve(name):
                    if name.startswith("gate"):
                        if int(name[4:]) < 23:
                            make_lo(PIECE[J_GATE, 0] + int(name[4:]) + 1)
                    elif name[0] == "S" and name[1:].isdigit():
                        a = int(name[1:])
                        if a >= 4:
                            arrived(dve, f"PT{a - 4}")
                        o = arrived(dve, name)
                        scale = MLA_SCALE if a < H else 1.0
                        for i, (lo, hi) in enumerate(((0, P), (P, P + T))):
                            ins = dve.tensor_tensor_reduce(sm[:, a % 4, lo:hi], o[:, lo:hi],
                                                           causal[:, 0:P] if i == 0 else causal[:, P:P + T],
                                                           -scale, 3e38, ALU.add, ALU.min, att[:, 0, 2 * a + i:2 * a + i + 1])
                        ins.then_inc(free(name), 1)
                        if a >= 2:
                            probabilities(a - 2)
                    elif name.startswith("PT"):
                        a = int(name[2:]) + PT_LAG + 1
                        if a - 2 in (2 * H - 2, 2 * H - 1):
                            probabilities(a - 2)
                    elif name[0] == "O":
                        a = int(name[1:])
                        h, r = a % H, 64 * (a % 2)
                        o = arrived(dve, name)
                        dve.tensor_copy(oT[0 if a < H else 2][r:r + 64, h // 2, :], o[r:r + 64, 0:T]).then_inc(free(name), 1)
                    elif name.startswith("gn"):
                        i = int(name[2:])
                        dve.wait_ge(ev["grstd_ready"], i + 1)
                        q = cv[:, 2 * i:2 * i + 2, :]
                        dve.tensor_tensor(q, q, grstd[:, 2 * i:2 * i + 2, :], ALU.mult).then_inc(ev["qk_ready"], 1)
                        if i == 3:
                            dve.wait_ge(ev["qk_ready"], 4)
                            dve.wait_ge(ev["beta_ready"], 1)
                            spread(bB, 4, "bb_ready")
                    elif name == "gcc":
                        o = arrived(dve, name)
                        dve.tensor_copy(gcc[:, :, :], o[:, 0:16].rearrange("p (t c) -> p t c", t=TT)).then_inc(free(name), 1)
                        landed(dve, name)
                        dve.tensor_tensor(tex[:, 0, :, :], gcc[:, :, 4:8], gcc[:, :, 0:4], ALU.subtract).then_inc(ev["tok_diff"], 1)
                    elif name.startswith("gcb"):
                        t = int(name[3:])
                        o = arrived(dve, name)
                        dve.tensor_tensor(DEC[:, 4 * t:4 * t + 4, :], halves(o[:, :], 4), rows4(gcc[:, t, 0:4]),
                                          ALU.subtract).then_inc(ev["decay_diff"], 1)
                        if t == 1:
                            dve.wait_ge(ev["decay_diff"], 2)
                            dve.tensor_scalar(DEC[:, :, :], DEC[:, :, :], 0.0, None, ALU.min).then_inc(ev["decay_min"], 1)
                            dve.wait_ge(ev["tok_exp"], 1)
                            link(dve.tensor_tensor(tex[:, 3, :, :], tex[:, 1, :, :], small[:, 4, :, 4:8], ALU.mult))
                    elif name.startswith("gbt"):
                        t = int(name[3:])
                        dve.wait_ge(ev["decay_ready"], 1)
                        o = arrived(dve, name)
                        dve.tensor_tensor(LT[:, 4 * t:4 * t + 4, :], halves(o[:, :], 4), DEC[:, 4 * t:4 * t + 4, :],
                                          ALU.mult).then_inc(free(name), 1)
                    elif name.startswith("kk"):
                        t = int(name[2:])
                        landed(dve, f"gbt{t}")
                        o = arrived(dve, name)
                        dve.tensor_tensor(LT[:, 4 * t:4 * t + 4, :], halves(o[:, :], 4), LT[:, 4 * t:4 * t + 4, :],
                                          ALU.mult).then_inc(free(name), 1)
                        if t == 1:
                            landed(dve, "kk0")
                            landed(dve, "kk1")
                            link(dve.tensor_tensor(T1, LT, masks4(level(0)), ALU.mult))
                            dve.tensor_tensor(Y, masks4(ident), T1, ALU.subtract).then_inc(ev["y_first"], 1)
                    elif name.startswith("kq"):
                        t = int(name[2:])
                        o = arrived(dve, name)
                        dve.tensor_tensor(AT[:, 4 * t:4 * t + 4, :], halves(o[:, :], 4), DEC[:, 4 * t:4 * t + 4, :],
                                          ALU.mult).then_inc(free(name), 1)
                    elif name == "tk1" or name == "tv1":
                        arrived(dve, name)
                        for t in range(TT):
                            o = arrived(dve, f"{name[:2]}{t}")
                            if name == "tk1":
                                dve.tensor_tensor(RK[:, 4 * t:4 * t + 4, :], halves(o[:, :], 4), rows4(tex[:, 3, t, :]), ALU.mult)
                                ins = dve.tensor_tensor(KD[:, 4 * t:4 * t + 4, :], halves(o[:, :], 4), rows4(tex[:, 2, t, :]), ALU.mult)
                            else:
                                ins = dve.tensor_tensor(RV[:, 4 * t:4 * t + 4, :], halves(o[:, :], 4),
                                                        rows4(small[:, 4, t, 4:8]), ALU.mult)
                            ins.then_inc(free(f"{name[:2]}{t}"), 1)
                    elif name[:3] in ("xd_", "yd_"):
                        t = int(name[-1])
                        dst = (X if name[0] == "x" else Y)[:, 4 * t:4 * t + 4, :]
                        o = arrived(dve, name)
                        if name.startswith("xd_2_"):
                            landed(dve, f"tx{t}")
                        dve.tensor_tensor(dst, dst, halves(o[:, :], 4), ALU.subtract).then_inc(free(name), 1)
                    elif name.startswith("ot"):
                        n = int(name[2:])
                        o = arrived(dve, name)
                        dve.tensor_copy(oT[1][:, :, n * GC:(n + 1) * GC], o[:, 0:GH * GC].rearrange("p (h c) -> p h c", c=GC))\
                           .then_inc(free(name), 1)
                        if 0 < n < 3:
                            t, r = n // 2, 64 * (n % 2)
                            last = EGC[:, 4 * t:4 * t + 4, r + 63]
                            link(dve.tensor_tensor(state[:, :, :], state[:, :, :], rows4(last), ALU.mult))
                    elif name.startswith("su"):
                        o = arrived(dve, name)
                        if name == "su0":
                            dve.tensor_copy(state[:, :, :], halves(o[:, :], 4)).then_inc(free(name), 1)
                        else:
                            dve.tensor_tensor(state[:, :, :], state[:, :, :], halves(o[:, :], 4), ALU.add).then_inc(free(name), 1)
                    elif name == "gr1":
                        dve.wait_ge(ev["oh_made"], 1)
                        dve.tensor_tensor(branch_halves(0)[1], oT[0][:, :, :], branch_halves(0)[0].bitcast(F32), ALU.subtract)\
                           .then_inc(ev["o_mla_lo"], 1)
                        make_lo(*range(PIECE[J_BR, 0], PIECE[J_BR, 4 * P]))
                        og = oT[1].rearrange("p h c -> p (h c)")
                        for i in range(2):
                            dve.wait_ge(ev["orstd_ready"], i + 1)
                            part = og[:, 512 * i:512 * i + 512]
                            link(dve.scalar_tensor_tensor(part, part, pc[:, R_ON:R_ON + 1],
                                                          DEC[:, 4 * i:4 * i + 4, :].rearrange("p a b -> p (a b)"), ALU.mult, ALU.mult))
                            dve.tensor_tensor(part, part, zs[:, 2 * i:2 * i + 2, :].rearrange("p a b -> p (a b)"), ALU.mult)\
                               .then_inc(ev["og_ready"], 1)

                for name in MIX:
                    step_dve(name)

                first = PIECE[J_BR, 0]
                for n in range(NB):
                    for i in range(4):
                        ahead = first + 8 * n + 2 * i + 4
                        make_lo(*range(min(ahead, len(PIECES)), min(ahead + 2, len(PIECES))))
                        dve.wait_ge(ev["gates_sig"], 2 * n + i // 2 + 1)
                        g = (gate_lo[:, 8 * n + 2 * i:8 * n + 2 * i + 2, :] if n < 2 else gate_hi[:, 2 * i:2 * i + 2, :])
                        o = arrived(dve, f"br{n}_{i}")
                        m = merged[:, 2 * i:2 * i + 2, :]
                        if n == 0:
                            dve.tensor_tensor(m, halves(o[:, :]), g, ALU.mult).then_inc(free(f"br{n}_{i}"), 1)
                        else:
                            dve.tensor_tensor(brtmp[:, i % 2, :], o[:, :], g.rearrange("p a b -> p (a b)"), ALU.mult)\
                               .then_inc(free(f"br{n}_{i}"), 1)
                            landed(dve, f"br{n}_{i}")
                            ins = dve.tensor_tensor(m, m, halves(brtmp[:, i % 2, :]), ALU.add)
                            if n == 1:
                                link(ins)
                            else:
                                ins.then_inc(ev["merged_ready"], 1)

                dve.wait_ge(ev["merged_ready"], 4)
                dve.sem_inc(gdn_mem_free, 1)

                def statistics(t, i):
                    ins = dve.bn_stats(bnst[:, t, i, :], res[:, t, 512 * i:512 * i + 512])
                    if i:
                        link(ins)
                        dve.bn_aggr(lnst[:, 4 * t:4 * t + 2], bnst[:, t, :, :].rearrange("p a b -> p (a b)")).then_inc(ev["ln_var"], 1)

                def norm(which, tiles):
                    dve.wait_ge(ev["lnp_loaded"], 16 * (which + 1))
                    for t in tiles:
                        dve.wait_ge(ev["ln_rstd"], 2 * which + t + 1)
                        a, b = res[:, t, 0:512], res[:, t, 512:D]
                        dve.tensor_scalar(b, b, lnst[:, 4 * t:4 * t + 1], rstd(t), ALU.subtract, ALU.mult).then_inc(ev["ln_scaled"], 1)
                        link(dve.tensor_scalar(a, a, lnst[:, 4 * t:4 * t + 1], rstd(t), ALU.subtract, ALU.mult))
                        link(dve.tensor_tensor(a, a, lnp[:, 0, 0:512], ALU.mult))
                        dve.tensor_tensor(x_tok[:, t, 0:512], a, lnp[:, 1, 0:512], ALU.add).then_inc(ev["x_normed_a"], 1)

                def mixed(i, t):
                    c = slice(512 * i, 512 * i + 512)
                    o = arrived(dve, f"wo{i}_{t}")
                    dve.scalar_tensor_tensor(res[:, t, c], x_tok[:, t, c], ALPHA, o[:, :], ALU.mult, ALU.add)\
                       .then_inc(free(f"wo{i}_{t}"), 1)
                    landed(dve, f"wo{i}_{t}")
                    statistics(t, i)

                def split_x(t):
                    dve.wait_ge(ev["xt_hi_made"], t + 1)
                    dve.tensor_tensor(xt_lo[:, t, :], x_tok[:, t, :], xt_hi[:, t, :].bitcast(F32), ALU.subtract)\
                       .then_inc(ev["xt_lo_made"], 1)

                mixed(0, 0)
                mixed(1, 0)
                norm(0, [0])
                mixed(0, 1)
                turned("xb", 1)
                split_x(0)
                mixed(1, 1)
                norm(0, [1])
                turned("xb", 3)
                split_x(1)

                landed(dve, "rt")
                score = rtt[:, 0, 0:32]
                sel, flag, tmp = rtt[:, 1, 0:32], rtt[:, 2, 0:32], rtt[:, 3, 0:32]
                big, big2 = rtt[:, 4, :], rtt[:, 5, :]
                gsc, gfl, den = rtt[:, 6, 0:8], rtt[:, 6, 8:16], rtt[:, 6, 16:18]
                rb = rowb[:, L * 16:L * 16 + E].unsqueeze(1).broadcast_to([P, TT, E])
                link(dve.tensor_tensor(halves(sel), halves(score), rb, ALU.add))

                def best(values, n, limit, out_flag):
                    vj = values.rearrange("p (g e) -> p g e", e=4).unsqueeze(2).broadcast_to([P, n, 4, 4])
                    vi = values.rearrange("p (g e) -> p g e", e=4).unsqueeze(3).broadcast_to([P, n, 4, 4])
                    b1 = big[:, 0:16 * n].rearrange("p (g i j) -> p g i j", i=4, j=4)
                    b2 = big2[:, 0:16 * n].rearrange("p (g i j) -> p g i j", i=4, j=4)
                    dve.tensor_tensor(b1, vj, vi, ALU.is_gt)
                    link(dve.tensor_tensor(b2, vj, vi, ALU.is_equal))
                    b2r = big2[:, 0:16 * n].rearrange("p (g m) -> p g m", m=16)
                    link(dve.tensor_tensor(b2r, b2r, misc(12, n=16).unsqueeze(1).broadcast_to([P, n, 16]), ALU.mult))
                    link(dve.tensor_tensor(big[:, 0:16 * n], big[:, 0:16 * n], big2[:, 0:16 * n], ALU.add))
                    link(dve.tensor_reduce(tmp[:, 0:4 * n], big[:, 0:16 * n].rearrange("p (m j) -> p m j", j=4), AX.X, ALU.add))
                    link(dve.tensor_scalar(out_flag, tmp[:, 0:4 * n], limit - 0.5, None, ALU.is_lt))

                best(sel, 8, 2, flag)
                link(dve.tensor_tensor(tmp, sel, flag, ALU.mult))
                link(dve.tensor_reduce(gsc, tmp.rearrange("p (g e) -> p g e", e=4), AX.X, ALU.add))
                best(gsc, 2, 1, gfl)
                dve.tensor_tensor(flag.rearrange("p (g e) -> p g e", e=4), flag.rearrange("p (g e) -> p g e", e=4),
                                  gfl.unsqueeze(2).broadcast_to([P, 8, 4]), ALU.mult).then_inc(ev["route_mask"], 1)
                dve.wait_ge(ev["route_mask"], 1)
                dve.memset(slot[:, :, E:E + 2], -1.0)
                dve.memset(comb[:, :, E:E + 2], 0.0)
                link(dve.tensor_tensor(tmp, flag, score, ALU.mult))
                link(dve.tensor_reduce(den, halves(tmp), AX.X, ALU.add))
                link(dve.reciprocal(den, den))
                link(dve.tensor_tensor(comb[:, :, 0:E], halves(tmp), den.unsqueeze(2).broadcast_to([P, TT, E]), ALU.mult))
                o = arrived(dve, "rp")
                link(dve.tensor_tensor(tmp, o[:, 0:2 * E], flag, ALU.mult))
                dve.tensor_reduce(over[:, 0:1], o[:, 2 * E:3 * E], AX.X, ALU.max).then_inc(free("rp"), 1)
                link(dve.tensor_scalar(slot[:, :, 0:E], halves(tmp), -1.0, None, ALU.add))
                landed(dve, "rp")
                dve.tensor_scalar(over_flag[:, :], over[:, 0:1], CAP + 0.5, None, ALU.is_gt).then_inc(over_known, 1)
                link(dve.tensor_scalar(comb_over[:, :, :], slot[:, :, 0:E], CAP - 0.5, None, ALU.is_gt))
                link(dve.tensor_tensor(comb_over[:, :, :], comb_over[:, :, :], comb[:, :, 0:E], ALU.mult))

                def col(tile, t, e):
                    return tile[:, t, e:e + 1] if isinstance(e, int) else tile[:, t, bass.ds(e, 1)]

                def gather_matrix(e):
                    for t in range(TT):
                        for odd in range(2):
                            ins = dve.tensor_scalar(G[:, t, CAP * odd:CAP * odd + CAP], cst[:, C_SLOT:C_SLOT + CAP],
                                                    col(slot, t, e + odd), None, ALU.is_equal)
                    ins.then_inc(ev["g_made"], 1)

                gather_matrix(0)
                dve.memset(oe, 0.0)
                dve.memset(hT_scat, 0.0).then_inc(ev["moe_zero"], 1)
                for half in range(2):
                    o = arrived(dve, f"XT{half}")
                    dve.tensor_copy(xgT[:, 4 * half:4 * half + 4, :], halves(o[:, :], 4)).then_inc(free(f"XT{half}"), 1)

                with dve.Fori(0, PAIRS) as i:
                    for odd in range(2):
                        gu = arrived_p(dve, i, f"GU{odd}")
                        dve.wait_ge(ev["silu_gate"], i * 2 + odd + 1)
                        dve.tensor_tensor(hh[0:CAP, :], gu[64:128, :], hs[0:CAP, :], ALU.mult).then_inc(free_p(f"GU{odd}"), 1)
                        if odd:
                            for half in range(2):
                                o = arrived_p(dve, i, f"XT{half}")
                                dve.tensor_copy(xgT[:, 4 * half:4 * half + 4, :], halves(o[:, :], 4)).then_inc(free_p(f"XT{half}"), 1)
                        else:
                            gather_matrix(i * 2 + 2)
                            for t in range(TT):
                                for h in range(2):
                                    ins = dve.tensor_scalar(Gw[:, t, CAP * h:CAP * h + CAP], cst[:, C_SLOT:C_SLOT + CAP],
                                                            col(slot, t, i * 2 + h), col(comb, t, i * 2 + h), ALU.is_equal, ALU.mult)
                            ins.then_inc(ev["gw_made"], 1)
                        o = arrived_p(dve, i, f"DN{odd}")
                        r = CAP * odd
                        dve.tensor_copy(oe[r:r + CAP, 0:512], o[0:CAP, :])
                        dve.tensor_copy(oe[r:r + CAP, 512:D], o[CAP:P, :]).then_inc(free_p(f"DN{odd}"), 1)
                over_here = overflow(dve, l)
                dve.wait_ge(ev["x_normed_b"], 2)
                for t in range(TT):
                    for i in range(2):
                        o = arrived(dve, f"Y{2 * t + i}")
                        c = slice(512 * i, 512 * i + 512)
                        dve.scalar_tensor_tensor(res[:, t, c], x_tok[:, t, c], ALPHA, o[:, :], ALU.mult, ALU.add)\
                           .then_inc(free(f"Y{2 * t + i}"), 1)
                for i in range(4):
                    landed(dve, f"Y{i}")
                with dve.If(over_here):
                    with dve.Fori(0, E) as e:
                        for t in range(TT):
                            landed_d(dve, e, f"G{t}")
                            o = arrived_d(dve, e, f"U{t}")
                            dve.tensor_tensor(dense_h[:, t, :], o[:, :], dense_s[:, t, :], ALU.mult)\
                               .then_inc(drained[DENSE[f"U{t}"][0]], 1)
                        for t in range(TT):
                            for i in range(2):
                                o = arrived_d(dve, e, f"D{t}_{i}")
                                b, k = DENSE[f"D{t}_{i}"]
                                dve.wait_ge(drained[b], e * PER_DENSE[b] + (AFTER[b] + k - 1))
                                part = res[:, t, 512 * i:512 * i + 512]
                                dve.scalar_tensor_tensor(part, o[:, :], comb_over[:, t, bass.ds(e, 1)], part, ALU.mult, ALU.add)\
                                   .then_inc(drained[b], 1)
                    for b in (6, 7):
                        dve.wait_ge(drained[b], AFTER[b] + 2 * E)
                for t in range(TT):
                    for i in range(2):
                        statistics(t, i)
                norm(1, range(TT))
                dve.drain().then_inc(layer_done, 1)
                dve.wait_ge(layer_go, l + 1)

        @block.gpsimd
        def _(pool):
            pool.wait_ge(consts_loaded, 16 * N_CONST)
            with pool.Fori(0, L) as l:
                pool.memset(pre[:, :, 0:3], 0.0).then_inc(ev["pad_zero"], 1)
                pool.wait_ge(ev["pad_zero"], 1)
                pool.wait_ge(ev["kr_turned"], 1)
                pool.tensor_copy(mk[64:96, :, :], kr[64:96, 1, :].unsqueeze(1).broadcast_to([32, H, T])).then_inc(ev["kr_ready"], 1)
                pool.wait_ge(ev["kr_ready"], 1)
                pool.wait_ge(ev["decay_exp"], 1)
                pool.tensor_tensor(DEC[:, :, :], DEC[:, :, :], tri_bd.unsqueeze(1).broadcast_to([P, 8, P]), ALU.mult)\
                    .then_inc(ev["decay_ready"], 1)
                pool.wait_ge(ev["decay_ready"], 1)
                landed(pool, "fF")
                pool.tensor_copy(fq[64:80, :, :], fe[64:80, 0, :].unsqueeze(1).broadcast_to([16, H, T])).then_inc(ev["fext_ready"], 1)
                pool.wait_ge(ev["fext_ready"], 1)
                pool.tensor_tensor(fk[64:80, :, :], fe[64:80, 1, :].unsqueeze(1).broadcast_to([16, H, T]),
                                   cst[64:80, C_MISC + 4:C_MISC + 12].unsqueeze(2).broadcast_to([16, H, T]), ALU.mult)\
                    .then_inc(ev["fext_ready"], 1)
                pool.wait_ge(ev["fext_ready"], 2)
                landed(pool, "kk0")
                landed(pool, "kk1")
                for n in range(1, len(LEVELS)):
                    if n > 1:
                        arrived(pool, f"t1_{LEVELS[n - 1]}_1")
                    pool.tensor_tensor(CT[:, :, :], LT, level(n).unsqueeze(1).broadcast_to([P, 8, P]), ALU.mult)\
                        .then_inc(ev["ct_ready"], 1)
                    if n == 1:
                        arrived(pool, "kq1")
                        landed(pool, "gcb0")
                        landed(pool, "gcb1")
                        for t in range(TT):
                            q = cv[:, 0:4, t * P:(t + 1) * P]
                            ins = pool.tensor_tensor(q, q, EGC[:, 4 * t:4 * t + 4, :], ALU.mult)
                        ins.then_inc(ev["qd_ready"], 1)
                for n in (1, 2):
                    pool.wait_ge(ev["oh_made"], n + 1)
                    pool.tensor_tensor(branch_halves(n)[1], oT[n][:, :, :], branch_halves(n)[0].bitcast(F32), ALU.subtract)\
                        .then_inc(ev["ol_made"], 1)
                for which in range(2):
                    pool.wait_ge(ev["lnp_loaded"], 16 * (which + 1))
                    for t in range(TT):
                        b = res[:, t, 512:D]
                        pool.wait_ge(ev["ln_scaled"], 2 * which + t + 1)
                        pool.tensor_tensor(b, b, lnp[:, 0, 512:D], ALU.mult).then_inc(ev["ln_b_mult"], 1)
                        pool.wait_ge(ev["ln_b_mult"], 2 * which + t + 1)
                        pool.tensor_tensor(x_tok[:, t, 512:D], b, lnp[:, 1, 512:D], ALU.add).then_inc(ev["x_normed_b"], 1)
                pool.drain()
                pool.wait_ge(layer_done, l * 3 + 3)
                pool.sem_inc(layer_seen, 1)
                pool.sem_clear(range(of_a_layer[0], of_a_layer[-1] + 1))
                pool.sem_inc(layer_go, 1)


def kernel(x, positions, w_in, mla_q_norm, mla_w_uq, mla_kv_norm, mla_w_ukv, gdn_conv, gdn_a_log, gdn_dt_bias,
           gdn_out_norm, fox_f_bias, w_branch, w_out, ln1_g, ln1_b, router_w, router_bias,
           exp_w_gate, exp_w_up, exp_w_down, ln2_g, ln2_b):
    import concourse.bacc as _bacc
    from concourse.bass_utils import run_bass_kernel_spmd as _run

    def arr(a):
        return np.ascontiguousarray(a)

    rows = []
    for l in range(L):
        rows += [arr(mla_q_norm[l]).reshape(2, P), arr(mla_kv_norm[l]).reshape(1, P), arr(gdn_out_norm[l]).reshape(1, P),
                 arr(gdn_conv[l]).reshape(CONV * 12, P)]
    row_params = np.concatenate([np.concatenate([arr(gdn_a_log[l]), arr(gdn_dt_bias[l]), arr(fox_f_bias[l])]) for l in range(L)]
                                + [arr(router_bias)])
    ln_params = np.concatenate([np.stack([arr(g[l]), arr(b[l])])[None] for l in range(L)
                                for g, b in ((ln1_g, ln1_b), (ln2_g, ln2_b))])
    arrays = {
        "x": arr(x).reshape(T, D), "positions": arr(positions).reshape(T), "w_in": arr(w_in), "w_uq": arr(mla_w_uq),
        "w_ukv": arr(mla_w_ukv), "w_branch": arr(w_branch), "w_out": arr(w_out),
        "w_gate": arr(exp_w_gate).reshape(L * E, D, F), "w_up": arr(exp_w_up).reshape(L * E, D, F),
        "w_down": arr(exp_w_down).reshape(L * E, F, D), "router_w": arr(router_w), "param_rows": np.concatenate(rows),
        "row_params": row_params, "ln_params": ln_params, "consts": constants(),
    }
    nc = _bacc.Bacc("TRN2", target_bir_lowering=False, num_devices=1, dynamic_dma_scratch_size=1024)
    args = {n: nc.dram_tensor(f"in_{n}", a.shape, mybir.dt.from_np(a.dtype), kind="ExternalInput").ap() for n, a in arrays.items()}
    o = nc.dram_tensor("out", (T, D), F32, kind="ExternalOutput").ap()
    build(nc, *args.values(), o)
    r = _run(nc, [{f"in_{n}": a for n, a in arrays.items()}], core_ids=[0])
    return np.asarray(r.results[0]["out"]).reshape(1, T, D)
```
